# Optimizing a Trainium2 kernel written in Bass

```python
import math
import numpy as np
import jax, jax.numpy as jnp
from jax import lax

D_MODEL = 1024
BATCH = 1
SEQ = 256
DEPTH = 2

N_EVEN = (DEPTH + 1) // 2
N_ODD = DEPTH // 2

MLSTM_HEADS = 4
MLSTM_HEAD_DIM = 128
MLSTM_W = MLSTM_HEADS * MLSTM_HEAD_DIM
MLSTM_CHUNK = 128
CONV_K = 4
NSA_HEADS = 8
NSA_GROUPS = 2
NSA_HPG = NSA_HEADS // NSA_GROUPS
NSA_HEAD_DIM = 64
NSA_W = NSA_HEADS * NSA_HEAD_DIM
NSA_KV_W = NSA_GROUPS * NSA_HEAD_DIM
CMP_LEN = 32
CMP_STRIDE = 16
CMP_HIDDEN = 128
SEL_BLOCK = 64
SEL_TOPK = 16
WINDOW = 512
Q_BLOCK = 128
ROPE_THETA = 500000.0
ROPE_DIM = NSA_HEAD_DIM // 4
EVEN_MIX_W = MLSTM_W + NSA_W
MLSTM_SPLITS = (MLSTM_W,) * 5 + (MLSTM_HEADS, MLSTM_HEADS)
NSA_SPLITS = (NSA_W,) + (NSA_KV_W,) * 6 + (3 * NSA_HEADS, NSA_W)
MLSTM_COLS = sum(MLSTM_SPLITS)
NSA_COLS = sum(NSA_SPLITS)
EVEN_IN_COLS = MLSTM_COLS + NSA_COLS
HGRN_HEADS = 8
HGRN_HEAD_DIM = 128
HGRN_W = HGRN_HEADS * HGRN_HEAD_DIM
HGRN_CHUNK = 64
ODD_IN_COLS = 4 * HGRN_W
EPS = 1e-6
NEG = -1e30


def split_cols(a, sizes):
    idx = np.cumsum(sizes)[:-1].tolist()
    return jnp.split(a, idx, axis=-1)

def rms_norm(x, w):
    xf = x.astype(jnp.float32)
    return xf * lax.rsqrt(jnp.mean(xf * xf, axis=-1, keepdims=True) + EPS) * w.astype(jnp.float32)

def heads(a, n_heads):
    b, s, _ = a.shape
    return a.reshape(b, s, n_heads, -1).transpose(0, 2, 1, 3)

def partial_rope(x, pos):
    half = ROPE_DIM // 2
    inv_freq = ROPE_THETA ** (-jnp.arange(half, dtype=jnp.float32) / half)
    ang = pos.astype(jnp.float32)[:, None] * inv_freq
    cos, sin = jnp.cos(ang), jnp.sin(ang)
    x1, x2, rest = x[..., :half], x[..., half:ROPE_DIM], x[..., ROPE_DIM:]
    return jnp.concatenate([x1 * cos - x2 * sin, x1 * sin + x2 * cos, rest], axis=-1)

def masked_softmax(s, mask):
    p = jax.nn.softmax(jnp.where(mask, s, NEG), axis=-1)
    return jnp.where(mask, p, 0.0)

def causal_conv(x, w, b):
    c = x.shape[-1]
    out = lax.conv_general_dilated(
        x, w.astype(jnp.float32).reshape(CONV_K, 1, c), window_strides=(1,),
        padding=[(CONV_K - 1, 0)], dimension_numbers=('NWC', 'WIO', 'NWC'),
        feature_group_count=c)
    return out + b

def mlstm_chunkwise(q, k, v, i_pre, f_pre):
    b_, h_, s_, d = q.shape
    L = MLSTM_CHUNK
    nc = s_ // L
    logf = jax.nn.log_sigmoid(f_pre)

    def to_chunks(a):
        return jnp.moveaxis(a.reshape(b_, h_, nc, L, *a.shape[3:]), 2, 0)

    causal = jnp.tril(jnp.ones((L, L), dtype=bool))

    def step(carry, xs):
        C, n, m = carry
        qj, kj, vj, ij, fj = xs
        bcum = jnp.cumsum(fj, axis=-1)
        D = jnp.where(causal, bcum[..., :, None] - bcum[..., None, :] + ij[..., None, :], -jnp.inf)
        inter = bcum + m[..., None]
        m_row = jnp.maximum(jnp.max(D, axis=-1), inter)
        Smat = jnp.einsum('bhjd,bhsd->bhjs', qj, kj) * jnp.exp(D - m_row[..., None])
        w_inter = jnp.exp(inter - m_row)
        num = jnp.einsum('bhjs,bhse->bhje', Smat, vj) + w_inter[..., None] * jnp.einsum('bhjd,bhde->bhje', qj, C)
        den = Smat.sum(-1) + w_inter * jnp.einsum('bhjd,bhd->bhj', qj, n)
        h = num / jnp.maximum(jnp.abs(den), jnp.exp(-m_row))[..., None]
        bL = bcum[..., -1]
        dl = bL[..., None] - bcum + ij
        m_new = jnp.maximum(bL + m, jnp.max(dl, axis=-1))
        wk = jnp.exp(dl - m_new[..., None])
        decay = jnp.exp(bL + m - m_new)
        C_new = decay[..., None, None] * C + jnp.einsum('bhs,bhsd,bhse->bhde', wk, kj, vj)
        n_new = decay[..., None] * n + jnp.einsum('bhs,bhsd->bhd', wk, kj)
        return (C_new, n_new, m_new), h

    init = (jnp.zeros((b_, h_, d, d), jnp.float32), jnp.zeros((b_, h_, d), jnp.float32),
            jnp.zeros((b_, h_), jnp.float32))
    _, hs = lax.scan(step, init, (to_chunks(q), to_chunks(k), to_chunks(v), to_chunks(i_pre), to_chunks(logf)))
    return jnp.moveaxis(hs, 0, 2).reshape(b_, h_, s_, d)

def mlstm_branch(cols, f_bias, conv_w, conv_b, head_norm):
    b_, s_, _ = cols.shape
    q, k, v, o, z, ig, fg = split_cols(cols, MLSTM_SPLITS)
    qk = jax.nn.silu(causal_conv(jnp.concatenate([q, k], axis=-1), conv_w, conv_b))
    q, k = jnp.split(qk, 2, axis=-1)
    qh = heads(q, MLSTM_HEADS)
    kh = heads(k, MLSTM_HEADS) * (MLSTM_HEAD_DIM ** -0.5)
    vh = heads(v, MLSTM_HEADS)
    i_pre = ig.transpose(0, 2, 1)
    f_pre = (fg + f_bias).transpose(0, 2, 1)
    h = mlstm_chunkwise(qh, kh, vh, i_pre, f_pre).transpose(0, 2, 1, 3)
    h = rms_norm(h, head_norm.reshape(MLSTM_HEADS, MLSTM_HEAD_DIM)).reshape(b_, s_, MLSTM_W)
    return h * jax.nn.sigmoid(o) * jax.nn.silu(z)

def compress(blocks, w1, w2):
    flat = blocks.reshape(*blocks.shape[:3], CMP_LEN * NSA_HEAD_DIM)
    return jax.nn.gelu(flat @ w1) @ w2

def nsa_branch(cols, q_norm, k_norm, ck_pos, ck_w1, ck_w2, cv_pos, cv_w1, cv_w2):
    b_, s_, _ = cols.shape
    G, R, d = NSA_GROUPS, NSA_HPG, NSA_HEAD_DIM
    q, kc, vc, ks, vs, kw, vw, gt, z = split_cols(cols, NSA_SPLITS)
    pos = jnp.arange(s_)
    qh = partial_rope(rms_norm(heads(q, NSA_HEADS), q_norm), pos) * (d ** -0.5)
    qh = qh.reshape(b_, G, R, s_, d)
    ks_h = partial_rope(rms_norm(heads(ks, G), k_norm[1]), pos)
    vs_h = heads(vs, G)
    kw_h = partial_rope(rms_norm(heads(kw, G), k_norm[2]), pos)
    vw_h = heads(vw, G)

    n_cmp = (s_ - CMP_LEN) // CMP_STRIDE + 1
    cmp_idx = np.arange(n_cmp)[:, None] * CMP_STRIDE + np.arange(CMP_LEN)[None, :]
    cmp_end = jnp.asarray(cmp_idx[:, -1])
    k_cmp = compress(heads(kc, G)[:, :, cmp_idx] + ck_pos, ck_w1, ck_w2)
    k_cmp = partial_rope(rms_norm(k_cmp, k_norm[0]), cmp_end)
    v_cmp = compress(heads(vc, G)[:, :, cmp_idx] + cv_pos, cv_w1, cv_w2)

    n_sel = s_ // SEL_BLOCK
    cs = np.arange(n_cmp) * CMP_STRIDE
    ss = np.arange(n_sel) * SEL_BLOCK
    ov = np.clip(np.minimum(cs[:, None] + CMP_LEN, ss[None, :] + SEL_BLOCK)
                 - np.maximum(cs[:, None], ss[None, :]), 0, None).astype(np.float32)
    ov = jnp.asarray(ov)
    k_top = min(SEL_TOPK, n_sel)

    gates = jax.nn.sigmoid(gt.reshape(b_, s_, NSA_HEADS, 3)).transpose(0, 2, 1, 3).reshape(b_, G, R, s_, 3)
    kw_pad = jnp.pad(kw_h, ((0, 0), (0, 0), (WINDOW, 0), (0, 0)))
    vw_pad = jnp.pad(vw_h, ((0, 0), (0, 0), (WINDOW, 0), (0, 0)))
    bi = jnp.arange(b_)[:, None, None, None]
    gi = jnp.arange(G)[None, :, None, None]
    nqb = s_ // Q_BLOCK

    def to_blocks(a):
        a = a.reshape(*a.shape[:-2], nqb, Q_BLOCK, a.shape[-1])
        return jnp.moveaxis(a, -3, 0)

    def block_fn(args):
        qb, q_blk, g_blk = args
        t = qb * Q_BLOCK + jnp.arange(Q_BLOCK)
        s_c = jnp.einsum('bgrqd,bgnd->bgrqn', q_blk, k_cmp)
        p_c = masked_softmax(s_c, cmp_end[None, :] <= t[:, None])
        o_c = jnp.einsum('bgrqn,bgnd->bgrqd', p_c, v_cmp)
        imp = jnp.einsum('bgrqn,nm->bgqm', p_c, ov)
        blk = jnp.arange(n_sel)[None, :]
        cur = (t // SEL_BLOCK)[:, None]
        forced = (blk == 0) | (blk == cur) | (blk == cur - 1)
        imp = jnp.where(blk > cur, NEG, jnp.where(forced, -NEG, imp))
        _, sel = lax.top_k(imp, k_top)
        valid = sel <= cur[None, None]
        tok = (sel[..., None] * SEL_BLOCK + jnp.arange(SEL_BLOCK)).reshape(b_, G, Q_BLOCK, k_top * SEL_BLOCK)
        tok_ok = jnp.repeat(valid, SEL_BLOCK, axis=-1) & (tok <= t[:, None])
        ks_g = ks_h[bi, gi, tok]
        vs_g = vs_h[bi, gi, tok]
        s_s = jnp.einsum('bgrqd,bgqnd->bgrqn', q_blk, ks_g)
        p_s = masked_softmax(s_s, tok_ok[:, :, None])
        o_s = jnp.einsum('bgrqn,bgqnd->bgrqd', p_s, vs_g)
        kwb = lax.dynamic_slice_in_dim(kw_pad, qb * Q_BLOCK, Q_BLOCK + WINDOW, axis=2)
        vwb = lax.dynamic_slice_in_dim(vw_pad, qb * Q_BLOCK, Q_BLOCK + WINDOW, axis=2)
        sp = qb * Q_BLOCK - WINDOW + jnp.arange(Q_BLOCK + WINDOW)
        wmask = (sp[None, :] >= 0) & (sp[None, :] <= t[:, None]) & (t[:, None] - sp[None, :] < WINDOW)
        s_w = jnp.einsum('bgrqd,bgnd->bgrqn', q_blk, kwb)
        p_w = masked_softmax(s_w, wmask)
        o_w = jnp.einsum('bgrqn,bgnd->bgrqd', p_w, vwb)
        return g_blk[..., 0:1] * o_c + g_blk[..., 1:2] * o_s + g_blk[..., 2:3] * o_w

    out = lax.map(block_fn, (jnp.arange(nqb), to_blocks(qh), to_blocks(gates)))
    out = jnp.moveaxis(out, 0, 3).reshape(b_, NSA_HEADS, s_, d).transpose(0, 2, 1, 3).reshape(b_, s_, NSA_W)
    return out * jax.nn.silu(z)

def hgrn2_chunkwise(q, k, v, logf):
    b_, h_, s_, dk = q.shape
    dv = v.shape[-1]
    L = HGRN_CHUNK
    nc = s_ // L

    def to_chunks(a):
        return jnp.moveaxis(a.reshape(b_, h_, nc, L, a.shape[-1]), 2, 0)

    causal = jnp.tril(jnp.ones((L, L), dtype=bool))[..., None]

    def step(Sst, xs):
        qj, kj, vj, gj = xs
        bcum = jnp.cumsum(gj, axis=-2)
        diff = bcum[..., :, None, :] - bcum[..., None, :, :]
        dec = jnp.exp(jnp.where(causal, diff, -jnp.inf))
        A = jnp.einsum('bhjc,bhsc,bhjsc->bhjs', qj, kj, dec)
        o = jnp.einsum('bhjs,bhsv->bhjv', A, vj) + jnp.einsum('bhjc,bhcv->bhjv', qj * jnp.exp(bcum), Sst)
        bL = bcum[..., -1, :]
        S_new = jnp.exp(bL)[..., None] * Sst + jnp.einsum('bhsc,bhsv->bhcv', kj * jnp.exp(bL[..., None, :] - bcum), vj)
        return S_new, o

    init = jnp.zeros((b_, h_, dk, dv), jnp.float32)
    _, os_ = lax.scan(step, init, (to_chunks(q), to_chunks(k), to_chunks(v), to_chunks(logf)))
    return jnp.moveaxis(os_, 0, 2).reshape(b_, h_, s_, dv)

def hgrn2_layer(h, w_in, b_in, lb, head_norm, w_out):
    b_, s_, _ = h.shape
    proj = h @ w_in + b_in
    fp, iv, qp, z = jnp.split(proj, 4, axis=-1)
    logf = jnp.log(lb + (1.0 - lb) * jax.nn.sigmoid(fp))
    k = (1.0 - lb) * jax.nn.sigmoid(-fp)
    q = jax.nn.silu(qp)
    o = hgrn2_chunkwise(heads(q, HGRN_HEADS), heads(k, HGRN_HEADS), heads(iv, HGRN_HEADS), heads(logf, HGRN_HEADS))
    o = rms_norm(o.transpose(0, 2, 1, 3), head_norm.reshape(HGRN_HEADS, HGRN_HEAD_DIM)).reshape(b_, s_, HGRN_W)
    return (o * jax.nn.silu(z)) @ w_out

def even_layer(h, w_in, b_in, f_bias, conv_w, conv_b, head_norm, q_norm, k_norm,
               ck_pos, ck_w1, ck_w2, cv_pos, cv_w1, cv_w2, w_out):
    proj = h @ w_in + b_in
    m_cols, n_cols = jnp.split(proj, [MLSTM_COLS], axis=-1)
    ya = mlstm_branch(m_cols, f_bias, conv_w, conv_b, head_norm)
    yb = nsa_branch(n_cols, q_norm, k_norm, ck_pos, ck_w1, ck_w2, cv_pos, cv_w1, cv_w2)
    return jnp.concatenate([ya, yb], axis=-1) @ w_out

def first_inputs(seed: int = 0) -> dict:
    key = jax.random.key(seed)
    ks = jax.random.split(key, 24)

    def nrm(k, shape, scale):
        return scale * jax.random.normal(k, shape, jnp.float32)

    NE, NO = N_EVEN, N_ODD
    return {
        "x": nrm(ks[0], (BATCH, SEQ, D_MODEL), 1.0),
        "norm_w": 1.0 + nrm(ks[1], (DEPTH, D_MODEL), 0.02),
        "ev_w_in": nrm(ks[2], (NE, D_MODEL, EVEN_IN_COLS), D_MODEL ** -0.5),
        "ev_b_in": nrm(ks[3], (NE, EVEN_IN_COLS), 0.02),
        "mlstm_f_bias": jnp.linspace(3.0, 6.0, MLSTM_HEADS, dtype=jnp.float32)[None, :] + nrm(ks[4], (NE, MLSTM_HEADS), 0.1),
        "mlstm_conv_w": nrm(ks[5], (NE, CONV_K, 2 * MLSTM_W), CONV_K ** -0.5),
        "mlstm_conv_b": nrm(ks[6], (NE, 2 * MLSTM_W), 0.02),
        "mlstm_head_norm": 1.0 + nrm(ks[7], (NE, MLSTM_W), 0.02),
        "nsa_q_norm": 1.0 + nrm(ks[8], (NE, NSA_HEAD_DIM), 0.02),
        "nsa_k_norm": 1.0 + nrm(ks[9], (NE, 3, NSA_HEAD_DIM), 0.02),
        "cmp_k_pos": nrm(ks[10], (NE, CMP_LEN, NSA_HEAD_DIM), 0.1),
        "cmp_k_w1": nrm(ks[11], (NE, CMP_LEN * NSA_HEAD_DIM, CMP_HIDDEN), (CMP_LEN * NSA_HEAD_DIM) ** -0.5),
        "cmp_k_w2": nrm(ks[12], (NE, CMP_HIDDEN, NSA_HEAD_DIM), CMP_HIDDEN ** -0.5),
        "cmp_v_pos": nrm(ks[13], (NE, CMP_LEN, NSA_HEAD_DIM), 0.1),
        "cmp_v_w1": nrm(ks[14], (NE, CMP_LEN * NSA_HEAD_DIM, CMP_HIDDEN), (CMP_LEN * NSA_HEAD_DIM) ** -0.5),
        "cmp_v_w2": nrm(ks[15], (NE, CMP_HIDDEN, NSA_HEAD_DIM), CMP_HIDDEN ** -0.5),
        "ev_w_out": nrm(ks[16], (NE, EVEN_MIX_W, D_MODEL), EVEN_MIX_W ** -0.5),
        "od_w_in": nrm(ks[17], (NO, D_MODEL, ODD_IN_COLS), D_MODEL ** -0.5),
        "od_b_in": nrm(ks[18], (NO, ODD_IN_COLS), 0.02),
        "hgrn_lb_logits": nrm(ks[19], (NO + 1, HGRN_W), 0.5),
        "hgrn_head_norm": 1.0 + nrm(ks[20], (NO, HGRN_W), 0.02),
        "od_w_out": nrm(ks[21], (NO, HGRN_W, D_MODEL), HGRN_W ** -0.5),
    }

def first_block(x, norm_w, ev_w_in, ev_b_in, mlstm_f_bias, mlstm_conv_w, mlstm_conv_b, mlstm_head_norm,
              nsa_q_norm, nsa_k_norm, cmp_k_pos, cmp_k_w1, cmp_k_w2, cmp_v_pos, cmp_v_w1, cmp_v_w2,
              ev_w_out, od_w_in, od_b_in, hgrn_lb_logits, hgrn_head_norm, od_w_out):
    lbs = jnp.cumsum(jax.nn.softmax(hgrn_lb_logits.astype(jnp.float32), axis=0), axis=0)
    for layer in range(DEPTH):
        h = rms_norm(x, norm_w[layer])
        j = layer // 2
        if layer % 2 == 0:
            y = even_layer(h, ev_w_in[j], ev_b_in[j], mlstm_f_bias[j], mlstm_conv_w[j], mlstm_conv_b[j],
                           mlstm_head_norm[j], nsa_q_norm[j], nsa_k_norm[j], cmp_k_pos[j], cmp_k_w1[j],
                           cmp_k_w2[j], cmp_v_pos[j], cmp_v_w1[j], cmp_v_w2[j], ev_w_out[j])
        else:
            y = hgrn2_layer(h, od_w_in[j], od_b_in[j], lbs[j], hgrn_head_norm[j], od_w_out[j])
        x = x + y.astype(x.dtype)
    return x


DEPTH_2 = 1

N_META = 16
BLOCK = 128
META_PAD = BLOCK - N_META
HEAD_DIM = 64
SB_HEADS = (D_MODEL // 2) // HEAD_DIM
RWKV_HEADS = (D_MODEL // 2) // HEAD_DIM
SB_WIDTH = SB_HEADS * HEAD_DIM
RWKV_WIDTH = RWKV_HEADS * HEAD_DIM
MIX_WIDTH = SB_WIDTH + RWKV_WIDTH
D_FF = 2816
W_LORA = 32
A_LORA = 32
G_LORA = 96
N_RWKV_COLS = 3 * RWKV_WIDTH + W_LORA + A_LORA + G_LORA
IN_COLS = 3 * SB_WIDTH + N_RWKV_COLS
RMS_EPS = 1e-6
LNX_EPS = 64e-5


def rms_norm_2(x, g):
    xf = x.astype(jnp.float32)
    y = xf * lax.rsqrt(jnp.mean(xf * xf, axis=-1, keepdims=True) + RMS_EPS)
    return (y * g.astype(jnp.float32)).astype(x.dtype)

def swiglu(h, w_gate, w_up, w_down):
    return (jax.nn.silu(h @ w_gate) * (h @ w_up)) @ w_down

def stick_breaking_attention(q, k, v):
    B, L, H, Dh = q.shape
    pad = ((0, 0), (META_PAD, 0), (0, 0), (0, 0))
    q, k, v = [jnp.pad(t, pad).transpose(0, 2, 1, 3) for t in (q, k, v)]
    Lp = L + META_PAD
    nblk = Lp // BLOCK
    key_pos = jnp.arange(Lp)
    scale = Dh ** -0.5
    qb = q.reshape(B, H, nblk, BLOCK, Dh).transpose(2, 0, 1, 3, 4)

    def block(args):
        q_blk, i = args
        q_pos = i * BLOCK + jnp.arange(BLOCK)
        z = jnp.einsum('bhqd,bhkd->bhqk', q_blk, k).astype(jnp.float32) * scale
        valid = (key_pos[None, :] < q_pos[:, None]) & (key_pos[None, :] >= META_PAD)
        log_keep = jnp.where(valid, -jax.nn.softplus(z), 0.0)
        log_rest = lax.cumsum(log_keep, axis=3, reverse=True) - log_keep
        attn = jnp.where(valid, jnp.exp(jax.nn.log_sigmoid(z) + log_rest), 0.0)
        return jnp.einsum('bhqk,bhkd->bhqd', attn.astype(v.dtype), v)

    out = lax.map(block, (qb, jnp.arange(nblk)))
    out = out.transpose(1, 0, 3, 2, 4).reshape(B, Lp, H * Dh)
    return out[:, META_PAD:]

def rwkv7_time_mix(p, mu, w0, w_up, a0, a_up, g_up, k_k, k_a, r_k, lnx_w, lnx_b):
    B, L, _ = p.shape
    C, H, N = RWKV_WIDTH, RWKV_HEADS, HEAD_DIM
    p_prev = jnp.pad(p, ((0, 0), (1, 0), (0, 0)))[:, :-1]
    p = p + (p_prev - p) * mu
    r = p[..., :C]
    k = p[..., C:2 * C]
    v = p[..., 2 * C:3 * C]
    xw = p[..., 3 * C:3 * C + W_LORA]
    xa = p[..., 3 * C + W_LORA:3 * C + W_LORA + A_LORA]
    xg = p[..., 3 * C + W_LORA + A_LORA:]
    w = -jax.nn.softplus(-(w0 + jnp.tanh(xw) @ w_up)) - 0.5
    decay = jnp.exp(-jnp.exp(w.astype(jnp.float32)))
    a = jax.nn.sigmoid(a0 + xa @ a_up)
    g = jax.nn.sigmoid(xg) @ g_up
    kk = (k * k_k).astype(jnp.float32).reshape(B, L, H, N)
    kk = kk / jnp.maximum(jnp.sqrt(jnp.sum(kk * kk, axis=-1, keepdims=True)), 1e-12)
    k = k * (1.0 + (a - 1.0) * k_a)

    rh, kh, vh, ah, dh = [t.astype(jnp.float32).reshape(B, L, H, N) for t in (r, k, v, a, decay)]

    def step(S, inp):
        r_t, w_t, k_t, v_t, kk_t, a_t = inp
        sa = jnp.einsum('bhij,bhj->bhi', S, -kk_t)
        S = (S * w_t[:, :, None, :] + sa[..., None] * (kk_t * a_t)[:, :, None, :]
             + v_t[..., None] * k_t[:, :, None, :])
        return S, jnp.einsum('bhij,bhj->bhi', S, r_t)

    xs = tuple(t.transpose(1, 0, 2, 3) for t in (rh, dh, kh, vh, kk, ah))
    S0 = jnp.zeros((B, H, N, N), jnp.float32)
    _, ys = lax.scan(step, S0, xs)
    y = ys.transpose(1, 0, 2, 3)
    mean = jnp.mean(y, axis=-1, keepdims=True)
    var = jnp.mean(jnp.square(y - mean), axis=-1, keepdims=True)
    y = ((y - mean) * lax.rsqrt(var + LNX_EPS)).reshape(B, L, C)
    y = y * lnx_w.astype(jnp.float32) + lnx_b.astype(jnp.float32)
    bonus = jnp.sum(rh * kh * r_k.astype(jnp.float32), axis=-1, keepdims=True) * vh
    y = y + bonus.reshape(B, L, C)
    return (y * g.astype(jnp.float32)).astype(p.dtype)

def second_inputs(seed: int = 0) -> dict:
    key = jax.random.key(seed)
    ks = jax.random.split(key, 32)
    nrm = lambda k, s: jax.random.normal(k, s, jnp.float32)
    gain = lambda k, s: 1.0 + 0.02 * nrm(k, s)
    Dd = DEPTH_2
    return {
        "x": nrm(ks[0], (BATCH, SEQ, D_MODEL)),
        "meta_tokens": nrm(ks[1], (N_META, D_MODEL)),
        "ffn1_norm": gain(ks[2], (Dd, D_MODEL)),
        "ffn1_w_gate": nrm(ks[3], (Dd, D_MODEL, D_FF)) * D_MODEL ** -0.5,
        "ffn1_w_up": nrm(ks[4], (Dd, D_MODEL, D_FF)) * D_MODEL ** -0.5,
        "ffn1_w_down": nrm(ks[5], (Dd, D_FF, D_MODEL)) * D_FF ** -0.5,
        "mix_norm": gain(ks[6], (Dd, D_MODEL)),
        "w_in": nrm(ks[7], (Dd, D_MODEL, IN_COLS)) * D_MODEL ** -0.5,
        "rwkv_mu": jax.random.uniform(ks[8], (Dd, N_RWKV_COLS), jnp.float32),
        "rwkv_w0": jax.random.uniform(ks[9], (Dd, RWKV_WIDTH), jnp.float32, -4.0, 1.0),
        "rwkv_w_up": nrm(ks[10], (Dd, W_LORA, RWKV_WIDTH)) * 0.5 * W_LORA ** -0.5,
        "rwkv_a0": 0.5 * nrm(ks[11], (Dd, RWKV_WIDTH)),
        "rwkv_a_up": nrm(ks[12], (Dd, A_LORA, RWKV_WIDTH)) * 0.5 * A_LORA ** -0.5,
        "rwkv_g_up": nrm(ks[13], (Dd, G_LORA, RWKV_WIDTH)) * G_LORA ** -0.5,
        "rwkv_k_k": 0.85 + 0.05 * nrm(ks[14], (Dd, RWKV_WIDTH)),
        "rwkv_k_a": 1.0 + 0.05 * nrm(ks[15], (Dd, RWKV_WIDTH)),
        "rwkv_r_k": 0.1 * nrm(ks[16], (Dd, RWKV_HEADS, HEAD_DIM)),
        "rwkv_lnx_w": gain(ks[17], (Dd, RWKV_WIDTH)),
        "rwkv_lnx_b": 0.02 * nrm(ks[18], (Dd, RWKV_WIDTH)),
        "w_out": nrm(ks[19], (Dd, MIX_WIDTH, D_MODEL)) * MIX_WIDTH ** -0.5,
        "ffn2_norm": gain(ks[20], (Dd, D_MODEL)),
        "ffn2_w_gate": nrm(ks[21], (Dd, D_MODEL, D_FF)) * D_MODEL ** -0.5,
        "ffn2_w_up": nrm(ks[22], (Dd, D_MODEL, D_FF)) * D_MODEL ** -0.5,
        "ffn2_w_down": nrm(ks[23], (Dd, D_FF, D_MODEL)) * D_FF ** -0.5,
        "final_norm": gain(ks[24], (D_MODEL,)),
    }

def second_block(x, meta_tokens, ffn1_norm, ffn1_w_gate, ffn1_w_up, ffn1_w_down, mix_norm, w_in,
              rwkv_mu, rwkv_w0, rwkv_w_up, rwkv_a0, rwkv_a_up, rwkv_g_up, rwkv_k_k, rwkv_k_a,
              rwkv_r_k, rwkv_lnx_w, rwkv_lnx_b, w_out, ffn2_norm, ffn2_w_gate, ffn2_w_up,
              ffn2_w_down, final_norm):
    B = x.shape[0]
    meta = jnp.broadcast_to(meta_tokens[None].astype(x.dtype), (B, N_META, D_MODEL))
    h = jnp.concatenate([meta, x], axis=1)
    for l in range(DEPTH_2):
        n = rms_norm_2(h, ffn1_norm[l])
        h = h + 0.5 * swiglu(n, ffn1_w_gate[l], ffn1_w_up[l], ffn1_w_down[l])
        n = rms_norm_2(h, mix_norm[l])
        proj = n @ w_in[l]
        Bn, L, _ = proj.shape
        q = proj[..., :SB_WIDTH].reshape(Bn, L, SB_HEADS, HEAD_DIM)
        k = proj[..., SB_WIDTH:2 * SB_WIDTH].reshape(Bn, L, SB_HEADS, HEAD_DIM)
        v = proj[..., 2 * SB_WIDTH:3 * SB_WIDTH].reshape(Bn, L, SB_HEADS, HEAD_DIM)
        sb_out = stick_breaking_attention(q, k, v)
        rw_out = rwkv7_time_mix(proj[..., 3 * SB_WIDTH:], rwkv_mu[l], rwkv_w0[l], rwkv_w_up[l],
                                rwkv_a0[l], rwkv_a_up[l], rwkv_g_up[l], rwkv_k_k[l], rwkv_k_a[l],
                                rwkv_r_k[l], rwkv_lnx_w[l], rwkv_lnx_b[l])
        h = h + jnp.concatenate([sb_out, rw_out], axis=-1) @ w_out[l]
        n = rms_norm_2(h, ffn2_norm[l])
        h = h + 0.5 * swiglu(n, ffn2_w_gate[l], ffn2_w_up[l], ffn2_w_down[l])
    return rms_norm_2(h, final_norm)[:, N_META:]


def setup_inputs(seed=0):
    out = dict(first_inputs(seed))
    for name, value in second_inputs(seed + 1).items():
        if name != "x":
            out[name + "_2"] = value
    return out


def reference(
    x, norm_w, ev_w_in, ev_b_in, mlstm_f_bias, mlstm_conv_w, mlstm_conv_b, mlstm_head_norm,
    nsa_q_norm, nsa_k_norm, cmp_k_pos, cmp_k_w1, cmp_k_w2, cmp_v_pos, cmp_v_w1, cmp_v_w2,
    ev_w_out, od_w_in, od_b_in, hgrn_lb_logits, hgrn_head_norm, od_w_out, meta_tokens_2,
    ffn1_norm_2, ffn1_w_gate_2, ffn1_w_up_2, ffn1_w_down_2, mix_norm_2, w_in_2, rwkv_mu_2,
    rwkv_w0_2, rwkv_w_up_2, rwkv_a0_2, rwkv_a_up_2, rwkv_g_up_2, rwkv_k_k_2, rwkv_k_a_2,
    rwkv_r_k_2, rwkv_lnx_w_2, rwkv_lnx_b_2, w_out_2, ffn2_norm_2, ffn2_w_gate_2, ffn2_w_up_2,
    ffn2_w_down_2, final_norm_2,
):
    x = first_block(
        x, norm_w, ev_w_in, ev_b_in, mlstm_f_bias, mlstm_conv_w, mlstm_conv_b, mlstm_head_norm,
        nsa_q_norm, nsa_k_norm, cmp_k_pos, cmp_k_w1, cmp_k_w2, cmp_v_pos, cmp_v_w1, cmp_v_w2,
        ev_w_out, od_w_in, od_b_in, hgrn_lb_logits, hgrn_head_norm, od_w_out,
    )
    return second_block(
        x, meta_tokens_2, ffn1_norm_2, ffn1_w_gate_2, ffn1_w_up_2, ffn1_w_down_2, mix_norm_2,
        w_in_2, rwkv_mu_2, rwkv_w0_2, rwkv_w_up_2, rwkv_a0_2, rwkv_a_up_2, rwkv_g_up_2,
        rwkv_k_k_2, rwkv_k_a_2, rwkv_r_k_2, rwkv_lnx_w_2, rwkv_lnx_b_2, w_out_2, ffn2_norm_2,
        ffn2_w_gate_2, ffn2_w_up_2, ffn2_w_down_2, final_norm_2,
    )


_drawn_inputs = setup_inputs


def setup_inputs(seed=0):
    import zlib

    import numpy as np

    out = dict(_drawn_inputs(seed))
    spreads = {}
    factors = {'mlstm_conv_b': 8.0,
     'mlstm_head_norm': 8.0,
     'nsa_q_norm': 8.0,
     'nsa_k_norm': 8.0,
     'cmp_k_pos': 8.0,
     'cmp_v_pos': 3.322,
     'hgrn_head_norm': 4.989,
     'ffn1_norm_2': 7.26,
     'mix_norm_2': 4.452,
     'rwkv_w_up_2': 4.806,
     'rwkv_k_k_2': 200.0,
     'rwkv_k_a_2': 3.846,
     'rwkv_lnx_w_2': 195.586,
     'rwkv_lnx_b_2': 194.794,
     'ffn2_norm_2': 27.916,
     'final_norm_2': 22.902}
    for name, (base, spread) in spreads.items():
        noise = np.random.default_rng([zlib.crc32(name.encode()), seed]).standard_normal(out[name].shape)
        drawn = base * np.exp(spread * noise) if base else spread * noise
        out[name] = __import__('jax').numpy.asarray(drawn.astype(out[name].dtype))
    for name, factor in factors.items():
        out[name] = (out[name] * factor).astype(out[name].dtype)
    return out
```

```python
from contextlib import ExitStack

import numpy as np
import concourse.bass as bass
from concourse import mybir

F32 = mybir.dt.float32
BF16 = mybir.dt.bfloat16
U32 = mybir.dt.uint32
ALU = mybir.AluOpType
ACT = mybir.ActivationFunctionType
AX = mybir.AxisListType

P = 128
D = 1024
KT = D // P
T = 256
TM = 16
TT = T + TM
EPS = 1e-6
LNX_EPS = 64e-5
BIG = 1e30
NCMP = 15
FF = 2816
FT = FF // P
SLOTS = 8
LEVELS = (1, 2, 4, 8, 16, 32, 64)
RW_CHUNK = 64
RW_CHUNKS = [(c, min(RW_CHUNK, TT - c)) for c in range(0, TT, RW_CHUNK)]
TILES2 = [(0, 128), (128, 128), (256, 16)]
DECAY = float(np.exp(-0.5))

E_UNITS = 35
C_UNITS = 4
H_UNITS = 32
GU_UNITS = 2 * FT
DN_UNITS = FT
P_UNITS = 26
U_E = 0
U_C = U_E + E_UNITS
U_EO = U_C + C_UNITS
U_H = U_EO + KT
U_HO = U_H + H_UNITS
U_F1 = U_HO + KT
U_P = U_F1 + GU_UNITS + DN_UNITS
U_PO = U_P + P_UNITS
U_F2 = U_PO + KT
N_UNITS = U_F2 + GU_UNITS + DN_UNITS

E_OWNER = "v" + "aa" + "aaaa" + "aa" + "vv" + "aaaa" + "aaaa" + "vvvv" + "aaaa" + "aaaa" + "aaaa"
H_OWNER = "a" * 8 + "a" * 8 + "v" * 8 + "a" * 8
G_E = 0
G_EO = G_E + E_UNITS
G_H = G_EO + KT
G_HO = G_H + H_UNITS
G_F1 = G_HO + KT
G_P = G_F1 + GU_UNITS + KT
G_PO = G_P + P_UNITS
G_F2 = G_PO + KT
OWNER = (E_OWNER + "v" * KT + H_OWNER + "v" * KT + "v" * (GU_UNITS + KT) + "a" * P_UNITS
         + "v" * KT + "v" * (GU_UNITS + KT))
MM_BANKS = 4


def drained(owner, g):
    return OWNER[:g + 1].count(owner)


def _offsets(parts):
    at, out = 0, {}
    for name, n in parts:
        out[name] = at
        at += n
    return out, at


VEC, NVEC = _offsets([
    ("norm0", 8), ("norm1", 8), ("ffn1", 8), ("mix", 8), ("ffn2", 8), ("final", 8),
    ("ev_b", 35), ("conv_w", 32), ("conv_b", 8), ("mnorm", 4), ("nqk", 6), ("kcn", 1),
    ("fp_b", 8), ("qp_b", 8), ("z_b", 8), ("lb0", 8), ("lb1", 8), ("hnorm", 8),
    ("mu", 14), ("w0", 4), ("a0", 4), ("k_k", 4), ("k_a", 4), ("r_k", 4), ("lnx_w", 4), ("lnx_b", 4),
    ("kpos", 16), ("vpos", 16)])
ROW, NROW = _offsets([("small", 32), ("fbias", 4), ("vs", 128), ("vw", 128), ("v", 512), ("iv", 1024)])
MAT, NMAT = _offsets([("w2k", 64), ("w2v", 64), ("wup", 512), ("gup", 512)])
CST, NCST = _offsets([
    ("ident", 128), ("ones", 128), ("blk", 128), ("ge", 128), ("le", 128), ("gt", 128),
    ("cos", 256), ("sin", 256), ("rot", 128), ("dup0", 128), ("dup1", 128), ("pick", 512),
    ("cosc", NCMP), ("sinc", NCMP), ("cneg", 2 * NCMP), ("cok", 2 * NCMP),
    ("hlev", 7 * 128), ("sbok", 432), ("rwmask", 512), ("rlev", 6 * 128), ("rlevt", 128),
    ("istack", 64)])


def constants():
    c = np.zeros((P, NCST), np.float32)

    def put(name, a):
        c[:a.shape[0], CST[name]:CST[name] + a.shape[1]] = a

    i = np.arange(P)
    row, col = i[:, None], i[None, :]
    put("ident", np.eye(P))
    put("ones", np.ones((P, P)))
    put("blk", (row // 64 == col // 64) * 1.0)
    put("ge", (row >= col) * 1.0)
    put("le", (row <= col) * 1.0)
    put("gt", (row > col) * 1.0)

    def rope(pos):
        half = 8
        inv = (500000.0 ** (-np.arange(half, dtype=np.float32) / np.float32(half))).astype(np.float32)
        ang = pos.astype(np.float32)[None, :] * inv[:, None]
        cos, sin = np.ones((P, len(pos))), np.zeros((P, len(pos)))
        for g in range(2):
            for s in range(2):
                cos[64 * g + 8 * s:64 * g + 8 * s + 8] = np.cos(ang)
                sin[64 * g + 8 * s:64 * g + 8 * s + 8] = np.sin(ang)
        return cos, sin

    cos, sin = rope(np.arange(T))
    put("cos", cos)
    put("sin", sin)
    cos, sin = rope(np.arange(NCMP) * 16 + 31)
    put("cosc", cos)
    put("sinc", sin)
    rot = np.zeros((P, P))
    for g in range(2):
        for k in range(8):
            rot[64 * g + 8 + k, 64 * g + k] = -1.0
            rot[64 * g + k, 64 * g + 8 + k] = 1.0
    put("rot", rot)
    for g in range(2):
        dup = np.zeros((P, P))
        for d in range(64):
            dup[64 * g + d, d] = dup[64 * g + d, 64 + d] = 1.0
        put(f"dup{g}", dup)
    pick = np.zeros((4, 4, P))
    for h in range(4):
        pick[h, h] = 1.0
    put("pick", pick.reshape(4, 512))
    ok = (np.arange(NCMP)[None, None, :] * 16 + 31 <= (np.arange(2)[None, :, None] * P + i[:, None, None]))
    put("cok", ok.reshape(P, -1) * 1.0)
    put("cneg", np.where(ok, 0.0, -BIG).reshape(P, -1))
    lev = [((row // (2 * b) == col // (2 * b)) & (row % (2 * b) < b) & (col % (2 * b) >= b)) for b in LEVELS]
    put("hlev", np.concatenate(lev, 1) * 1.0)
    put("rlev", np.concatenate([m.T for m in lev[:6]], 1) * 1.0)
    put("rlevt", lev[0] * 1.0)
    strict, incl = (row < col), (row <= col)
    put("sbok", np.concatenate([strict, np.ones((P, 144)), strict, np.ones((P, 16)), strict[:, :16]], 1) * 1.0)
    same = row // RW_CHUNK == col // RW_CHUNK
    put("rwmask", np.concatenate([strict & same, incl & same] * 2, 1) * 1.0)
    put("istack", (row % 64 == np.arange(64)[None, :]) * 1.0)
    return c


def pack(i):
    f = {k: np.asarray(v) for k, v in i.items()}
    ev_w, ev_b = f["ev_w_in"][0], f["ev_b_in"][0]
    nsa = 2568
    r = np.arange
    pair = [np.concatenate([r(64) + 64 * j, r(64) + 64 * (4 + j)]) for j in range(4)]
    ev_cols = [np.concatenate([r(2560, 2568), nsa + 1280 + r(24)])]
    ev_cols += [nsa + 512 + r(128), nsa + 640 + r(128)]
    ev_cols += [nsa + pair[j] for j in range(4)]
    ev_cols += [nsa + 768 + r(128), nsa + 1024 + r(128), nsa + 896 + r(128), nsa + 1152 + r(128)]
    ev_cols += [r(128) + 128 * j for j in (0, 1, 2, 3, 4, 5, 6, 7, 8, 9, 10, 11, 12, 13, 14, 15, 16, 17, 18, 19)]
    ev_cols += [nsa + 1304 + pair[j] for j in range(4)]
    assert len(ev_cols) == E_UNITS
    stream = np.zeros((N_UNITS, P, KT * P), np.float32)
    at = [0]

    def unit(w):
        k, n = w.shape[0] // P, w.shape[1]
        stream[at[0]].reshape(P, KT, P)[:, :k, :n] = w.reshape(k, P, n).transpose(1, 0, 2)
        at[0] += 1

    def units(w):
        for m in range(w.shape[1] // P):
            unit(w[:, m * P:(m + 1) * P])

    def ffn(gate, up, down):
        for m in range(FT):
            unit(gate[:, m * P:(m + 1) * P])
            unit(up[:, m * P:(m + 1) * P])
        blocks = down.reshape(FT, P, KT, P).transpose(2, 0, 1, 3).reshape(FT, KT, P, P)
        for u in range(FT):
            stream[at[0]].reshape(P, KT, P)[:] = blocks[u].transpose(1, 0, 2)
            at[0] += 1

    for c in ev_cols:
        unit(ev_w[:, c])
    for w1 in (f["cmp_k_w1"][0], f["cmp_v_w1"][0]):
        unit(w1[:1024])
        unit(w1[1024:])
    rows = np.concatenate([r(512)] + [512 + pair[j] for j in range(4)])
    units(f["ev_w_out"][0][rows])
    od = f["od_w_in"][0]
    for part in (0, 2, 1, 3):
        units(od[:, part * D:(part + 1) * D])
    units(f["od_w_out"][0])
    ffn(f["ffn1_w_gate_2"][0], f["ffn1_w_up_2"][0], f["ffn1_w_down_2"][0])
    w_in = f["w_in_2"][0]
    units(w_in[:, :3072])
    unit(w_in[:, 3072:3136])
    unit(w_in[:, 3136:3232])
    units(f["w_out_2"][0])
    ffn(f["ffn2_w_gate_2"][0], f["ffn2_w_up_2"][0], f["ffn2_w_down_2"][0])
    assert at[0] == N_UNITS

    vec = np.zeros((P, NVEC), np.float32)

    def col(name, v):
        v = v.reshape(-1, P).T
        vec[:, VEC[name]:VEC[name] + v.shape[1]] = v

    col("norm0", f["norm_w"][0])
    col("norm1", f["norm_w"][1])
    for name, key in (("ffn1", "ffn1_norm_2"), ("mix", "mix_norm_2"), ("ffn2", "ffn2_norm_2"), ("final", "final_norm_2"),
                      ("conv_b", "mlstm_conv_b"), ("mnorm", "mlstm_head_norm"), ("hnorm", "hgrn_head_norm"),
                      ("w0", "rwkv_w0_2"), ("a0", "rwkv_a0_2"), ("k_k", "rwkv_k_k_2"), ("k_a", "rwkv_k_a_2"),
                      ("r_k", "rwkv_r_k_2"), ("lnx_w", "rwkv_lnx_w_2"), ("lnx_b", "rwkv_lnx_b_2")):
        col(name, f[key])
    for m, c in enumerate(ev_cols):
        if len(c) == P:
            vec[:, VEC["ev_b"] + m] = ev_b[c]
    vec[:, VEC["conv_w"]:VEC["conv_w"] + 32] = f["mlstm_conv_w"][0].reshape(4, 8, P).transpose(2, 1, 0).reshape(P, 32)
    qn, kn = f["nsa_q_norm"][0], f["nsa_k_norm"][0]
    for m, v in enumerate([qn] * 4 + [kn[1], kn[2]]):
        vec[:64, VEC["nqk"] + m] = vec[64:, VEC["nqk"] + m] = v
    vec[:64, VEC["kcn"]] = vec[64:, VEC["kcn"]] = kn[0]
    ob = f["od_b_in"][0]
    col("fp_b", ob[:D])
    col("qp_b", ob[2 * D:3 * D])
    col("z_b", ob[3 * D:])
    col("lb0", f["hgrn_lb_logits"][0])
    col("lb1", f["hgrn_lb_logits"][1])
    mu = f["rwkv_mu_2"][0]
    col("mu", mu[:1536])
    vec[:64, VEC["mu"] + 12] = mu[1536:1600]
    vec[:96, VEC["mu"] + 13] = mu[1600:]
    col("kpos", f["cmp_k_pos"][0].reshape(16, P))
    col("vpos", f["cmp_v_pos"][0].reshape(16, P))

    row = np.zeros((1, NROW), np.float32)
    for name, v in (("small", ev_b[ev_cols[0]]), ("fbias", f["mlstm_f_bias"][0]), ("vs", ev_b[ev_cols[9]]),
                    ("vw", ev_b[ev_cols[10]]), ("v", ev_b[1024:1536]), ("iv", ob[D:2 * D])):
        row[0, ROW[name]:ROW[name] + len(v)] = v
    mat = np.zeros((P, NMAT), np.float32)
    mat[:, MAT["w2k"]:MAT["w2k"] + 64] = f["cmp_k_w2"][0]
    mat[:, MAT["w2v"]:MAT["w2v"] + 64] = f["cmp_v_w2"][0]
    mat[0:32, MAT["wup"]:MAT["wup"] + 512] = f["rwkv_w_up_2"][0]
    mat[32:64, MAT["wup"]:MAT["wup"] + 512] = f["rwkv_a_up_2"][0]
    mat[0:96, MAT["gup"]:MAT["gup"] + 512] = f["rwkv_g_up_2"][0]
    x_t = f["x"][0].T.reshape(KT, P, T).transpose(1, 0, 2)
    meta_t = f["meta_tokens_2"].T.reshape(KT, P, TM).transpose(1, 0, 2)
    x_in = np.concatenate([meta_t, x_t], 2)
    return {"stream": stream, "vec": vec, "row": row, "mat": mat, "cst": constants(),
            "x": np.ascontiguousarray(x_in, np.float32)}


ONCE = {
    "TensorE": (
        "dup_done", "w2_done", "kc_ss", "kc_rot", "nqk_ss", "nqk_rot", "bcum", "gate_rows", "mh_ss",
        "cmp_s", "hg_o", "hg_ss", "lora_up", "kk_ss", "sb_vt", "gn_mean", "gn_var", "bonus", "g_out"),
    "ScalarE": (
        "hx_sq", "hx_th", "kc_sq", "kc_rs", "nqk_sq", "nqk_rs", "log1p", "gates_th", "qk_th", "mh_sq",
        "mh_rs", "oz_th", "nz_th", "cmp_e", "lb_th", "f_th", "f_log", "q_th", "z_th", "hg_sq", "hg_rs",
        "lora_th", "g_th", "decay_th", "a_th", "kk_sq", "kk_rs", "e_c", "e_cx", "e_nc", "sb_v", "gn_sq",
        "gn_rs"),
    "VectorE": (
        "hx_x", "hx_arg", "gelu_ready", "kc_n", "kc_ready", "logf", "cmp_sub", "cmp_p", "lb_arg", "f_read",
        "q_ready", "kk_n2", "cum", "cum_x", "bonus_in", "g_in"),
}
NORMS = ("norm0", "norm1", "ffn1", "mix", "ffn2", "final")


def used_by(g):
    for g0, u0, n in ((G_E, U_E, E_UNITS), (G_EO, U_EO, KT), (G_H, U_H, H_UNITS), (G_HO, U_HO, KT),
                      (G_F1, U_F1, GU_UNITS), (G_P, U_P, P_UNITS), (G_PO, U_PO, KT), (G_F2, U_F2, GU_UNITS)):
        if g0 <= g < g0 + n:
            return u0 + (g - g0) + 1
    g0, u0 = (G_F1, U_F1) if g < G_P else (G_F2, U_F2)
    m = g - g0 - GU_UNITS
    return u0 + GU_UNITS + (FT * (m + 1) - 1) // KT + 1


def program(nc, stream, vec_d, row_d, mat_d, cst_d, x_d, out_d):
    with ExitStack() as ctx:
        def sb(name, shape, dt=F32, at=ctx):
            return at.enter_context(nc.sbuf_tensor(name, shape, dt))

        sems = {}

        def S(name):
            for engine, names in ONCE.items():
                if name in names:
                    name = engine + "_once"
            if name not in sems:
                sems[name] = ctx.enter_context(nc.semaphore(name))
            return sems[name]

        def once(name):
            for names in ONCE.values():
                if name in names:
                    return S(name), names.index(name) + 1

        ring = sb("ring", [P, SLOTS, KT * P])
        xT = sb("xT", [P, KT, TT])
        hT = sb("hT", [P, KT, TT])
        mixT = sb("mixT", [P, KT, TT])
        sq = sb("sq", [P, KT, TT])
        vec = sb("vec", [P, NVEC])
        row = sb("row", [P, NROW])
        mat = sb("mat", [P, NMAT])
        cst = sb("cst", [P, NCST])
        eps = sb("eps", [P, 4])
        ident_bf = sb("ident_bf", [P, P], BF16)
        later_bf = sb("later_bf", [P, P], BF16)
        before_bf = sb("before_bf", [P, P], BF16)
        notyet_bf = sb("notyet_bf", [P, P], BF16)
        rstd = sb("rstd", [P, TT])
        ps = ctx.enter_context(nc.psum_tensor("ps", [P, 8, 512], F32))

        ev = ExitStack()
        small = sb("small", [P, 2, 32], at=ev)
        kcvc = sb("kcvc", [P, 2, T], at=ev)
        nqk = sb("nqk", [P, 6, T], at=ev)
        nz = sb("nz", [P, 4, T], at=ev)
        vsw = sb("vsw", [P, 2, 2, P], at=ev)
        qkpre = sb("qkpre", [P, 8, 3 + T], at=ev)
        oz = sb("oz", [P, 8, T], at=ev)
        vtok = sb("vtok", [P, 2, 512], at=ev)
        qk = sb("qk", [P, 8, T], at=ev)
        th = sb("th", [P, 8, T], at=ev)
        gl = sb("gl", [P, 6, 8], at=ev)
        rows4 = sb("rows4", [4, 4, T], at=ev)
        mE = sb("mE", [P, 2, 384], at=ev)
        mST = sb("mST", [P, 2, 384], at=ev)
        mem = sb("mem", [P, 2, T], at=ev)
        mad = sb("mad", [P, 2, T], at=ev)
        hm = sb("hm", [P, 4, T], at=ev)
        rs = sb("rs", [P, 6, T], at=ev)
        kc2 = sb("kc2", [P, 2, 2, T], at=ev)
        xc = sb("xc", [P, 2, 16, 2 * NCMP], at=ev)
        hx = sb("hx", [P, 4, 4 * NCMP], at=ev)
        kct = sb("kct", [P, 4, NCMP], at=ev)
        vct = sb("vct", [NCMP, P], at=ev)
        pc = sb("pc", [P, 16, NCMP], at=ev)
        cs = sb("cs", [P, 3, 16], at=ev)
        prob = sb("prob", [P, 2, 4, 512], at=ev)
        pst = sb("pst", [P, 2, 4, 4], at=ev)
        pt = sb("pt", [P, 2, 512], at=ev)
        ev.close()

        hg = ExitStack()
        fF = sb("fF", [P, 8, T], at=hg)
        fK = sb("fK", [P, 8, T], at=hg)
        fQ = sb("fQ", [P, 8, T], at=hg)
        fZ = sb("fZ", [P, 8, T], at=hg)
        fC = sb("fC", [P, 8, T], at=hg)
        ivt = sb("ivt", [P, 2, D], at=hg)
        dif = sb("dif", [P, 2, 8 * T], at=hg)
        qkl = sb("qkl", [P, 2, 8 * T], at=hg)
        hA = sb("hA", [P, 8, 3, P], at=hg)
        lbs = sb("lbs", [P, 6, 8], at=hg)
        hg.close()

        ff = ExitStack()
        fact = sb("fact", [P, FT, TT], at=ff)
        fth = sb("fth", [P, 4, TT], at=ff)
        fhalf = sb("fhalf", [P, TT], at=ff)
        ff.close()

        mx = ExitStack()
        pr = sb("pr", [P, 14, 1 + TT], at=mx)
        pA = sb("pA", [P, 4, TT], at=mx)
        pK = sb("pK", [P, 4, TT], at=mx)
        pC = sb("pC", [P, 4, TT], at=mx)
        pD = sb("pD", [P, 4, TT], at=mx)
        pT = sb("pT", [P, 4, TT], at=mx)
        yT = sb("yT", [P, 4, TT], at=mx)
        eL = sb("eL", [P, 4, 5], at=mx)
        state = sb("state", [P, 2, 4, 64], at=mx)
        AR = hT[:].rearrange("p (m w) t -> p m w t", w=2)
        BK = sq[:].rearrange("p (m w) t -> p m w t", w=2)
        att = ExitStack()
        sbq = sb("sbq", [P, 4, TT], at=att)
        sbk = sb("sbk", [P, 4, 3 * P], at=att)
        sbv = sb("sbv", [P, 4, 3 * P], at=att)
        sbvt = sb("sbvt", [P, 3, 512], at=att)
        zs = sb("zs", [P, 2, 432], at=att)
        zl = sb("zl", [P, 2, 432], at=att)
        zp = sb("zp", [P, 2, 432], at=att)
        zA = sb("zA", [P, 2, 432], at=att)
        att.close()
        rw = ExitStack()
        rA = sb("rA", [P, 8, 512], at=rw)
        rN0 = sb("rN0", [P, 8, P], at=rw)
        rG = sb("rG", [P, 8, P], at=rw)
        rI = sb("rI", [P, 8, P], at=rw)
        rN = sb("rN", [P, 8, P], at=rw)
        rX = sb("rX", [P, 8, P], at=rw)
        rWA = sb("rWA", [P, 8, P], at=rw)
        rUM = sb("rUM", [P, 8, P], at=rw)
        tok = sb("tok", [P, 3, 512], at=rw)
        phi = sb("phi", [P, 2, 4, 64], at=rw)
        psi = sb("psi", [P, 2, 4, 64], at=rw)
        rR = sb("rR", [P, 4, P], at=rw)
        rw.close()
        mx.close()

        def V(name, i=0):
            return vec[:, VEC[name] + i:VEC[name] + i + 1]

        def C(name, n=P, rows=P):
            return cst[0:rows, CST[name]:CST[name] + n]

        def mid(ap, n):
            return ap.unsqueeze(1).broadcast_to([ap.shape[0], n, ap.shape[-1]])

        def end(ap, n):
            return ap.unsqueeze(2).broadcast_to([ap.shape[0], ap.shape[1], n])

        def in_order(eng, own):
            n = {}

            def step(ins, sem=own):
                key = next((e for e, names in ONCE.items() if sem in names), sem)
                n[key] = n.get(key, 0) + 1
                assert key == sem or once(sem)[1] == n[key], sem
                ins.then_inc(S(sem), 1)
                eng.wait_ge(S(sem), n[key])
            return step, n

        block = ctx.enter_context(nc.Block())

        @block.sync
        def _(sp):
            sp.dma_start(xT[:], x_d).then_inc(S("x_in"), 16)
            sp.dma_start(vec[:], vec_d).then_inc(S("consts_in"), 16)
            sp.dma_start(cst[:], cst_d).then_inc(S("consts_in"), 16)
            sp.dma_start(row[:], row_d.broadcast_to([P, NROW])).then_inc(S("consts_in"), 16)
            sp.dma_start(mat[:], mat_d).then_inc(S("consts_in"), 16)
            for s in range(SLOTS):
                sp.dma_start(ring[:, s, :], stream[s]).then_inc(S(f"w_ready{s}"), 16)
            rounds = N_UNITS // SLOTS
            with sp.Fori(1, rounds) as it:
                for s in range(SLOTS):
                    sp.wait_ge(S("w_used"), it * SLOTS + (s + 1 - SLOTS))
                    sp.dma_start(ring[:, s, :], stream[it * SLOTS + s]).then_inc(S(f"w_ready{s}"), 16)
            for u in range(rounds * SLOTS, N_UNITS):
                sp.wait_ge(S("w_used"), u - SLOTS + 1)
                sp.dma_start(ring[:, u % SLOTS, :], stream[u]).then_inc(S(f"w_ready{u % SLOTS}"), 16)
            sp.wait_ge(S("norm_h"), len(NORMS) * KT)
            sp.dma_start(out_d, hT[:, :, TM:TT]).then_inc(S("out_done"), 16)
            sp.wait_ge(S("out_done"), 16)

        @block.tensor
        def _(pe):
            def mm(out, lhsT, rhs, start=True, stop=True):
                return nc.tensor.matmul(out, lhsT, rhs, start=start, stop=stop, skip_group_check=True)

            def weights(u):
                pe.wait_ge(S(f"w_ready{u % SLOTS}"), 16 * (u // SLOTS + 1))
                return ring[:, u % SLOTS, :].rearrange("p (k n) -> p k n", n=P)

            def bank(g):
                if g >= MM_BANKS:
                    who = OWNER[g - MM_BANKS]
                    pe.wait_ge(S("drained_" + who), drained(who, g - MM_BANKS))
                return g % MM_BANKS

            def feature_tile(u, g, src, t0, t1, width=P):
                w, b = weights(u), bank(g)
                for k in range(KT):
                    m = mm(ps[0:width, b, 0:t1 - t0], w[:, k, 0:width], src[:, k, t0:t1], k == 0, k == KT - 1)
                m.then_inc(S("w_used"), 1)

            def token_tile(u, g, src, t0, width=P):
                w, b = weights(u), bank(g)
                for tt in range(2):
                    for k in range(KT):
                        m = mm(ps[:, b, tt * P:tt * P + width], src[:, k, t0 + tt * P:t0 + tt * P + P], w[:, k, 0:width],
                               k == 0, k == KT - 1)
                m.then_inc(S("w_used"), 1)

            def norm(tag, n):
                for k in range(KT):
                    pe.wait_ge(S("norm_sq"), KT * NORMS.index(tag) + k + 1)
                    m = mm(ps[:, 7, 0:n], C("ones"), sq[:, k, 0:n], k == 0, k == KT - 1)
                m.then_inc(S("norm_ss"), 1)

            def even_in():
                pe.wait_ge(S("norm_h"), 1 * KT)
                for j in range(E_UNITS):
                    if j == 0:
                        token_tile(U_E, G_E, hT, TM, 32)
                    elif E_OWNER[j] == "v":
                        token_tile(U_E + j, G_E + j, hT, TM)
                    else:
                        feature_tile(U_E + j, G_E + j, hT, TM, TT)

            def compress():
                pe.wait_ge(S("drained_a"), drained("a", G_E + 2))
                for kind in range(2):
                    for g in range(2):
                        m = mm(ps[:, 4 + kind, g * T:(g + 1) * T], C(f"dup{g}"), kcvc[:, kind, :])
                m.then_inc(S("dup_done"), 1)
                pe.wait_ge(S("xc_ready"), 8)
                for kind in range(2):
                    for half in range(2):
                        w = weights(U_C + 2 * kind + half)
                        for j in range(8):
                            m = mm(ps[:, 6, kind * 32:kind * 32 + 30], w[:, j, :], xc[:, kind, 8 * half + j, :],
                                   half == 0 and j == 0, half == 1 and j == 7)
                        m.then_inc(S("w_used"), 1)
                pe.wait_ge(*once("gelu_ready"))
                for g in range(2):
                    mm(ps[64 * g:64 * g + 64, 6, 64:64 + NCMP], mat[:, MAT["w2k"]:MAT["w2k"] + 64], hx[:, 0, g * NCMP:(g + 1) * NCMP])
                    m = mm(ps[0:NCMP, 6, 128 + 64 * g:192 + 64 * g], hx[:, 0, 30 + g * NCMP:30 + (g + 1) * NCMP],
                           mat[:, MAT["w2v"]:MAT["w2v"] + 64])
                m.then_inc(S("w2_done"), 1)
                pe.wait_ge(*once("kc_sq"))
                mm(ps[:, 6, 256:256 + NCMP], C("blk"), kct[:, 1, :]).then_inc(S("kc_ss"), 1)
                pe.wait_ge(*once("kc_n"))
                mm(ps[:, 6, 288:288 + NCMP], C("rot"), kct[:, 2, :]).then_inc(S("kc_rot"), 1)
                pe.wait_ge(*once("nqk_sq"))
                pe.wait_ge(S("drained_v"), drained("v", G_EO - 1))
                for j in range(3):
                    m = mm(ps[:, j, :], C("blk"), rs[:, 2 * j:2 * j + 2, :].rearrange("p a b -> p (a b)"))
                m.then_inc(S("nqk_ss"), 1)
                pe.wait_ge(S("nqk_n"), 6)
                for j in range(3):
                    m = mm(ps[:, j, :], C("rot"), nqk[:, 2 * j:2 * j + 2, :].rearrange("p a b -> p (a b)"))
                m.then_inc(S("nqk_rot"), 1)

            def mlstm():
                pe.wait_ge(*once("logf"))
                mm(ps[:, 4, 0:4], C("le"), gl[:, 3, 0:4])
                mm(ps[:, 4, 4:8], C("le"), gl[:, 3, 4:8], True, False)
                mm(ps[:, 4, 4:8], C("ones"), gl[:, 3, 0:4], False, True).then_inc(S("bcum"), 1)
                pe.wait_ge(S("gate_cols"), 2)
                for what in range(2):
                    for tt in range(2):
                        m = nc.tensor.transpose(ps[0:4, 4, what * T + tt * P:what * T + tt * P + P],
                                                gl[:, 4 + what, tt * 4:tt * 4 + 4], C("ident"))
                m.then_inc(S("gate_rows"), 1)
                pe.wait_ge(S("row_max"), 3)
                pe.wait_ge(S("qk_ready"), 2)
                pe.wait_ge(S("rope_done"), 3)

                def front(h):
                    b = 4 * (h % 2)
                    if h >= 2:
                        pe.wait_ge(S("mlstm_h"), h - 1)
                    one = C("pick", 512, 4)[:, h * P:(h + 1) * P]
                    mm(ps[:, b + 1, 0:T], one, rows4[:, 2, :], True, False)
                    mm(ps[:, b + 1, 0:P], ident_bf[:], before_bf[:], False, True)
                    mm(ps[:, b + 1, T:T + P], one, rows4[:, 2, P:T], True, False)
                    mm(ps[:, b + 1, T:T + P], ident_bf[:], before_bf[:], False, True)
                    mm(ps[:, b, 0:T], one, rows4[:, 3, :])
                    mm(ps[:, b + 2, 0:T], qk[:, 4 + h, 0:P], qk[:, h, :])
                    mm(ps[:, b + 2, T:T + P], qk[:, 4 + h, P:T], qk[:, h, P:T]).then_inc(S("mlstm_s"), 1)

                def back(h):
                    b = 4 * (h % 2)
                    pe.wait_ge(S("mlstm_st"), h + 1)
                    st = mST[:, h % 2, :]
                    for out, l0, l1 in ((0, vtok[:, 0, h * P:(h + 1) * P], vtok[:, 1, h * P:(h + 1) * P]),
                                        (T, C("ones"), C("ones"))):
                        mm(ps[:, b + 3, out:out + T], l0, st[:, 0:T], True, False)
                        m = mm(ps[:, b + 3, out + P:out + T], l1, st[:, T:T + P], False, True)
                    m.then_inc(S("mlstm_o"), 1)

                for h in range(5):
                    if h < 4:
                        front(h)
                    if h >= 1:
                        back(h - 1)
                pe.wait_ge(*once("mh_sq"))
                for j in range(2):
                    m = mm(ps[:, 4 + j, :], C("ones"), sq[:, 4 * j:4 * j + 4, 0:P].rearrange("p a b -> p a b"))
                m.then_inc(S("mh_ss"), 1)

            def attention():
                pe.wait_ge(S("rope_done"), 4)
                pe.wait_ge(*once("mh_rs"))
                for qt in range(2):
                    for h in range(8):
                        i, g = h % 4, h // 4
                        m = mm(ps[:, 6 + g, (qt * 4 + i) * NCMP:(qt * 4 + i + 1) * NCMP],
                               nqk[64 * g:64 * g + 64, i, qt * P:(qt + 1) * P], kct[64 * g:64 * g + 64, 3, :])
                m.then_inc(S("cmp_s"), 1)

                def scores(n):
                    qt, g = n // 2, n % 2
                    nk = P * (qt + 1)
                    for i in range(4):
                        if n >= 1:
                            pe.wait_ge(S("att_exp"), 8 * (n - 1) + 2 * i + 2)
                        q = nqk[64 * g:64 * g + 64, i, qt * P:(qt + 1) * P]
                        for kind in range(2):
                            o = kind * T
                            mm(ps[:, i, o:o + nk], q, nqk[64 * g:64 * g + 64, 4 + kind, 0:nk], True, False)
                            m = mm(ps[:, i, o + nk - P:o + nk], ident_bf[:], later_bf[:], False, True)
                        m.then_inc(S("att_s"), 1)

                turn = [0]

                def outputs(n):
                    qt, g = n // 2, n % 2
                    pe.wait_ge(S("att_p"), 8 * n + 8)
                    pe.wait_ge(*once("cmp_p"))
                    parts = [(None, 0)] + [(kind, st) for kind in range(2) for st in range(qt + 1)]
                    if n >= 2:
                        pe.wait_ge(S("att_o"), n - 1)
                    for j, (kind, st) in enumerate(parts):
                        t = turn[0]
                        turn[0] += 1
                        if t >= 2:
                            pe.wait_ge(S("att_pt"), t - 1)
                        for i in range(4):
                            if kind is None:
                                m = nc.tensor.transpose(ps[0:NCMP, 4 + t % 2, i * P:(i + 1) * P],
                                                        pc[:, qt * 8 + 4 * g + i, :], C("ident"))
                            else:
                                m = nc.tensor.transpose(ps[:, 4 + t % 2, i * P:(i + 1) * P],
                                                        prob[:, n % 2, i, kind * T + st * P:kind * T + (st + 1) * P], C("ident"))
                        m.then_inc(S("att_tr"), 1)
                        pe.wait_ge(S("att_pt"), t + 1)
                        out = ps[64 * g:64 * g + 64, 6 + n % 2, :]
                        if kind is None:
                            m = mm(out, vct[:, 64 * g:64 * g + 64], pt[0:NCMP, t % 2, :], True, False)
                        else:
                            m = mm(out, vsw[:, kind, st, 64 * g:64 * g + 64], pt[:, t % 2, :], False, j == len(parts) - 1)
                    m.then_inc(S("att_av"), 1)

                for n in range(5):
                    if n < 4:
                        scores(n)
                    if n == 0:
                        pe.wait_ge(*once("cmp_e"))
                    if n >= 1:
                        outputs(n - 1)

            def project(u0, g0, ready, n, t0, src=None):
                for sem, value in ready:
                    pe.wait_ge(S(sem), value)
                for m in range(KT):
                    feature_tile(u0 + m, g0 + m, mixT, t0, TT)

            def hgrn_in():
                pe.wait_ge(S("norm_h"), 2 * KT)
                for j in range(H_UNITS):
                    if H_OWNER[j] == "v":
                        token_tile(U_H + j, G_H + j, hT, TM)
                    else:
                        feature_tile(U_H + j, G_H + j, hT, TM, TT)

            def hgrn():
                pe.wait_ge(S("drained_a"), drained("a", G_HO - 1))
                for lev in range(9):
                    q = qkl[:, lev % 2, :].rearrange("p (h t w) -> p h t w", h=8, t=2)
                    pe.wait_ge(S("lev_qk"), 2 * lev + 2)
                    if lev < 8:
                        b0 = 4 * (lev % 2)
                        if lev >= 2:
                            pe.wait_ge(S("lev_a"), 4 * (lev - 1))
                        for j in range(16):
                            h, tt = j // 2, j % 2
                            key = q[:, h, tt, :] if lev else fK[:, h, tt * P:(tt + 1) * P]
                            query = q[:, h, tt, :] if lev else fQ[:, h, tt * P:(tt + 1) * P]
                            m = mm(ps[:, b0 + j // 4, (j % 4) * P:(j % 4 + 1) * P], key, query)
                            if j % 4 == 3:
                                m.then_inc(S("lev_s"), 1)
                    else:
                        pe.wait_ge(S("lev_a"), 4 * 7)
                        for h in range(8):
                            m = mm(ps[:, h // 4, (h % 4) * P:(h % 4 + 1) * P], q[:, h, 0, :], q[:, h, 1, :])
                            if h % 4 == 3:
                                m.then_inc(S("lev_s"), 1)
                pe.wait_ge(S("lev_a"), 4 * 8 + 2)
                for h in range(8):
                    o = ps[:, 4 + h // 2, (h % 2) * T:(h % 2 + 1) * T]
                    mm(o, ivt[:, 0, h * P:(h + 1) * P], hA[:, h, 0:2, :].rearrange("p a b -> p (a b)"), True, False)
                    m = mm(o[:, P:T], ivt[:, 1, h * P:(h + 1) * P], hA[:, h, 2, :], False, True)
                m.then_inc(S("hg_o"), 1)
                pe.wait_ge(*once("hg_sq"))
                for j in range(4):
                    m = mm(ps[:, j, :], C("ones"), dif[:, 0, j * 512:(j + 1) * 512])
                m.then_inc(S("hg_ss"), 1)

            def ffn(tag, u0, g0):
                d0 = drained("v", g0 - 1)
                pe.wait_ge(S("norm_h"), (NORMS.index(tag) + 1) * KT)

                def gate_up(it, f4):
                    for j in range(2 * f4, 2 * f4 + 2):
                        pe.wait_ge(S(f"w_ready{(u0 + j) % SLOTS}"), it * 16 + 16 * ((u0 + j) // SLOTS + 1))
                        pe.wait_ge(S("drained_v"), it * 8 + (d0 + j - 3))
                        for k in range(KT):
                            m = mm(ps[:, (g0 + j) % MM_BANKS, 0:TT], ring[:, (u0 + j) % SLOTS, k * P:(k + 1) * P],
                                   hT[:, k, :], k == 0, k == KT - 1)
                        m.then_inc(S("w_used"), 1)

                with pe.Fori(0, FT // 4) as it:
                    for f4 in range(4):
                        gate_up(it, f4)
                for f4 in range(FT % 4):
                    gate_up(FT // 4, f4)
                pe.wait_ge(S("drained_v"), d0 + GU_UNITS)
                for m in range(KT):
                    b = bank(g0 + GU_UNITS + m)
                    for k in range(FT):
                        n = m * FT + k
                        u = u0 + GU_UNITS + n // KT
                        if n % KT == 0:
                            weights(u)
                        last = mm(ps[:, b, 0:TT], ring[:, u % SLOTS, (n % KT) * P:(n % KT + 1) * P], fact[:, k, :],
                                  k == 0, k == FT - 1)
                        if n % KT == KT - 1:
                            last.then_inc(S("w_used"), 1)

            def mixer_in():
                pe.wait_ge(S("norm_h"), 4 * KT)
                for j in range(P_UNITS):
                    feature_tile(U_P + j, G_P + j, hT, 0, TT)

            def decays():
                pe.wait_ge(*once("lora_th"))
                low = pr[:, 12, 1:1 + TT]
                for j in range(4):
                    mm(ps[:, j, 0:TT], mat[0:32, MAT["wup"] + j * P:MAT["wup"] + (j + 1) * P], low[0:32])
                    m = mm(ps[:, 4 + j, 0:TT], mat[32:64, MAT["wup"] + j * P:MAT["wup"] + (j + 1) * P], low[32:64])
                m.then_inc(S("lora_up"), 1)
                pe.wait_ge(*once("kk_sq"))
                for j in range(4):
                    m = mm(ps[:, j, 0:TT], C("blk"), pT[:, j, :])
                m.then_inc(S("kk_ss"), 1)

            def sticks():
                pe.wait_ge(*once("kk_n2"))
                pe.wait_ge(S("sb_pad"), 2)
                for tt in range(3):
                    for j in range(4):
                        m = nc.tensor.transpose(ps[:, 4 + tt, j * P:(j + 1) * P], sbv[:, j, tt * P:(tt + 1) * P], C("ident"))
                m.then_inc(S("sb_vt"), 1)
                pe.wait_ge(*once("sb_v"))
                for h in range(10):
                    if h < 8:
                        a, j, b = 64 * (h % 2), h // 2, h % 4
                        if h >= 4:
                            pe.wait_ge(S("sb_ln"), h - 3)
                        mm(ps[:, b, 0:272], sbk[a:a + 64, j, 0:P], sbq[a:a + 64, j, :])
                        mm(ps[:, b, 272:416], sbk[a:a + 64, j, P:2 * P], sbq[a:a + 64, j, P:TT])
                        mm(ps[:, b, 416:432], sbk[a:a + 64, j, 2 * P:3 * P], sbq[a:a + 64, j, 2 * P:TT]).then_inc(S("sb_z"), 1)
                    if 1 <= h <= 8:
                        r, o = h - 1, ps[:, 4 + (h - 1) % 2, :]
                        pe.wait_ge(S("sb_sp"), r + 1)
                        if r >= 2:
                            pe.wait_ge(S("sb_arg"), r - 1)
                        s = zp[:, r % 2, :]
                        mm(o[:, 0:272], C("ge"), s[:, 0:272], True, False)
                        mm(o[:, 128:272], C("ones"), s[:, 272:416], False, False)
                        mm(o[:, 256:272], C("ones"), s[:, 416:432], False, False)
                        mm(o[:, 0:128], ident_bf[:], notyet_bf[:], False, True)
                        mm(o[:, 272:416], C("ge"), s[:, 272:416], True, False)
                        mm(o[:, 400:416], C("ones"), s[:, 416:432], False, False)
                        mm(o[:, 272:400], ident_bf[:], notyet_bf[:], False, True)
                        mm(o[:, 416:432], C("ge"), s[:, 416:432], True, False)
                        mm(o[:, 416:432], ident_bf[:], notyet_bf[:, 0:16], False, True).then_inc(S("sb_rest"), 1)
                    if h >= 2:
                        r = h - 2
                        a, o, A = 64 * (r % 2), ps[64 * (r % 2):64 * (r % 2) + 64, 6 + r % 2, :], zA[:, r % 2, :]
                        pe.wait_ge(S("sb_A"), r + 1)
                        if r >= 2:
                            pe.wait_ge(S("sb_out"), r - 1)
                        mm(o[:, 0:272], sbvt[:, 0, r * 64:r * 64 + 64], A[:, 0:272], True, False)
                        mm(o[:, 128:272], sbvt[:, 1, r * 64:r * 64 + 64], A[:, 272:416], False, False)
                        mm(o[:, 256:272], sbvt[:, 2, r * 64:r * 64 + 64], A[:, 416:432], False, True).then_inc(S("sb_av"), 1)

            def rwkv():
                pe.wait_ge(S("bk_ready"), 2)
                pe.wait_ge(S("sb_out"), 8)
                nth = [0]
                for tau, (t0, n) in enumerate(TILES2):
                    ar = lambda h: AR[64 * (h % 2):64 * (h % 2) + 64, h // 2, :, t0:t0 + n]
                    bk = lambda h, w: BK[64 * (h % 2):64 * (h % 2) + 64, h // 2, w, t0:t0 + n]
                    if tau:
                        pe.wait_ge(S("y_done"), tau)
                    for h in range(8):
                        m = mm(ps[0:n, 6 + h % 2, (h // 2) * n:(h // 2 + 1) * n], ar(h)[:, 0, :], bk(h, 0))
                    m.then_inc(S("r_ab"), 1)
                    for h in range(8):
                        b = h % 6
                        if h >= 6:
                            pe.wait_ge(S("r_mask"), 8 * tau + h - 5)
                        o = ps[0:n, b, 0:4 * n].rearrange("p (k w t) -> p k w t", k=2, w=2)
                        mm(o[:, 0], bk(h, 0), ar(h))
                        mm(o[:, 1], bk(h, 1), ar(h)).then_inc(S("r_mats"), 1)
                    for w in range(4):
                        b = 2 + w
                        pe.wait_ge(S("r_mask"), 8 * tau + b + 1)
                        for j in range(4):
                            src = (AR[:, j, 0, t0:t0 + n], BK[:, j, 0, t0:t0 + n], BK[:, j, 1, t0:t0 + n],
                                   pr[:, 8 + j, 1 + t0:1 + t0 + n])[w]
                            m = nc.tensor.transpose(ps[0:n, b, j * P:(j + 1) * P], src, C("ident"))
                        m.then_inc(S("r_tok"), 1)
                    levels = [b for b in LEVELS[1:6] if b < n]
                    pe.wait_ge(S("r_tokc"), 4 * tau + 4)
                    for lev in levels:
                        nth[0] += 1
                        i = nth[0]
                        pe.wait_ge(S("r_n"), i)
                        for q in range(8):
                            m = mm(ps[0:n, q // 4, (q % 4) * n:(q % 4 + 1) * n], rN[0:n, q, 0:n], rG[0:n, q, 0:n])
                        m.then_inc(S("r_x"), 1)
                        pe.wait_ge(S("r_xc"), i)
                        for q in range(8):
                            mm(ps[0:n, 2 + q // 4, (q % 4) * n:(q % 4 + 1) * n], rI[0:n, q, 0:n], rX[0:n, q, 0:n])
                            m = mm(ps[0:n, 4 + q // 4, (q % 4) * n:(q % 4 + 1) * n], rX[0:n, q, 0:n], rI[0:n, q, 0:n])
                        m.then_inc(S("r_d"), 1)
                    for h in range(8):
                        q = (h % 2) * 4 + h // 2
                        m = mm(ps[0:n, 6, h * 64:h * 64 + 64], rA[0:n, q, 2 * n:3 * n], tok[0:n, 2, h * 64:h * 64 + 64])
                    m.then_inc(S("r_w"), 1)
                    pe.wait_ge(S("r_wc"), tau + 1)
                    pe.wait_ge(S("r_g"), tau + 1)
                    for h in range(8):
                        q = (h % 2) * 4 + h // 2
                        m = mm(ps[0:n, h // 4, (h % 4) * P:(h % 4 + 1) * P], rG[0:n, q, 0:n], rWA[0:n, h, :])
                    m.then_inc(S("r_u"), 1)
                    pe.wait_ge(S("r_uc"), tau + 1)
                    for h in range(8):
                        q, a = (h % 2) * 4 + h // 2, 64 * (h % 2)
                        col = slice((h // 2) * n, (h // 2 + 1) * n)
                        mm(ps[a:a + 64, 2, col], rUM[0:n, h, 64:128], rA[0:n, q, n:2 * n])
                        mm(ps[a:a + 64, 3, col], rUM[0:n, h, 0:64], rA[0:n, q, n:2 * n], True, False)
                        m = mm(ps[a:a + 64, 3, col], tok[0:n, 2, h * 64:h * 64 + 64], rA[0:n, q, 3 * n:4 * n], False, True)
                    m.then_inc(S("r_y0"), 1)
                    chunks = [c for c, (s, _) in enumerate(RW_CHUNKS) if t0 <= s < t0 + n]
                    if tau < 2:
                        for c in chunks:
                            rows = slice(64 * (c % 2), 64 * (c % 2) + 64)
                            for h in range(8):
                                a, hh = 64 * (h % 2), slice(h * 64, h * 64 + 64)
                                o = slice((h // 2) * 64, (h // 2 + 1) * 64)
                                mm(ps[a:a + 64, 4 + c % 2, o], rUM[rows, h, 64:128], tok[rows, 0, hh])
                                o = slice(256 + (h // 2) * 64, 256 + (h // 2 + 1) * 64)
                                mm(ps[a:a + 64, 4 + c % 2, o], tok[rows, 0, hh], rUM[rows, h, 0:64], True, False)
                                m = mm(ps[a:a + 64, 4 + c % 2, o], tok[rows, 1, hh], tok[rows, 2, hh], False, True)
                            m.then_inc(S("r_phi"), 1)
                    for c in chunks:
                        cols = RW_CHUNKS[c]
                        if c >= 1:
                            pe.wait_ge(S("r_state"), c)
                            pe.wait_ge(S("r_r"), tau + 1)
                            for h in range(8):
                                a = 64 * (h % 2)
                                o = (h // 2) * n + cols[0] - t0
                                m = mm(ps[a:a + 64, 6 + h % 2, o:o + cols[1]], state[a:a + 64, c % 2, h // 2, :],
                                       rR[a:a + 64, h // 2, cols[0] - t0:cols[0] - t0 + cols[1]])
                            m.then_inc(S("r_ys"), 1)
                            if c < 4:
                                pe.wait_ge(S("r_phic"), c + 1)
                                for h in range(8):
                                    a = 64 * (h % 2)
                                    m = mm(ps[a:a + 64, h % 2, (h // 2) * 64:(h // 2 + 1) * 64],
                                           phi[a:a + 64, c % 2, h // 2, :], state[a:a + 64, c % 2, h // 2, :])
                                m.then_inc(S("r_s"), 1)
                pe.wait_ge(S("y_done"), 3)
                for j in range(4):
                    m = mm(ps[:, j, 0:TT], C("blk"), yT[:, j, :])
                m.then_inc(S("gn_mean"), 1)
                pe.wait_ge(*once("gn_sq"))
                for j in range(4):
                    m = mm(ps[:, 4 + j, 0:TT], C("blk"), pT[:, j, :])
                m.then_inc(S("gn_var"), 1)
                pe.wait_ge(*once("bonus_in"))
                for j in range(4):
                    m = mm(ps[:, j, 0:TT], C("blk"), pK[:, j, :])
                m.then_inc(S("bonus"), 1)
                pe.wait_ge(*once("g_in"))
                pe.wait_ge(*once("gn_rs"))
                for j in range(4):
                    m = mm(ps[:, 4 + j, 0:TT], mat[:, MAT["gup"] + j * P:MAT["gup"] + (j + 1) * P], pr[:, 13, 1:1 + TT])
                m.then_inc(S("g_out"), 1)

            norm("norm0", T)
            even_in()
            compress()
            mlstm()
            attention()
            project(U_EO, G_EO, (("m_out", 4), ("att_o", 4)), T, TM)
            norm("norm1", T)
            hgrn_in()
            hgrn()
            project(U_HO, G_HO, (("hg_out", 8),), T, TM)
            norm("ffn1", TT)
            ffn("ffn1", U_F1, G_F1)
            norm("mix", TT)
            mixer_in()
            decays()
            sticks()
            rwkv()
            project(U_PO, G_PO, (("sb_out", 8), ("rw_out", 4)), TT, 0)
            norm("ffn2", TT)
            ffn("ffn2", U_F2, G_F2)
            norm("final", TT)

        @block.scalar
        def _(act):
            step, act_n = in_order(act, "act_step")

            def func(out, in_, f, sem="act_step", **kw):
                step(nc.scalar.activation(out, in_, f, **kw), sem)

            LOG_EXP = "natural_log_exp_and_others"

            def norm(tag, c0, n):
                nc.scalar.preload_act_table_set(LOG_EXP)
                for k in range(KT):
                    if tag == "norm0":
                        act.wait_ge(S("x_in"), 16)
                        act.wait_ge(S("setup"), 11)
                    else:
                        act.wait_ge(S(before_norm[tag][0]), before_norm[tag][1] + k + 1)
                    func(sq[:, k, 0:n], xT[:, k, c0:c0 + n], ACT.Square, "norm_sq")
                act.wait_ge(S("norm_ss"), NORMS.index(tag) + 1)
                func(rstd[:, 0:n], ps[:, 7, 0:n], ACT.Ln, scale=1.0 / D, bias=eps[:, 0:1])
                func(rstd[:, 0:n], rstd[:, 0:n], ACT.Exp, "norm_rstd", scale=-0.5)

            before_norm = {"norm1": ("drained_v", drained("v", G_EO - 1)), "ffn1": ("drained_v", drained("v", G_HO - 1)),
                           "mix": ("drained_v", drained("v", G_F1 + GU_UNITS - 1)), "ffn2": ("drained_v", drained("v", G_PO - 1)),
                           "final": ("drained_v", drained("v", G_F2 + GU_UNITS - 1))}

            def drain(g, out, width=T, bias=None, rows=P):
                act.wait_ge(S("w_used"), used_by(g))
                kw = {"bias": bias} if bias is not None else {}
                func(out, ps[0:rows, g % MM_BANKS, 0:width], ACT.Identity, "drained_a", **kw)

            def even_in():
                dst = {1: kcvc[:, 0, :], 2: kcvc[:, 1, :]}
                for j in range(6):
                    dst[3 + j] = nqk[:, j, :]
                for j in range(8):
                    dst[11 + j] = qkpre[:, j, 3:3 + T]
                    dst[23 + j] = oz[:, j, :]
                for j in range(4):
                    dst[31 + j] = nz[:, j, :]
                for j in range(E_UNITS):
                    if E_OWNER[j] == "a":
                        drain(G_E + j, dst[j], bias=V("ev_b", j))

            def compress():
                act.wait_ge(*once("hx_x"))
                func(hx[:, 1, :], hx[:, 0, :], ACT.Square, "hx_sq")
                act.wait_ge(*once("hx_arg"))
                func(hx[:, 2, :], hx[:, 1, :], ACT.Tanh, "hx_th", scale=0.7978845608028654)
                act.wait_ge(*once("w2_done"))
                func(vct[:], ps[0:NCMP, 6, 128:256], ACT.Copy)
                func(kct[:, 0, :], ps[:, 6, 64:64 + NCMP], ACT.Copy)
                func(kct[:, 1, :], kct[:, 0, :], ACT.Square, "kc_sq")
                act.wait_ge(*once("kc_ss"))
                func(kct[:, 3, :], ps[:, 6, 256:256 + NCMP], ACT.Ln, scale=1.0 / 64, bias=eps[:, 0:1])
                func(kct[:, 3, :], kct[:, 3, :], ACT.Exp, "kc_rs", scale=-0.5)
                func(rs[:], nqk[:], ACT.Square, "nqk_sq")
                act.wait_ge(*once("nqk_ss"))
                r = rs[:].rearrange("p a b -> p (a b)").rearrange("p (a b) -> p a b", b=512)
                func(r, ps[:, 0:3, :], ACT.Ln, scale=1.0 / 64, bias=eps[:, 0:1])
                func(rs[:], rs[:], ACT.Exp, "nqk_rs", scale=-0.5)

            def mlstm():
                act.wait_ge(S("fgate"), 2)
                func(gl[:, 1, :], gl[:, 0, :], ACT.Abs)
                func(gl[:, 1, :], gl[:, 1, :], ACT.Exp, scale=-1.0)
                func(gl[:, 2, :], gl[:, 1, :], ACT.Ln, "log1p", bias=eps[:, 2:3])
                func(small[:, :, 8:32], small[:, :, 8:32], ACT.Tanh, "gates_th", scale=0.5)
                act.wait_ge(S("conv"), 8)
                func(th[:], qk[:], ACT.Tanh, "qk_th", scale=0.5)
                for h in range(5):
                    if h < 4:
                        b = 4 * (h % 2)
                        act.wait_ge(S("mlstm_s"), h + 1)
                        if h >= 2:
                            act.wait_ge(S("mlstm_h"), h - 1)
                        func(mE[:, h % 2, 0:T], ps[:, b + 1, 0:T], ACT.Exp, scale=-1.0, bias=gl[:, 5, h:h + 1])
                        func(mE[:, h % 2, T:T + P], ps[:, b + 1, T:T + P], ACT.Exp, "mlstm_e", scale=-1.0,
                             bias=gl[:, 5, 4 + h:5 + h])
                        func(mem[:, h % 2, :], ps[:, b, 0:T], ACT.Exp, scale=-1.0)
                    if h >= 1:
                        act.wait_ge(S("mlstm_o"), h)
                        func(mad[:, (h - 1) % 2, :], ps[:, 4 * ((h - 1) % 2) + 3, T:2 * T], ACT.Abs, "mlstm_d")
                act.wait_ge(S("mlstm_h"), 4)
                func(sq[:, :, 0:P], hm[:].rearrange("p a b -> p (a b)").rearrange("p (a b) -> p a b", b=P), ACT.Square, "mh_sq")
                act.wait_ge(*once("mh_ss"))
                r = rs[:, 0:4, :].rearrange("p a b -> p (a b)").rearrange("p (a b) -> p a b", b=512)
                func(r, ps[:, 4:6, :], ACT.Ln, scale=1.0 / P, bias=eps[:, 0:1])
                func(rs[:, 0:4, :], rs[:, 0:4, :], ACT.Exp, "mh_rs", scale=-0.5)
                func(th[:], oz[:], ACT.Tanh, "oz_th", scale=0.5)
                act.wait_ge(S("m_out"), 4)
                func(th[:, 0:4, :], nz[:], ACT.Tanh, "nz_th", scale=0.5)

            def attention():
                act.wait_ge(*once("cmp_sub"))
                func(pc[:], pc[:], ACT.Exp, "cmp_e")
                turn = [0]
                for n in range(5):
                    if n < 4:
                        qt = n // 2
                        nk = P * (qt + 1)
                        for i in range(4):
                            act.wait_ge(S("att_max"), 4 * n + i + 1)
                            if n >= 2:
                                act.wait_ge(S("att_av"), n - 1)
                            for kind in range(2):
                                func(prob[:, n % 2, i, kind * T:kind * T + nk], ps[:, i, kind * T:kind * T + nk], ACT.Exp, "att_exp",
                                     bias=pst[:, n % 2, i, kind:kind + 1], accum_out=pst[:, n % 2, i, 2 + kind:3 + kind])
                    if n >= 1:
                        for j in range(1 + 2 * ((n - 1) // 2 + 1)):
                            t = turn[0]
                            turn[0] += 1
                            act.wait_ge(S("att_tr"), t + 1)
                            rows = NCMP if j == 0 else P
                            func(pt[0:rows, t % 2, :], ps[0:rows, 4 + t % 2, :], ACT.Copy, "att_pt")

            def hgrn_in():
                act.wait_ge(*once("lb_arg"))
                func(lbs[:, 0, :], lbs[:, 0, :], ACT.Tanh, "lb_th", scale=0.5)
                for j in range(H_UNITS):
                    if H_OWNER[j] == "a":
                        kind = j // 8
                        dst = {0: fF, 1: fQ, 3: fZ}[kind][:, j % 8, :]
                        drain(G_H + j, dst, bias=V({0: "fp_b", 1: "qp_b", 3: "z_b"}[kind], j % 8))
                        if j == 7:
                            func(dif[:, 1, :].rearrange("p (a b) -> p a b", a=8), fF[:], ACT.Tanh, "f_th", scale=0.5)
                            act.wait_ge(S("f_ready"), 8)
                            func(fF[:], fF[:], ACT.Ln, "f_log")
                        if j == 15:
                            act.wait_ge(*once("f_read"))
                            func(dif[:, 1, :].rearrange("p (a b) -> p a b", a=8), fQ[:], ACT.Tanh, "q_th", scale=0.5)

            def hgrn():
                act.wait_ge(*once("q_ready"))
                func(fF[:], fZ[:], ACT.Tanh, "z_th", scale=0.5)
                for lev, b in enumerate(LEVELS + (P,)):
                    act.wait_ge(S("lev_d"), lev + 1)
                    d = dif[:, lev % 2, :].rearrange("p (n w) -> p n w", w=2 * b)
                    func(d[:, :, 0:b], d[:, :, 0:b], ACT.Exp, "lev_e", scale=-1.0)
                    func(d[:, :, b:], d[:, :, b:], ACT.Exp, "lev_e")
                act.wait_ge(*once("hg_o"))
                func(dif[:, 0, :], ps[:, 4:8, :].rearrange("p a b -> p (a b)"), ACT.Square, "hg_sq")
                act.wait_ge(*once("hg_ss"))
                func(dif[:, 1, :], ps[:, 0:4, :].rearrange("p a b -> p (a b)"), ACT.Ln, scale=1.0 / P, bias=eps[:, 0:1])
                func(dif[:, 1, :], dif[:, 1, :], ACT.Exp, "hg_rs", scale=-0.5)

            def ffn(u0, g0, first):
                d0 = drained("v", g0 - 1)

                def gate(it, f4):
                    act.wait_ge(S("w_used"), it * 8 + (u0 + 2 * f4 + 1))
                    act.wait_ge(S("drained_v"), it * 8 + (d0 + 2 * f4 + 1 - 8))
                    nc.scalar.activation(fth[:, f4, :], ps[:, (g0 + 2 * f4) % MM_BANKS, 0:TT], ACT.Tanh,
                                         scale=0.5).then_inc(S("ffn_th"), 1)

                with act.Fori(0, FT // 4) as it:
                    for f4 in range(4):
                        gate(it, f4)
                for f4 in range(FT % 4):
                    gate(FT // 4, f4)
                act.wait_ge(S("ffn_th"), first + FT)

            def mixer_in():
                for j in range(P_UNITS):
                    if j < 12:
                        dst = (sbq, sbk, sbv)[j // 4][:, j % 4, 0:TT]
                        act.wait_ge(S("w_used"), used_by(G_P + j))
                        func(dst, ps[:, (G_P + j) % MM_BANKS, 0:TT], ACT.Copy, "drained_a", scale=0.125 if j < 4 else 1.0)
                    else:
                        drain(G_P + j, pr[:, j - 12, 1:1 + TT], TT)
                act.wait_ge(S("shifted"), 14)
                func(pr[0:32, 12, 1:1 + TT], pr[0:32, 12, 1:1 + TT], ACT.Tanh, "lora_th")
                func(pr[:, 13, 1:1 + TT], pr[:, 13, 1:1 + TT], ACT.Tanh, "g_th", scale=0.5)
                act.wait_ge(*once("lora_up"))
                for j in range(4):
                    func(pD[:, j, :], ps[:, j, 0:TT], ACT.Tanh, "decay_th" if j == 3 else "act_step", scale=0.5, bias=V("w0", j))
                for j in range(4):
                    func(pA[:, j, :], ps[:, 4 + j, 0:TT], ACT.Tanh, "a_th" if j == 3 else "act_step", scale=0.5, bias=V("a0", j))
                nc.scalar.preload_act_table_set(LOG_EXP)
                act.wait_ge(S("kk_raw"), 4)
                func(pT[:], pK[:], ACT.Square, "kk_sq")
                act.wait_ge(*once("kk_n2"))
                func(pT[:], pT[:], ACT.Ln, scale=2.0 ** 20)
                func(pT[:], pT[:], ACT.Exp, "kk_rs", scale=-0.5, bias=eps[:, 3:4])
                act.wait_ge(*once("cum"))
                func(pT[:], pC[:], ACT.Exp, "e_c")
                act.wait_ge(*once("cum_x"))
                func(pD[:], pD[:], ACT.Exp, "e_cx")
                func(pC[:], pC[:], ACT.Exp, "e_nc", scale=-1.0)

            def sticks():
                act.wait_ge(*once("sb_vt"))
                func(sbvt[:], ps[:, 4:7, :], ACT.Copy, "sb_v")
                for h in range(10):
                    if h < 8:
                        p = h % 2
                        act.wait_ge(S("sb_z"), h + 1)
                        if h >= 2:
                            act.wait_ge(S("sb_arg"), h - 1)
                        z = ps[:, h % 4, 0:432]
                        func(zs[:, p, :], z, ACT.Copy)
                        func(zl[:, p, :], z, ACT.Abs)
                        func(zl[:, p, :], zl[:, p, :], ACT.Exp, scale=-1.0)
                        func(zl[:, p, :], zl[:, p, :], ACT.Ln, "sb_ln", bias=eps[:, 2:3])
                    if 1 <= h <= 8:
                        r = h - 1
                        act.wait_ge(S("sb_arg"), r + 1)
                        if r >= 2:
                            act.wait_ge(S("sb_av"), r - 1)
                        func(zA[:, r % 2, :], zs[:, r % 2, :], ACT.Exp, "sb_A")
                    if h >= 2:
                        r = h - 2
                        a = 64 * (r % 2)
                        act.wait_ge(S("sb_av"), r + 1)
                        func(mixT[a:a + 64, r // 2, :], ps[a:a + 64, 6 + r % 2, 0:TT], ACT.Copy, "sb_out")

            def rwkv():
                nth = [0]
                for tau, (t0, n) in enumerate(TILES2):
                    for w in range(4):
                        act.wait_ge(S("r_tok"), 4 * tau + w + 1)
                        src = ps[0:n, 2 + w, :]
                        if w == 0:
                            func(rWA[0:n, :, 64:128], src.rearrange("p (h j) -> p h j", j=64), ACT.Copy, "r_tokc")
                        else:
                            func(tok[0:n, w - 1, :], src, ACT.Copy, "r_tokc")
                    for _ in [b for b in LEVELS[1:6] if b < n]:
                        nth[0] += 1
                        act.wait_ge(S("r_x"), nth[0])
                        for q in range(2):
                            func(rX[0:n, 4 * q:4 * q + 4, 0:n], ps[0:n, q, 0:4 * n].rearrange("p (q t) -> p q t", q=4), ACT.Copy,
                                 "r_xc" if q else "act_step")
                    act.wait_ge(S("r_w"), tau + 1)
                    func(rWA[0:n, :, 0:64], ps[0:n, 6, :].rearrange("p (h j) -> p h j", j=64), ACT.Copy, "r_wc")
                    act.wait_ge(S("r_u"), tau + 1)
                    for q in range(2):
                        func(rUM[0:n, 4 * q:4 * q + 4, :], ps[0:n, q, :].rearrange("p (q t) -> p q t", q=4), ACT.Copy,
                             "r_uc" if q else "act_step", scale=-1.0)
                    act.wait_ge(S("r_y0"), tau + 1)
                    func(yT[:, :, t0:t0 + n], ps[:, 3, 0:4 * n].rearrange("p (q t) -> p q t", q=4), ACT.Copy, "r_y0c")
                act.wait_ge(S("gn_d"), 4)
                func(pT[:], yT[:], ACT.Square, "gn_sq")
                act.wait_ge(*once("gn_var"))
                nc.scalar.preload_act_table_set(LOG_EXP)
                func(pT[:], ps[:, 4:8, 0:TT], ACT.Ln, scale=1.0 / 64, bias=eps[:, 1:2])
                func(pT[:], pT[:], ACT.Exp, "gn_rs", scale=-0.5)

            norm("norm0", TM, T)
            even_in()
            compress()
            mlstm()
            attention()
            norm("norm1", TM, T)
            hgrn_in()
            hgrn()
            norm("ffn1", 0, TT)
            ffn(U_F1, G_F1, 0)
            norm("mix", 0, TT)
            mixer_in()
            sticks()
            rwkv()
            norm("ffn2", 0, TT)
            ffn(U_F2, G_F2, FT)
            norm("final", 0, TT)

        @block.vector
        def _(dve):
            step, dve_n = in_order(dve, "dve_step")

            def tt(out, a, b, op, sem="dve_step"):
                step(nc.vector.tensor_tensor(out, a, b, op), sem)

            def ts(out, a, s1, s2, op0, op1=None, sem="dve_step"):
                if op1 is None:
                    step(nc.vector.tensor_scalar(out, a, s1, s2, op0), sem)
                else:
                    step(nc.vector.tensor_scalar(out, a, s1, s2, op0, op1), sem)

            def stt(out, a, s, b, op0, op1, sem="dve_step"):
                step(nc.vector.scalar_tensor_tensor(out=out, in0=a, scalar=s, in1=b, op0=op0, op1=op1), sem)

            def norm(tag, c0, n, w, src=None):
                dve.wait_ge(S("norm_rstd"), NORMS.index(tag) + 1)
                for k in range(KT):
                    stt(hT[:, k, c0:c0 + n], xT[:, k, c0:c0 + n], V(w, k), rstd[:, 0:n], ALU.mult, ALU.mult, "norm_h")

            def setup():
                for j, v in enumerate((EPS, LNX_EPS, 1.0, 10 * float(np.log(2.0)))):
                    step(nc.vector.memset(eps[:, j:j + 1], v), "setup")
                step(nc.vector.memset(qkpre[:, :, 0:3], 0.0), "setup")
                dve.wait_ge(S("consts_in"), 64)
                step(nc.vector.tensor_copy(ident_bf[:], C("ident")), "setup")
                ts(before_bf[:], C("gt"), BIG, None, ALU.mult, sem="setup")
                ts(notyet_bf[:], C("ge"), BIG, None, ALU.mult, sem="setup")
                ts(later_bf[:], C("ge"), 1.0, BIG, ALU.subtract, ALU.mult, sem="setup")
                ts(vec[:, VEC["w0"]:VEC["w0"] + 8], vec[:, VEC["w0"]:VEC["w0"] + 8], 0.5, None, ALU.mult, sem="setup")
                ts(vec[:, VEC["nqk"]:VEC["nqk"] + 4], vec[:, VEC["nqk"]:VEC["nqk"] + 4], 0.125, None, ALU.mult, sem="setup")

            def drain_token(g, outs, off, width=P):
                dve.wait_ge(S("w_used"), used_by(g))
                for j, out in enumerate(outs):
                    tt(out, ps[:, g % MM_BANKS, j * P:j * P + width], row[:, off:off + width], ALU.add,
                       "drained_v" if j == 1 else "dve_step")

            def even_in():
                drain_token(G_E, [small[:, 0, :], small[:, 1, :]], ROW["small"], 32)
                drain_token(G_E + 9, [vsw[:, 0, 0, :], vsw[:, 0, 1, :]], ROW["vs"])
                drain_token(G_E + 10, [vsw[:, 1, 0, :], vsw[:, 1, 1, :]], ROW["vw"])
                for j in range(8):
                    dve.wait_ge(S("drained_a"), drained("a", G_E + 11 + j))
                    c = lambda tap: V("conv_w", 4 * j + tap)
                    ts(qk[:, j, :], qkpre[:, j, 0:T], c(0), V("conv_b", j), ALU.mult, ALU.add)
                    for tap in range(1, 4):
                        stt(qk[:, j, :], qkpre[:, j, tap:tap + T], c(tap), qk[:, j, :], ALU.mult, ALU.add,
                            "conv" if tap == 3 else "dve_step")
                for j in range(4):
                    drain_token(G_E + 19 + j, [vtok[:, 0, j * P:(j + 1) * P], vtok[:, 1, j * P:(j + 1) * P]], ROW["v"] + j * P)

            def compress():
                dve.wait_ge(*once("dup_done"))
                for kind in range(2):
                    d = ps[:, 4 + kind, :].rearrange("p (g t) -> p g t", g=2)
                    step(nc.vector.tensor_copy(kc2[0:64, kind, :, :], d[0:64]))
                    step(nc.vector.tensor_copy(kc2[64:128, kind, :, 0:T - 1], d[64:128, :, 1:T]))
                for kind in range(2):
                    for g in range(2):
                        for a in range(2):
                            pos = vec[:, VEC[("kpos", "vpos")[kind]] + 8 * a:VEC[("kpos", "vpos")[kind]] + 8 * a + 8]
                            v = kc2[:, kind, g, :].rearrange("p (n j two) -> p j n two", n=16, two=2)[:, :, a:a + NCMP, 0]
                            tt(xc[:, kind, 8 * a:8 * a + 8, g * NCMP:(g + 1) * NCMP], v, end(pos, NCMP), ALU.add, "xc_ready")
                dve.wait_ge(S("w_used"), U_C + C_UNITS)
                h4 = ps[:, 6, 0:64].rearrange("p (k n) -> p k n", k=2)[:, :, 0:30]
                step(nc.vector.tensor_copy(hx[:, 0, :].rearrange("p (k n) -> p k n", k=2), h4), "hx_x")
                dve.wait_ge(*once("hx_sq"))
                ts(hx[:, 1, :], hx[:, 1, :], 0.044715, 1.0, ALU.mult, ALU.add)
                tt(hx[:, 1, :], hx[:, 1, :], hx[:, 0, :], ALU.mult, "hx_arg")
                dve.wait_ge(*once("hx_th"))
                ts(hx[:, 2, :], hx[:, 2, :], 0.5, 0.5, ALU.mult, ALU.add)
                tt(hx[:, 0, :], hx[:, 2, :], hx[:, 0, :], ALU.mult, "gelu_ready")
                dve.wait_ge(*once("kc_rs"))
                stt(kct[:, 2, :], kct[:, 0, :], V("kcn"), kct[:, 3, :], ALU.mult, ALU.mult, "kc_n")
                dve.wait_ge(*once("kc_rot"))
                tt(kct[:, 0, :], ps[:, 6, 288:288 + NCMP], C("sinc", NCMP), ALU.mult)
                tt(kct[:, 3, :], kct[:, 2, :], C("cosc", NCMP), ALU.mult)
                tt(kct[:, 3, :], kct[:, 3, :], kct[:, 0, :], ALU.add, "kc_ready")
                dve.wait_ge(*once("nqk_rs"))
                for j in range(6):
                    stt(nqk[:, j, :], nqk[:, j, :], V("nqk", j), rs[:, j, :], ALU.mult, ALU.mult, "nqk_n")
                dve.wait_ge(*once("nqk_rot"))
                r = rs[:].rearrange("p a b -> p (a b)").rearrange("p (a b) -> p a b", b=512)
                for j in range(3):
                    tt(rs[:, 2 * j:2 * j + 2, :], ps[:, j, :].rearrange("p (a b) -> p a b", a=2), mid(C("sin", T), 2), ALU.mult, "rope_done")
                tt(nqk[:], nqk[:], mid(C("cos", T), 6), ALU.mult)
                tt(nqk[:], nqk[:], rs[:], ALU.add, "rope_done")

            def mlstm():
                for j in range(2):
                    tt(gl[:, 0, 4 * j:4 * j + 4], small[:, j, 4:8], row[:, ROW["fbias"]:ROW["fbias"] + 4], ALU.add, "fgate")
                dve.wait_ge(*once("log1p"))
                stt(gl[:, 3, :], gl[:, 0, :], 0.0, gl[:, 2, :], ALU.min, ALU.subtract, "logf")
                dve.wait_ge(*once("bcum"))
                step(nc.vector.tensor_copy(gl[:, 4, :], ps[:, 4, 0:8]), "gate_cols")
                tt(gl[:, 5, :].rearrange("p (a b) -> p a b", a=2), small[:, :, 0:4], gl[:, 4, :].rearrange("p (a b) -> p a b", a=2),
                   ALU.subtract, "gate_cols")
                dve.wait_ge(*once("gate_rows"))
                step(nc.vector.tensor_copy(rows4[:, 0:2, :].rearrange("p a b -> p (a b)"), ps[0:4, 4, :]), "row_max")
                step(nc.vector.tensor_tensor_scan(rows4[:, 2, :], rows4[:, 1, :], rows4[:, 1, :], 0.0, ALU.max, ALU.max), "row_max")
                tt(rows4[:, 3, :], rows4[:, 2, :], rows4[:, 0, :], ALU.add, "row_max")
                dve.wait_ge(*once("qk_th"))
                for j in range(2):
                    stt(qk[:, 4 * j:4 * j + 4, :], th[:, 4 * j:4 * j + 4, :], 1.0, qk[:, 4 * j:4 * j + 4, :], ALU.add, ALU.mult, "qk_ready")
                for h in range(5):
                    if h < 4:
                        dve.wait_ge(S("mlstm_e"), h + 1)
                        stt(mST[:, h % 2, :], ps[:, 4 * (h % 2) + 2, 0:384], 0.25 * P ** -0.5, mE[:, h % 2, :], ALU.mult, ALU.mult, "mlstm_st")
                    if h >= 1:
                        j = (h - 1) % 2
                        dve.wait_ge(S("mlstm_d"), h)
                        tt(mad[:, j, :], mad[:, j, :], mem[:, j, :], ALU.max)
                        step(nc.vector.reciprocal(mad[:, j, :], mad[:, j, :]))
                        tt(hm[:, h - 1, :], ps[:, 4 * j + 3, 0:T], mad[:, j, :], ALU.mult, "mlstm_h")
                dve.wait_ge(*once("mh_rs"))
                tt(hm[:], hm[:], rs[:, 0:4, :], ALU.mult)
                dve.wait_ge(*once("oz_th"))
                stt(hm[:], th[:, 0:4, :], 1.0, hm[:], ALU.add, ALU.mult)
                stt(oz[:, 4:8, :], th[:, 4:8, :], 1.0, oz[:, 4:8, :], ALU.add, ALU.mult)
                tt(hm[:], hm[:], oz[:, 4:8, :], ALU.mult)
                for h in range(4):
                    ts(mixT[:, h, TM:TT], hm[:, h, :], V("mnorm", h), 0.25, ALU.mult, ALU.mult, "m_out")

            def attention():
                dve.wait_ge(*once("cmp_s"))
                for qt in range(2):
                    for g in range(2):
                        s = ps[:, 6 + g, qt * 4 * NCMP:(qt + 1) * 4 * NCMP].rearrange("p (i n) -> p i n", i=4)
                        tt(pc[:, qt * 8 + 4 * g:qt * 8 + 4 * g + 4, :], s, mid(C("cneg", 2 * NCMP)[:, qt * NCMP:(qt + 1) * NCMP], 4), ALU.add)
                step(nc.vector.tensor_reduce(cs[:, 0, :], pc[:], AX.X, ALU.max))
                tt(pc[:], pc[:], end(cs[:, 0, :], NCMP), ALU.subtract, "cmp_sub")
                dve.wait_ge(*once("cmp_e"))
                step(nc.vector.tensor_reduce(cs[:, 1, :], pc[:], AX.X, ALU.add))
                for qt in range(2):
                    tt(pc[:, qt * 8:qt * 8 + 8, :], pc[:, qt * 8:qt * 8 + 8, :],
                       mid(C("cok", 2 * NCMP)[:, qt * NCMP:(qt + 1) * NCMP], 8), ALU.mult)
                step(nc.vector.reciprocal(cs[:, 1, :], cs[:, 1, :]))
                dve.wait_ge(*once("gates_th"))
                gates = small[:, :, 8:32]
                ts(gates, gates, 0.5, 0.5, ALU.mult, ALU.add)
                g3 = small[:, :, 8:32].rearrange("p t (h b) -> p t h b", b=3)
                tt(cs[:, 2, :].rearrange("p (t h) -> p t h", t=2), cs[:, 1, :].rearrange("p (t h) -> p t h", t=2), g3[:, :, :, 0], ALU.mult)
                tt(pc[:], pc[:], end(cs[:, 2, :], NCMP), ALU.mult, "cmp_p")
                dve.wait_ge(*once("nz_th"))
                stt(nz[:], th[:, 0:4, :], 1.0, nz[:], ALU.add, ALU.mult)
                for n in range(5):
                    if n < 4:
                        qt, g = n // 2, n % 2
                        nk = P * (qt + 1)
                        for i in range(4):
                            dve.wait_ge(S("att_s"), 4 * n + i + 1)
                            s = ps[:, i, :].rearrange("p (k n) -> p k n", k=2)[:, :, 0:nk]
                            step(nc.vector.tensor_reduce(pst[:, n % 2, i, 0:2], s, AX.X, ALU.max, negate=True), "att_max")
                        for i in range(4):
                            dve.wait_ge(S("att_exp"), 8 * n + 2 * i + 2)
                            r = pst[:, n % 2, i, 2:4]
                            step(nc.vector.reciprocal(r, r))
                            tt(r, r, g3[:, qt, 4 * g + i, 1:3], ALU.mult)
                            for kind in range(2):
                                p = prob[:, n % 2, i, kind * T:kind * T + nk]
                                ts(p, p, pst[:, n % 2, i, 2 + kind:3 + kind], None, ALU.mult, sem="att_p")
                    if n >= 1:
                        qt, g = (n - 1) // 2, (n - 1) % 2
                        dve.wait_ge(S("att_av"), n)
                        rows = slice(64 * g, 64 * g + 64)
                        stt(mixT[rows, 4:8, TM + qt * P:TM + (qt + 1) * P],
                            ps[rows, 6 + (n - 1) % 2, :].rearrange("p (i q) -> p i q", i=4), 0.5,
                            nz[rows, :, qt * P:(qt + 1) * P], ALU.mult, ALU.mult, "att_o")

            def residual(g0, c0, scale=1.0):
                for m in range(KT):
                    dve.wait_ge(S("w_used"), used_by(g0 + m))
                    stt(xT[:, m, c0:TT], ps[:, (g0 + m) % MM_BANKS, 0:TT - c0], scale, xT[:, m, c0:TT], ALU.mult, ALU.add, "drained_v")

            def hgrn_in():
                lb = lambda j: lbs[:, j, :]
                l0, l1 = vec[:, VEC["lb0"]:VEC["lb0"] + 8], vec[:, VEC["lb1"]:VEC["lb1"] + 8]
                tt(lb(0), l0, l1, ALU.subtract, "lb_arg")
                dve.wait_ge(*once("lb_th"))
                ts(lb(1), lb(0), -0.25, 0.25, ALU.mult, ALU.add)
                ts(lb(2), lb(1), -1.0, 1.0, ALU.mult, ALU.add)
                ts(lb(3), lb(1), 0.5, None, ALU.mult)
                ts(lb(4), lb(1), -0.5, None, ALU.mult)
                step(nc.vector.memset(dif[:, 0, :], 1.0))
                step(nc.vector.memset(dif[:, 0, :].rearrange("p (n w) -> p n w", w=P)[:, :, 0:1], 0.0))
                dve.wait_ge(*once("f_th"))
                t8 = dif[:, 1, :].rearrange("p (a b) -> p a b", a=8)
                for h in range(8):
                    ts(fF[:, h, :], t8[:, h, :], lbs[:, 1, h:h + 1], lbs[:, 2, h:h + 1], ALU.mult, ALU.add, "f_ready")
                for h in range(8):
                    ts(fK[:, h, :], t8[:, h, :], lbs[:, 4, h:h + 1], lbs[:, 3, h:h + 1], ALU.mult, ALU.add,
                       "f_read" if h == 7 else "dve_step")
                dve.wait_ge(*once("f_log"))
                step(nc.vector.tensor_tensor_scan(fC[:].rearrange("p a b -> p (a b)"), dif[:, 0, :], fF[:].rearrange("p a b -> p (a b)"),
                                                  0.0, ALU.mult, ALU.add))
                dve.wait_ge(*once("q_th"))
                stt(fQ[:], t8, 1.0, fQ[:], ALU.add, ALU.mult, "q_ready")
                for j in range(8):
                    drain_token(G_H + 16 + j, [ivt[:, 0, j * P:(j + 1) * P], ivt[:, 1, j * P:(j + 1) * P]], ROW["iv"] + j * P)

            def hgrn():
                blocks = lambda ap: ap.rearrange("p (h t w) -> p h t w", h=2, t=2)

                def banks_of(lev):
                    for j in range(4):
                        dve.wait_ge(S("lev_s"), 4 * lev + j + 1)
                        out = hA[:, 2 * j:2 * j + 2, 0:3:2, :]
                        src = blocks(ps[:, 4 * (lev % 2) + j, :])
                        if lev == 0:
                            m = C("ident")
                        else:
                            m = C("hlev", 7 * P)[:, (lev - 1) * P:lev * P]
                        m = m.unsqueeze(1).unsqueeze(1).broadcast_to([P, 2, 2, P])
                        if lev == 0:
                            for t in range(2):
                                tt(out[:, :, t, :], src[:, :, t, :], m[:, :, t, :], ALU.mult, "lev_a" if t else "dve_step")
                        else:
                            step(nc.vector.copy_predicated(out, m.bitcast(U32), src), "lev_a")

                def scaled(lev):
                    b = (LEVELS + (P,))[lev - 1]
                    cv = fC[:].rearrange("p a b -> p (a b)").rearrange("p (n w) -> p n w", w=2 * b)
                    d = dif[:, (lev - 1) % 2, :].rearrange("p (n w) -> p n w", w=2 * b)
                    n = 8 * T // (2 * b)
                    if lev < 8:
                        tt(d, cv, cv[:, :, b - 1:b].broadcast_to([P, n, 2 * b]), ALU.subtract, "lev_d")
                    else:
                        tt(d[:, :, 0:b], cv[:, :, 0:b], cv[:, :, b - 1:b].broadcast_to([P, n, b]), ALU.subtract)
                        step(nc.vector.tensor_copy(d[:, :, b:], cv[:, :, b:]), "lev_d")

                def products(lev):
                    b = (LEVELS + (P,))[lev - 1]
                    view = lambda ap: ap.rearrange("p (n w) -> p n w", w=2 * b)
                    d, o = view(dif[:, (lev - 1) % 2, :]), view(qkl[:, lev % 2, :])
                    flat = lambda t: view(t[:].rearrange("p a b -> p (a b)"))
                    dve.wait_ge(S("lev_e"), 2 * lev)
                    if lev >= 3:
                        dve.wait_ge(S("lev_s"), 4 * (lev - 1))
                    tt(o[:, :, 0:b], d[:, :, 0:b], flat(fK)[:, :, 0:b], ALU.mult, "lev_qk")
                    tt(o[:, :, b:], d[:, :, b:], flat(fQ)[:, :, b:], ALU.mult, "lev_qk")

                for j in range(2):
                    step(nc.vector.memset(lbs[:, 5, j:j + 1], 0.0), "lev_qk")
                scaled(1)
                for lev in range(1, 9):
                    if lev < 8:
                        scaled(lev + 1)
                    products(lev)
                    banks_of(lev - 1)
                for j in range(2):
                    dve.wait_ge(S("lev_s"), 4 * 8 + j + 1)
                    step(nc.vector.tensor_copy(hA[:, 4 * j:4 * j + 4, 1, :], ps[:, j, :].rearrange("p (h w) -> p h w", h=4)), "lev_a")
                dve.wait_ge(*once("z_th"))
                stt(fZ[:], fF[:], 1.0, fZ[:], ALU.add, ALU.mult)
                dve.wait_ge(*once("hg_rs"))
                flat = lambda t: t[:].rearrange("p a b -> p (a b)")
                tt(dif[:, 1, :], dif[:, 1, :], ps[:, 4:8, :].rearrange("p a b -> p (a b)"), ALU.mult)
                tt(dif[:, 1, :], dif[:, 1, :], flat(fZ), ALU.mult)
                for h in range(8):
                    ts(mixT[:, h, TM:TT], dif[:, 1, h * T:(h + 1) * T], V("hnorm", h), 0.5, ALU.mult, ALU.mult, "hg_out")

            def ffn(u0, g0, first):
                d0 = drained("v", g0 - 1)

                def pair(it, f4, f):
                    dve.wait_ge(S("ffn_th"), it * 4 + (first + f4 + 1))
                    dve.wait_ge(S("drained_v"), it * 8 + (d0 + 2 * f4))
                    nc.vector.scalar_tensor_tensor(out=fhalf[:], in0=fth[:, f4, :], scalar=1.0,
                                                   in1=ps[:, (g0 + 2 * f4) % MM_BANKS, 0:TT], op0=ALU.add,
                                                   op1=ALU.mult).then_inc(S("drained_v"), 1)
                    dve.wait_ge(S("drained_v"), it * 8 + (d0 + 2 * f4 + 1))
                    dve.wait_ge(S("w_used"), it * 8 + (u0 + 2 * f4 + 2))
                    nc.vector.tensor_tensor(fact[:, f, :], fhalf[:], ps[:, (g0 + 2 * f4 + 1) % MM_BANKS, 0:TT],
                                            ALU.mult).then_inc(S("drained_v"), 1)

                with dve.Fori(0, FT // 4) as it:
                    for f4 in range(4):
                        pair(it, f4, it * 4 + f4)
                for f4 in range(FT % 4):
                    pair(FT // 4, f4, FT - FT % 4 + f4)
                dve.wait_ge(S("drained_v"), d0 + GU_UNITS)
                dve_n["drained_v"] += GU_UNITS
                residual(g0 + GU_UNITS, 0, 0.25)

            def mixer_in():
                step(nc.vector.memset(pr[:, :, 0:1], 0.0))
                step(nc.vector.memset(sbk[:, :, TT:], 0.0), "sb_pad")
                step(nc.vector.memset(sbv[:, :, TT:], 0.0), "sb_pad")
                for j in range(14):
                    dve.wait_ge(S("drained_a"), drained("a", G_P + 12 + j))
                    tmp = pT[:, j % 4, :]
                    tt(tmp, pr[:, j, 0:TT], pr[:, j, 1:1 + TT], ALU.subtract)
                    stt(pr[:, j, 1:1 + TT], tmp, V("mu", j), pr[:, j, 1:1 + TT], ALU.mult, ALU.add, "shifted")
                k = pr[:, 4:8, 1:1 + TT]
                for j in range(4):
                    ts(pK[:, j, :], k[:, j, :], V("k_k", j), None, ALU.mult, sem="kk_raw")
                dve.wait_ge(*once("decay_th"))
                ts(pD[:], pD[:], -0.5 * DECAY, -0.5 * DECAY, ALU.mult, ALU.add)
                dve.wait_ge(*once("a_th"))
                ts(pA[:], pA[:], 0.5, 0.5, ALU.mult, ALU.add)
                dve.wait_ge(*once("kk_ss"))
                ts(pT[:], ps[:, 0:4, 0:TT], 1e-24, None, ALU.max, sem="kk_n2")
                dve.wait_ge(*once("kk_rs"))
                tt(pK[:], pK[:], pT[:], ALU.mult)
                for j in range(4):
                    ts(pT[:, j, :], pA[:, j, :], 1.0, V("k_a", j), ALU.subtract, ALU.mult)
                stt(k, pT[:], 1.0, k, ALU.add, ALU.mult)
                tt(pA[:], pA[:], pK[:], ALU.mult)
                step(nc.vector.memset(pT[:], 1.0))
                step(nc.vector.memset(pT[:, :, 0:TT:RW_CHUNK], 0.0))
                flat = lambda t: t[:].rearrange("p a b -> p (a b)")
                step(nc.vector.tensor_tensor_scan(flat(pC), flat(pT), flat(pD), 0.0, ALU.mult, ALU.add), "cum")
                tt(pD[:], pC[:], pD[:], ALU.subtract, "cum_x")
                dve.wait_ge(*once("e_c"))
                step(nc.vector.tensor_copy(eL[:, :, 0:4], pT[:, :, RW_CHUNK - 1:4 * RW_CHUNK:RW_CHUNK]))
                tt(AR[:, :, 1, :], pr[:, 0:4, 1:1 + TT], pT[:], ALU.mult)
                dve.wait_ge(*once("e_cx"))
                tt(AR[:, :, 0, :], pK[:], pD[:], ALU.mult)
                dve.wait_ge(*once("e_nc"))
                tt(BK[:, :, 0, :], pA[:], pC[:], ALU.mult, "bk_ready")
                tt(BK[:, :, 1, :], k, pC[:], ALU.mult, "bk_ready")

            def sticks():
                for h in range(9):
                    if h < 8:
                        p = h % 2
                        dve.wait_ge(S("sb_ln"), h + 1)
                        stt(zl[:, p, :], zs[:, p, :], 0.0, zl[:, p, :], ALU.max, ALU.add)
                        tt(zp[:, p, :], zl[:, p, :], C("sbok", 432), ALU.mult, "sb_sp")
                    if h >= 1:
                        r = h - 1
                        dve.wait_ge(S("sb_rest"), r + 1)
                        tt(zs[:, r % 2, :], zs[:, r % 2, :], ps[:, 4 + r % 2, 0:432], ALU.subtract, "sb_arg")

            def rwkv():
                dve.wait_ge(S("sb_out"), 8)
                nth = [0]
                for tau, (t0, n) in enumerate(TILES2):
                    q8 = lambda ap: mid(ap, 8)
                    part = lambda t: t[0:n, :, 0:n]
                    rl = lambda j: C("rlev", 6 * P)[0:n, j * P:j * P + n]
                    dve.wait_ge(S("r_ab"), tau + 1)
                    for q in range(2):
                        step(nc.vector.tensor_copy(rN0[0:n, 4 * q:4 * q + 4, 0:n], ps[0:n, 6 + q, 0:4 * n].rearrange("p (q t) -> p q t", q=4)))
                    mask = C("rwmask", 512)[0:n].rearrange("p (k t) -> p k t", k=4)[:, :, 0:n]
                    for h in range(8):
                        dve.wait_ge(S("r_mats"), 8 * tau + h + 1)
                        q = (h % 2) * 4 + h // 2
                        tt(rA[0:n, q, 0:4 * n].rearrange("p (k t) -> p k t", k=4),
                           ps[0:n, h % 6, 0:4 * n].rearrange("p (k t) -> p k t", k=4), mask, ALU.mult, "r_mask")
                    tt(part(rG), rA[0:n, :, 0:n], q8(C("rlevt")[0:n, 0:n]), ALU.mult)
                    tt(part(rG), q8(C("ident")[0:n, 0:n]), part(rG), ALU.subtract)
                    tt(part(rI), part(rN0), q8(rl(0)), ALU.mult)
                    tt(part(rI), q8(C("ident")[0:n, 0:n]), part(rI), ALU.subtract)
                    levels = [j for j in range(1, 6) if LEVELS[j] < n]
                    for j in levels:
                        nth[0] += 1
                        tt(part(rN), part(rN0), q8(rl(j)), ALU.mult, "r_n")
                        dve.wait_ge(S("r_d"), nth[0])
                        for dst, b in ((rG, 2), (rI, 4)):
                            for q in range(2):
                                d = dst[0:n, 4 * q:4 * q + 4, 0:n]
                                tt(d, d, ps[0:n, b + q, 0:4 * n].rearrange("p (q t) -> p q t", q=4), ALU.subtract,
                                   "r_g" if j == levels[-1] and b == 4 and q else "dve_step")
                    dve.wait_ge(S("r_y0"), tau + 1)
                    tt(rR[:, :, 0:n], ps[:, 2, 0:4 * n].rearrange("p (q t) -> p q t", q=4), AR[:, :, 1, t0:t0 + n], ALU.add, "r_r")
                    dve.wait_ge(S("r_y0c"), tau + 1)
                    if tau < 2:
                        for c in (2 * tau, 2 * tau + 1):
                            dve.wait_ge(S("r_phi"), c + 1)
                            v = ps[:, 4 + c % 2, :].rearrange("p (w q i) -> p w q i", w=2, q=4)
                            tt(psi[:, c % 2], v[:, 1], end(eL[:, :, c], 64), ALU.mult)
                            tt(phi[:, c % 2], v[:, 0], mid(C("istack", 64), 4), ALU.add, "r_phic")
                    for c in [c for c, (s, _) in enumerate(RW_CHUNKS) if t0 <= s < t0 + n]:
                        start, width = RW_CHUNKS[c]
                        if c >= 1:
                            dve.wait_ge(S("r_ys"), c)
                            for a in range(2):
                                rows = slice(64 * a, 64 * a + 64)
                                o = ps[rows, 6 + a, 0:4 * n].rearrange("p (q t) -> p q t", q=4)[:, :, start - t0:start - t0 + width]
                                tt(yT[rows, :, start:start + width], yT[rows, :, start:start + width], o, ALU.add)
                        if c == 0:
                            step(nc.vector.tensor_copy(state[:, 1], psi[:, 0]), "r_state")
                        elif c < 4:
                            dve.wait_ge(S("r_s"), c)
                            for a in range(2):
                                rows = slice(64 * a, 64 * a + 64)
                                s = state[rows, (c + 1) % 2]
                                tt(s, ps[rows, a, 0:256].rearrange("p (q i) -> p q i", q=4), end(eL[rows, :, c], 64), ALU.mult)
                            tt(state[:, (c + 1) % 2], state[:, (c + 1) % 2], psi[:, c % 2], ALU.add, "r_state")
                    step(nc.vector.memset(rstd[:, 0:1], 0.0), "y_done")
                for j in range(4):
                    if j == 0:
                        dve.wait_ge(*once("gn_mean"))
                    stt(yT[:, j, :], ps[:, j, 0:TT], -1.0 / 64, yT[:, j, :], ALU.mult, ALU.add, "gn_d")
                for j in range(4):
                    ts(pK[:, j, :], pr[:, j, 1:1 + TT], V("r_k", j), None, ALU.mult)
                tt(pK[:], pK[:], pr[:, 4:8, 1:1 + TT], ALU.mult, "bonus_in")
                dve.wait_ge(*once("g_th"))
                ts(pr[:, 13, 1:1 + TT], pr[:, 13, 1:1 + TT], 0.5, 0.5, ALU.mult, ALU.add, "g_in")
                dve.wait_ge(*once("gn_rs"))
                tt(yT[:], yT[:], pT[:], ALU.mult)
                for j in range(4):
                    ts(yT[:, j, :], yT[:, j, :], V("lnx_w", j), V("lnx_b", j), ALU.mult, ALU.add)
                dve.wait_ge(*once("bonus"))
                tt(pT[:], ps[:, 0:4, 0:TT], pr[:, 8:12, 1:1 + TT], ALU.mult)
                tt(yT[:], yT[:], pT[:], ALU.add)
                dve.wait_ge(*once("g_out"))
                for j in range(4):
                    tt(mixT[:, 4 + j, :], yT[:, j, :], ps[:, 4 + j, 0:TT], ALU.mult, "rw_out")

            setup()
            norm("norm0", TM, T, "norm0")
            even_in()
            compress()
            mlstm()
            attention()
            residual(G_EO, TM)
            norm("norm1", TM, T, "norm1")
            hgrn_in()
            hgrn()
            residual(G_HO, TM)
            norm("ffn1", 0, TT, "ffn1")
            ffn(U_F1, G_F1, 0)
            norm("mix", 0, TT, "mix")
            mixer_in()
            sticks()
            rwkv()
            residual(G_PO, 0)
            norm("ffn2", 0, TT, "ffn2")
            ffn(U_F2, G_F2, FT)
            norm("final", 0, TT, "final")


_ORDER = ("stream", "vec", "row", "mat", "cst", "x")


def kernel(**inputs):
    import concourse.bacc as bacc
    from concourse.bass_utils import run_bass_kernel_spmd

    packed = pack(inputs)
    nc = bacc.Bacc("TRN2", target_bir_lowering=False, num_devices=1)
    arrays = {"in_" + n: packed[n] for n in _ORDER}
    args = [nc.dram_tensor("in_" + n, packed[n].shape, F32, kind="ExternalInput").ap() for n in _ORDER]
    out = nc.dram_tensor("out", (P, KT, T), F32, kind="ExternalOutput").ap()
    program(nc, *args, out)
    r = run_bass_kernel_spmd(nc, [arrays], core_ids=[0])
    got = np.asarray(r.results[0]["out"])
    return np.ascontiguousarray(got.transpose(2, 1, 0).reshape(1, T, D))
```

```python
from contextlib import ExitStack

import numpy as np
import concourse.bass as bass
from concourse import mybir

F32 = mybir.dt.float32
F32R = mybir.dt.float32r
BF16 = mybir.dt.bfloat16
U32 = mybir.dt.uint32
ALU = mybir.AluOpType
ACT = mybir.ActivationFunctionType
AX = mybir.AxisListType

P = 128
D = 1024
KT = D // P
T = 256
TM = 16
TT = T + TM
EPS = 1e-6
LNX_EPS = 64e-5
BIG = 1e30
NCMP = 15
FF = 2816
FT = FF // P
SLOTS = 4
LEVELS = (1, 2, 4, 8, 16, 32, 64)
RW_CHUNK = 64
RW_CHUNKS = [(c, min(RW_CHUNK, TT - c)) for c in range(0, TT, RW_CHUNK)]
TILES2 = [(0, 128), (128, 128), (256, 16)]
DECAY = float(np.exp(-0.5))

E_UNITS = 35
C_UNITS = 4
H_UNITS = 32
GU_UNITS = 2 * FT
DN_UNITS = FT
P_UNITS = 26
U_E = 0
C_AFTER = 22
U_C = U_E + C_AFTER
U_EO = U_E + E_UNITS + C_UNITS
U_H = U_EO + KT
U_HO = U_H + H_UNITS
U_F1 = U_HO + KT
U_P = U_F1 + GU_UNITS + DN_UNITS
U_PO = U_P + P_UNITS
U_F2 = U_PO + KT
N_UNITS = U_F2 + GU_UNITS + DN_UNITS

E_KC, E_NQK, E_VSW, E_QK, E_V, E_SMALL, E_OZ, E_NZ = 0, 2, 8, 10, 18, 22, 23, 31
E_OWNER = "a" * 8 + "vv" + "a" * 8 + "vvvv" + "v" + "a" * 12
H_F, H_Q, H_Z0, H_IV, H_Z1 = 0, 8, 16, 17, 25
H_OWNER = "a" * 17 + "v" * 8 + "a" * 7
G_E = 0
G_EO = G_E + E_UNITS
G_H = G_EO + KT
G_HO = G_H + H_UNITS
G_F1 = G_HO + KT
G_P = G_F1 + GU_UNITS + KT
G_PO = G_P + P_UNITS
G_F2 = G_PO + KT
OWNER = (E_OWNER + "v" * KT + H_OWNER + "v" * KT + "v" * (GU_UNITS + KT) + "a" * P_UNITS
         + "v" * KT + "v" * (GU_UNITS + KT))
MM_BANKS = 4


def drained(owner, g):
    return OWNER[:g + 1].count(owner)


def even_unit(j):
    return U_E + j + (C_UNITS if j >= C_AFTER else 0)


def _offsets(parts):
    at, out = 0, {}
    for name, n in parts:
        out[name] = at
        at += n
    return out, at


VEC, NVEC = _offsets([
    ("norm0", 8), ("norm1", 8), ("ffn1", 8), ("mix", 8), ("ffn2", 8), ("final", 8),
    ("ev_b", 35), ("conv_w", 32), ("conv_b", 8), ("mnorm", 4), ("nqk", 6), ("kcn", 1),
    ("fp_b", 8), ("qp_b", 8), ("z_b", 8), ("lb0", 8), ("lb1", 8), ("hnorm", 8),
    ("mu", 14), ("w0", 4), ("a0", 4), ("k_k", 4), ("k_a", 4), ("r_k", 4), ("lnx_w", 4), ("lnx_b", 4),
    ("kpos", 16), ("vpos", 16)])
ROW, NROW = _offsets([("small", 32), ("fbias", 4), ("vs", 128), ("vw", 128), ("v", 512), ("iv", 1024)])
MAT, NMAT = _offsets([("w2k", 64), ("w2v", 64), ("wup", 512), ("gup", 512)])
CST, NCST = _offsets([
    ("ident", 128), ("ones", 128), ("blk", 128), ("ge", 128),
    ("sbok", 432), ("rwmask", 512), ("rlev", 6 * 128), ("rlevt", 128), ("istack", 64),
    ("le", 128), ("gt", 128), ("cos", 256), ("sin", 256), ("rot", 128), ("dup0", 128), ("dup1", 128),
    ("pick", 512), ("cosc", NCMP), ("sinc", NCMP), ("cneg", 2 * NCMP), ("cok", 2 * NCMP), ("hlev", 7 * 128)])
CST1 = CST["le"]


def constants():
    c = np.zeros((P, NCST), np.float32)

    def put(name, a):
        c[:a.shape[0], CST[name]:CST[name] + a.shape[1]] = a

    i = np.arange(P)
    row, col = i[:, None], i[None, :]
    put("ident", np.eye(P))
    put("ones", np.ones((P, P)))
    put("blk", (row // 64 == col // 64) * 1.0)
    put("ge", (row >= col) * 1.0)
    put("le", (row <= col) * 1.0)
    put("gt", (row > col) * 1.0)

    def rope(pos):
        half = 8
        inv = (500000.0 ** (-np.arange(half, dtype=np.float32) / np.float32(half))).astype(np.float32)
        ang = pos.astype(np.float32)[None, :] * inv[:, None]
        cos, sin = np.ones((P, len(pos))), np.zeros((P, len(pos)))
        for g in range(2):
            for s in range(2):
                cos[64 * g + 8 * s:64 * g + 8 * s + 8] = np.cos(ang)
                sin[64 * g + 8 * s:64 * g + 8 * s + 8] = np.sin(ang)
        return cos, sin

    cos, sin = rope(np.arange(T))
    put("cos", cos)
    put("sin", sin)
    cos, sin = rope(np.arange(NCMP) * 16 + 31)
    put("cosc", cos)
    put("sinc", sin)
    rot = np.zeros((P, P))
    for g in range(2):
        for k in range(8):
            rot[64 * g + 8 + k, 64 * g + k] = -1.0
            rot[64 * g + k, 64 * g + 8 + k] = 1.0
    put("rot", rot)
    for g in range(2):
        dup = np.zeros((P, P))
        for d in range(64):
            dup[64 * g + d, d] = dup[64 * g + d, 64 + d] = 1.0
        put(f"dup{g}", dup)
    pick = np.zeros((4, 4, P))
    for h in range(4):
        pick[h, h] = 1.0
    put("pick", pick.reshape(4, 512))
    ok = (np.arange(NCMP)[None, None, :] * 16 + 31 <= (np.arange(2)[None, :, None] * P + i[:, None, None]))
    put("cok", ok.reshape(P, -1) * 1.0)
    put("cneg", np.where(ok, 0.0, -BIG).reshape(P, -1))
    lev = [((row // (2 * b) == col // (2 * b)) & (row % (2 * b) < b) & (col % (2 * b) >= b)) for b in LEVELS]
    put("hlev", np.concatenate(lev, 1) * 1.0)
    put("rlev", np.concatenate([m.T for m in lev[:6]], 1) * 1.0)
    put("rlevt", lev[0] * 1.0)
    strict, incl = (row < col), (row <= col)
    put("sbok", np.concatenate([strict, np.ones((P, 144)), strict, np.ones((P, 16)), strict[:, :16]], 1) * 1.0)
    same = row // RW_CHUNK == col // RW_CHUNK
    put("rwmask", np.concatenate([strict & same, incl & same] * 2, 1) * 1.0)
    put("istack", (row % 64 == np.arange(64)[None, :]) * 1.0)
    return c


def pack(i):
    f = {k: np.asarray(v) for k, v in i.items()}
    ev_w, ev_b = f["ev_w_in"][0], f["ev_b_in"][0]
    nsa = 2568
    r = np.arange
    pair = [np.concatenate([r(64) + 64 * j, r(64) + 64 * (4 + j)]) for j in range(4)]
    ev_cols = [nsa + 512 + r(128), nsa + 640 + r(128)]
    ev_cols += [nsa + pair[j] for j in range(4)]
    ev_cols += [nsa + 768 + r(128), nsa + 1024 + r(128), nsa + 896 + r(128), nsa + 1152 + r(128)]
    ev_cols += [r(128) + 128 * j for j in range(12)]
    ev_cols += [np.concatenate([r(2560, 2568), nsa + 1280 + r(24)])]
    ev_cols += [r(128) + 128 * j for j in range(12, 20)]
    ev_cols += [nsa + 1304 + pair[j] for j in range(4)]
    assert len(ev_cols) == E_UNITS
    stream = np.zeros((N_UNITS, P, KT * P), np.float32)
    at = [0]

    def unit(w):
        k, n = w.shape[0] // P, w.shape[1]
        stream[at[0]].reshape(P, KT, P)[:, :k, :n] = w.reshape(k, P, n).transpose(1, 0, 2)
        at[0] += 1

    def units(w):
        for m in range(w.shape[1] // P):
            unit(w[:, m * P:(m + 1) * P])

    def ffn(gate, up, down):
        for m in range(FT):
            unit(gate[:, m * P:(m + 1) * P])
            unit(up[:, m * P:(m + 1) * P])
        blocks = down.reshape(FT, P, KT, P).transpose(2, 0, 1, 3).reshape(FT, KT, P, P)
        for u in range(FT):
            stream[at[0]].reshape(P, KT, P)[:] = blocks[u].transpose(1, 0, 2)
            at[0] += 1

    for c in ev_cols[:C_AFTER]:
        unit(ev_w[:, c])
    for w1 in (f["cmp_k_w1"][0], f["cmp_v_w1"][0]):
        unit(w1[:1024])
        unit(w1[1024:])
    for c in ev_cols[C_AFTER:]:
        unit(ev_w[:, c])
    rows = np.concatenate([r(512)] + [512 + pair[j] for j in range(4)])
    units(f["ev_w_out"][0][rows])
    od = f["od_w_in"][0]
    for lo, hi in ((0, D), (2 * D, 3 * D), (3 * D, 3 * D + P), (D, 2 * D), (3 * D + P, 4 * D)):
        units(od[:, lo:hi])
    units(f["od_w_out"][0])
    ffn(f["ffn1_w_gate_2"][0], f["ffn1_w_up_2"][0], f["ffn1_w_down_2"][0])
    w_in = f["w_in_2"][0]
    units(w_in[:, :3072])
    unit(w_in[:, 3072:3136])
    unit(w_in[:, 3136:3232])
    units(f["w_out_2"][0])
    ffn(f["ffn2_w_gate_2"][0], f["ffn2_w_up_2"][0], f["ffn2_w_down_2"][0])
    assert at[0] == N_UNITS

    vec = np.zeros((P, NVEC), np.float32)

    def col(name, v):
        v = v.reshape(-1, P).T
        vec[:, VEC[name]:VEC[name] + v.shape[1]] = v

    col("norm0", f["norm_w"][0])
    col("norm1", f["norm_w"][1])
    for name, key in (("ffn1", "ffn1_norm_2"), ("mix", "mix_norm_2"), ("ffn2", "ffn2_norm_2"), ("final", "final_norm_2"),
                      ("conv_b", "mlstm_conv_b"), ("mnorm", "mlstm_head_norm"), ("hnorm", "hgrn_head_norm"),
                      ("w0", "rwkv_w0_2"), ("a0", "rwkv_a0_2"), ("k_k", "rwkv_k_k_2"), ("k_a", "rwkv_k_a_2"),
                      ("r_k", "rwkv_r_k_2"), ("lnx_w", "rwkv_lnx_w_2"), ("lnx_b", "rwkv_lnx_b_2")):
        col(name, f[key])
    for m, c in enumerate(ev_cols):
        if len(c) == P:
            vec[:, VEC["ev_b"] + m] = ev_b[c]
    vec[:, VEC["conv_w"]:VEC["conv_w"] + 32] = f["mlstm_conv_w"][0].reshape(4, 8, P).transpose(2, 1, 0).reshape(P, 32)
    qn, kn = f["nsa_q_norm"][0], f["nsa_k_norm"][0]
    for m, v in enumerate([qn] * 4 + [kn[1], kn[2]]):
        vec[:64, VEC["nqk"] + m] = vec[64:, VEC["nqk"] + m] = v
    vec[:64, VEC["kcn"]] = vec[64:, VEC["kcn"]] = kn[0]
    ob = f["od_b_in"][0]
    col("fp_b", ob[:D])
    col("qp_b", ob[2 * D:3 * D])
    col("z_b", ob[3 * D:])
    col("lb0", f["hgrn_lb_logits"][0])
    col("lb1", f["hgrn_lb_logits"][1])
    mu = f["rwkv_mu_2"][0]
    col("mu", mu[:1536])
    vec[:64, VEC["mu"] + 12] = mu[1536:1600]
    vec[:96, VEC["mu"] + 13] = mu[1600:]
    col("kpos", f["cmp_k_pos"][0].reshape(16, P))
    col("vpos", f["cmp_v_pos"][0].reshape(16, P))

    row = np.zeros((1, NROW), np.float32)
    for name, v in (("small", ev_b[ev_cols[E_SMALL]]), ("fbias", f["mlstm_f_bias"][0]), ("vs", ev_b[ev_cols[E_VSW]]),
                    ("vw", ev_b[ev_cols[E_VSW + 1]]), ("v", ev_b[1024:1536]), ("iv", ob[D:2 * D])):
        row[0, ROW[name]:ROW[name] + len(v)] = v
    mat = np.zeros((P, NMAT), np.float32)
    mat[:, MAT["w2k"]:MAT["w2k"] + 64] = f["cmp_k_w2"][0]
    mat[:, MAT["w2v"]:MAT["w2v"] + 64] = f["cmp_v_w2"][0]
    mat[0:32, MAT["wup"]:MAT["wup"] + 512] = f["rwkv_w_up_2"][0]
    mat[32:64, MAT["wup"]:MAT["wup"] + 512] = f["rwkv_a_up_2"][0]
    mat[0:96, MAT["gup"]:MAT["gup"] + 512] = f["rwkv_g_up_2"][0]
    x_t = f["x"][0].T.reshape(KT, P, T).transpose(1, 0, 2)
    meta_t = f["meta_tokens_2"].T.reshape(KT, P, TM).transpose(1, 0, 2)
    x_in = np.concatenate([meta_t, x_t], 2)
    return {"stream": stream, "vec": vec, "row": row, "mat": mat, "cst": constants(),
            "x": np.ascontiguousarray(x_in, np.float32)}


ONCE = {
    "TensorE": (
        "nqk_ss", "nqk_rot", "dup_done", "w2_done", "kc_ss", "kc_rot", "bcum", "gate_rows", "mh_ss",
        "cmp_s", "hg_o", "hg_ss", "lora_up", "kk_ss", "sb_vt", "gn_mean", "gn_var", "bonus", "g_out"),
    "ScalarE": (
        "nqk_sq", "nqk_rs", "hx_sq", "hx_th", "kc_sq", "kc_rs", "log1p", "gates_th", "qk_th", "mh_sq",
        "mh_rs", "oz_th", "nz_th", "cmp_e", "lb_th", "f_th", "f_log", "q_th", "z_th", "hg_sq", "hg_rs",
        "lora_th", "g_th", "decay_th", "a_th", "kk_sq", "kk_rs", "e_c", "e_cx", "e_nc", "sb_v", "gn_sq",
        "gn_rs"),
    "VectorE": (
        "hx_x", "hx_arg", "gelu_ready", "kc_n", "logf", "kc_ready", "cmp_sub", "cmp_p", "lb_arg", "f_read",
        "q_ready", "kk_n2", "cum", "cum_x", "bonus_in", "g_in"),
}
NORMS = ("norm0", "norm1", "ffn1", "mix", "ffn2", "final")


def used_by(g):
    if G_E <= g < G_E + E_UNITS:
        return even_unit(g - G_E) + 1
    for g0, u0, n in ((G_EO, U_EO, KT), (G_H, U_H, H_UNITS), (G_HO, U_HO, KT),
                      (G_F1, U_F1, GU_UNITS), (G_P, U_P, P_UNITS), (G_PO, U_PO, KT), (G_F2, U_F2, GU_UNITS)):
        if g0 <= g < g0 + n:
            return u0 + (g - g0) + 1
    g0, u0 = (G_F1, U_F1) if g < G_P else (G_F2, U_F2)
    m = g - g0 - GU_UNITS
    return u0 + GU_UNITS + (FT * (m + 1) - 1) // KT + 1


def program(nc, stream, vec_d, row_d, mat_d, cst_d, x_d, out_d):
    with ExitStack() as ctx:
        def sb(name, shape, dt=F32, at=ctx):
            return at.enter_context(nc.sbuf_tensor(name, shape, dt))

        sems = {}

        def S(name):
            for engine, names in ONCE.items():
                if name in names:
                    name = engine + "_once"
            if name not in sems:
                sems[name] = ctx.enter_context(nc.semaphore(name))
            return sems[name]

        def once(name):
            for names in ONCE.values():
                if name in names:
                    return S(name), names.index(name) + 1

        ring = sb("ring", [P, SLOTS, KT * P])
        whi = sb("whi", [P, SLOTS, KT * P], F32R)
        wlo = sb("wlo", [P, SLOTS, KT * P], F32R)
        aH = sb("aH", [P, KT, TT], F32R)
        aL = sb("aL", [P, KT, TT], F32R)
        xT = sb("xT", [P, KT, TT])
        hT = sb("hT", [P, KT, TT])
        mixT = sb("mixT", [P, KT, TT])
        sq = sb("sq", [P, KT, TT])
        vec = sb("vec", [P, NVEC])
        mat = sb("mat", [P, NMAT])
        cst = sb("cst", [P, CST1])
        eps = sb("eps", [P, 4])
        ident_bf = sb("ident_bf", [P, P], BF16)
        later_bf = sb("later_bf", [P, P], BF16)
        before_bf = sb("before_bf", [P, P], BF16)
        notyet_bf = sb("notyet_bf", [P, P], BF16)
        rstd = sb("rstd", [P, TT])
        ps = ctx.enter_context(nc.psum_tensor("ps", [P, 8, 512], F32))

        b1 = ExitStack()
        row = sb("row", [P, NROW], at=b1)
        cst1 = sb("cst1", [P, NCST - CST1], at=b1)

        ev = ExitStack()
        small = sb("small", [P, 2, 32], at=ev)
        kcvc = sb("kcvc", [P, 2, T], at=ev)
        nqk = sb("nqk", [P, 6, T], at=ev)
        nz = sb("nz", [P, 4, T], at=ev)
        vsw = sb("vsw", [P, 2, 2, P], at=ev)
        qkpre = sb("qkpre", [P, 8, 3 + T], at=ev)
        flat_sq = sq[:].rearrange("p a b -> p (a b)")[:, 0:8 * T]
        oz = flat_sq.rearrange("p (a b) -> p a b", b=T)
        vtok = sb("vtok", [P, 2, 512], at=ev)
        th = qkpre[:, :, 3:3 + T]
        gl = sb("gl", [P, 6, 8], at=ev)
        rows4 = sb("rows4", [4, 4, T], at=ev)
        rs = sb("rs", [P, 6, T], at=ev)
        kct = sb("kct", [P, 4, NCMP], at=ev)
        vct = sb("vct", [NCMP, P], at=ev)
        pc = sb("pc", [P, 16, NCMP], at=ev)
        cs = sb("cs", [P, 3, 16], at=ev)
        pst = sb("pst", [P, 2, 4, 4], at=ev)
        ml = ExitStack()
        qk = sb("qk", [P, 8, T], at=ml)
        cmp = ExitStack()
        kc2 = sb("kc2", [P, 2, 2, T], at=cmp)
        xc = sb("xc", [P, 2, 16, 2 * NCMP], at=cmp)
        xcH = sb("xcH", [P, 2, 16, 2 * NCMP], F32R, at=cmp)
        xcL = sb("xcL", [P, 2, 16, 2 * NCMP], F32R, at=cmp)
        hx = sb("hx", [P, 4, 4 * NCMP], at=cmp)
        cmp.close()
        mE = sb("mE", [P, 2, 384], at=ml)
        mST = sb("mST", [P, 2, 384], at=ml)
        mem = sb("mem", [P, 2, T], at=ml)
        mad = sb("mad", [P, 2, T], at=ml)
        hm = sb("hm", [P, 4, T], at=ml)
        ml.close()
        prob = sb("prob", [P, 2, 4, 512], at=ev)
        pt = sb("pt", [P, 2, 512], at=ev)
        ev.close()

        hg = ExitStack()
        early = ExitStack()
        fF = sb("fF", [P, 8, T], at=early)
        early.close()
        hA = sb("hA", [P, 8, 3, P], at=hg)
        fK = sb("fK", [P, 8, T], at=hg)
        fQ = sb("fQ", [P, 8, T], at=hg)
        fZ = mixT[:, :, TM:TT]
        fC = flat_sq
        ivt = sb("ivt", [P, 2, D], at=hg)
        dif = sb("dif", [P, 2, 8 * T], at=hg)
        qkl = sb("qkl", [P, 2, 8 * T], at=hg)
        lbs = sb("lbs", [P, 6, 8], at=hg)
        hg.close()
        b1.close()

        ff = ExitStack()
        fact = sb("fact", [P, 2, TT], at=ff)
        fH = sb("fH", [P, FT, TT], F32R, at=ff)
        fL = sb("fL", [P, FT, TT], F32R, at=ff)
        fth = sb("fth", [P, 4, TT], at=ff)
        fhalf = sb("fhalf", [P, TT], at=ff)
        ff.close()

        mx = ExitStack()
        pr = sb("pr", [P, 14, 1 + TT], at=mx)
        pA = sb("pA", [P, 4, TT], at=mx)
        pK = sb("pK", [P, 4, TT], at=mx)
        pT = sb("pT", [P, 4, TT], at=mx)
        yT = sb("yT", [P, 4, TT], at=mx)
        eL = sb("eL", [P, 4, 5], at=mx)
        state = sb("state", [P, 2, 4, 64], at=mx)
        AR = hT[:].rearrange("p (m w) t -> p m w t", w=2)
        BK = sq[:].rearrange("p (m w) t -> p m w t", w=2)
        att = ExitStack()
        pC = sb("pC", [P, 4, TT], at=att)
        pD = sb("pD", [P, 4, TT], at=att)
        sbq = sb("sbq", [P, 4, TT], at=att)
        sbk = sb("sbk", [P, 4, 3 * P], at=att)
        sbv = sb("sbv", [P, 4, 3 * P], at=att)
        sbvt = sb("sbvt", [P, 3, 512], at=att)
        zs = sb("zs", [P, 2, 432], at=att)
        zl = sb("zl", [P, 2, 432], at=att)
        zp = sb("zp", [P, 2, 432], at=att)
        zA = sb("zA", [P, 2, 432], at=att)
        att.close()
        rw = ExitStack()
        rA = sb("rA", [P, 8, 512], at=rw)
        rN0 = sb("rN0", [P, 8, P], at=rw)
        rG = sb("rG", [P, 8, P], at=rw)
        rI = sb("rI", [P, 8, P], at=rw)
        rN = sb("rN", [P, 2, 8, P], at=rw)
        rX = sb("rX", [P, 8, P], at=rw)
        rWA = sb("rWA", [P, 8, P], at=rw)
        rUM = rX
        tok = sb("tok", [P, 3, 512], at=rw)
        phi = sb("phi", [P, 2, 4, 64], at=rw)
        psi = sb("psi", [P, 2, 4, 64], at=rw)
        rR = sb("rR", [P, 4, P], at=rw)
        rw.close()
        mx.close()

        def V(name, i=0):
            return vec[:, VEC[name] + i:VEC[name] + i + 1]

        def C(name, n=P, rows=P):
            at = CST[name]
            return cst[0:rows, at:at + n] if at < CST1 else cst1[0:rows, at - CST1:at - CST1 + n]

        def mid(ap, n):
            return ap.unsqueeze(1).broadcast_to([ap.shape[0], n, ap.shape[-1]])

        def end(ap, n):
            return ap.unsqueeze(2).broadcast_to([ap.shape[0], ap.shape[1], n])

        def in_order(eng, own):
            n = {}

            def step(ins, sem=own):
                key = next((e for e, names in ONCE.items() if sem in names), sem)
                n[key] = n.get(key, 0) + 1
                assert key == sem or once(sem)[1] == n[key], sem
                ins.then_inc(S(sem), 1)
                eng.wait_ge(S(sem), n[key])
            return step, n

        block = ctx.enter_context(nc.Block())

        @block.sync
        def _(sp):
            sp.dma_start(xT[:], x_d).then_inc(S("x_in"), 16)
            sp.dma_start(vec[:], vec_d).then_inc(S("early_in"), 16)
            sp.dma_start(cst[:, 0:2 * P], cst_d[:, 0:2 * P]).then_inc(S("early_in"), 16)
            for s in range(SLOTS):
                sp.dma_start(ring[:, s, :], stream[s]).then_inc(S(f"w_ready{s}"), 16)
            sp.dma_start(row[:], row_d.broadcast_to([P, NROW])).then_inc(S("consts_in"), 16)
            sp.dma_start(cst[:, 2 * P:], cst_d[:, 2 * P:CST1]).then_inc(S("consts_in"), 16)
            sp.dma_start(cst1[:], cst_d[:, CST1:NCST]).then_inc(S("consts_in"), 16)
            sp.dma_start(mat[:], mat_d).then_inc(S("consts_in"), 16)
            rounds = N_UNITS // SLOTS
            with sp.Fori(1, rounds) as it:
                for s in range(SLOTS):
                    sp.wait_ge(S("w_split"), it * SLOTS + (s + 1 - SLOTS))
                    sp.dma_start(ring[:, s, :], stream[it * SLOTS + s]).then_inc(S(f"w_ready{s}"), 16)
            for u in range(rounds * SLOTS, N_UNITS):
                sp.wait_ge(S("w_split"), u - SLOTS + 1)
                sp.dma_start(ring[:, u % SLOTS, :], stream[u]).then_inc(S(f"w_ready{u % SLOTS}"), 16)
            sp.wait_ge(S("norm_h"), len(NORMS) * KT)
            sp.dma_start(out_d, hT[:, :, TM:TT]).then_inc(S("out_done"), 16)
            sp.wait_ge(S("out_done"), 16)

        @block.gpsimd
        def _(pool):
            def low(s, u):
                pool.wait_ge(S("w_high"), u + 1)
                nc.gpsimd.tensor_tensor(wlo[:, s, :], ring[:, s, :], whi[:, s, :].bitcast(F32),
                                        ALU.subtract).then_inc(S("w_split"), 1)

            with pool.Fori(0, N_UNITS // SLOTS) as it:
                for s in range(SLOTS):
                    low(s, it * SLOTS + s)
            for u in range(N_UNITS // SLOTS * SLOTS, N_UNITS):
                low(u % SLOTS, u)

        @block.tensor
        def _(pe):
            def mm(out, lhsT, rhs, start=True, stop=True):
                return nc.tensor.matmul(out, lhsT, rhs, start=start, stop=stop, skip_group_check=True)

            def mm3(out, l_high, l_low, r_high, r_low, start, stop):
                mm(out, l_high, r_high, start, False)
                mm(out, l_high, r_low, False, False)
                return mm(out, l_low, r_high, False, stop)

            def weights(u):
                pe.wait_ge(S("w_split"), u + 1)
                return [w[:, u % SLOTS, :].rearrange("p (k n) -> p k n", n=P) for w in (whi, wlo)]

            def bank(g):
                if g >= MM_BANKS:
                    who = OWNER[g - MM_BANKS]
                    pe.wait_ge(S("drained_" + who), drained(who, g - MM_BANKS))
                return g % MM_BANKS

            def feature_tile(u, g, t0, ready):
                (wh, wl), b = weights(u), bank(g)
                for k in range(KT):
                    pe.wait_ge(S(ready[0]), ready[1] + k + 1)
                    m = mm3(ps[:, b, 0:TT - t0], wh[:, k, :], wl[:, k, :], aH[:, k, t0:TT], aL[:, k, t0:TT],
                            k == 0, k == KT - 1)
                m.then_inc(S("w_used"), 1)

            def token_tile(u, g, ready, width=P):
                (wh, wl), b = weights(u), bank(g)
                for tt in range(2):
                    for k in range(KT):
                        pe.wait_ge(S(ready[0]), ready[1] + k + 1)
                        tok = slice(TM + tt * P, TM + tt * P + P)
                        m = mm3(ps[:, b, tt * P:tt * P + width], aH[:, k, tok], aL[:, k, tok],
                                wh[:, k, 0:width], wl[:, k, 0:width], k == 0, k == KT - 1)
                m.then_inc(S("w_used"), 1)

            def token_pair(u, g, ready):
                pe.wait_ge(S("w_split"), u + 2)
                assert u % SLOTS + 1 < SLOTS
                b = bank(g + 1)
                wh, wl = [w[:, u % SLOTS:u % SLOTS + 2, :] for w in (whi, wlo)]
                for tt in range(2):
                    for k in range(KT):
                        pe.wait_ge(S(ready[0]), ready[1] + k + 1)
                        tok, at = slice(TM + tt * P, TM + tt * P + P), slice(k * P, (k + 1) * P)
                        m = mm3(ps[:, b, tt * T:(tt + 1) * T], aH[:, k, tok], aL[:, k, tok],
                                wh[:, :, at], wl[:, :, at], k == 0, k == KT - 1)
                m.then_inc(S("w_used"), 2)

            def norm(tag, n):
                i = NORMS.index(tag)
                if i == 0:
                    pe.wait_ge(S("early_in"), 32)
                pe.wait_ge(S("norm_sum"), (KT - 2) * (i + 1))
                mm(ps[:, 7, 0:n], C("ones"), sq[:, 0, 0:n], True, False)
                pe.wait_ge(S("norm_sq"), KT * (i + 1))
                mm(ps[:, 7, 0:n], C("ones"), sq[:, KT - 1, 0:n], False, True).then_inc(S("norm_ss"), 1)

            def even_in():
                ready = ("norm_h", 0)
                between = {13: queries_ss, 15: queries_rot, 17: doubled, C_AFTER - 1: compress, 23: second_layer,
                           25: kc_ss, 27: kc_rot, 29: forget_sums, 31: gate_rows}
                for j in range(E_UNITS):
                    if j in (E_VSW, E_V, E_V + 2):
                        token_pair(even_unit(j), G_E + j, ready)
                    elif j == E_SMALL:
                        token_tile(even_unit(j), G_E + j, ready, 32)
                    elif E_OWNER[j] == "a":
                        feature_tile(even_unit(j), G_E + j, TM, ready)
                    if j in between:
                        between[j]()

            def queries_ss():
                pe.wait_ge(S("consts_in"), 64)
                pe.wait_ge(*once("nqk_sq"))
                for j, b in enumerate((4, 5, 7)):
                    m = mm(ps[:, b, :], C("blk"), rs[:, 2 * j:2 * j + 2, :].rearrange("p a b -> p (a b)"))
                m.then_inc(S("nqk_ss"), 1)

            def queries_rot():
                pe.wait_ge(S("nqk_n"), 6)
                for j, b in enumerate((4, 5, 7)):
                    m = mm(ps[:, b, :], C("rot"), nqk[:, 2 * j:2 * j + 2, :].rearrange("p a b -> p (a b)"))
                m.then_inc(S("nqk_rot"), 1)

            def doubled():
                pe.wait_ge(S("rope_done"), 3)
                for kind in range(2):
                    for g in range(2):
                        m = mm(ps[:, 4 + kind, g * T:(g + 1) * T], C(f"dup{g}"), kcvc[:, kind, :])
                m.then_inc(S("dup_done"), 1)

            def compress():
                pe.wait_ge(S("xc_ready"), 10)
                for kind in range(2):
                    for half in range(2):
                        wh, wl = weights(U_C + 2 * kind + half)
                        for j in range(8):
                            m = mm3(ps[:, 6, kind * 32:kind * 32 + 30], wh[:, j, :], wl[:, j, :],
                                    xcH[:, kind, 8 * half + j, :], xcL[:, kind, 8 * half + j, :],
                                    half == 0 and j == 0, half == 1 and j == 7)
                        m.then_inc(S("w_used"), 1)

            def second_layer():
                pe.wait_ge(*once("gelu_ready"))
                for g in range(2):
                    mm(ps[64 * g:64 * g + 64, 6, 64:64 + NCMP], mat[:, MAT["w2k"]:MAT["w2k"] + 64], hx[:, 0, g * NCMP:(g + 1) * NCMP])
                    m = mm(ps[0:NCMP, 6, 128 + 64 * g:192 + 64 * g], hx[:, 0, 30 + g * NCMP:30 + (g + 1) * NCMP],
                           mat[:, MAT["w2v"]:MAT["w2v"] + 64])
                m.then_inc(S("w2_done"), 1)

            def kc_ss():
                pe.wait_ge(*once("kc_sq"))
                mm(ps[:, 6, 256:256 + NCMP], C("blk"), kct[:, 1, :]).then_inc(S("kc_ss"), 1)

            def kc_rot():
                pe.wait_ge(*once("kc_n"))
                mm(ps[:, 6, 288:288 + NCMP], C("rot"), kct[:, 2, :]).then_inc(S("kc_rot"), 1)

            def forget_sums():
                pe.wait_ge(*once("logf"))
                mm(ps[:, 4, 0:4], C("le"), gl[:, 3, 0:4])
                mm(ps[:, 4, 4:8], C("le"), gl[:, 3, 4:8], True, False)
                mm(ps[:, 4, 4:8], C("ones"), gl[:, 3, 0:4], False, True).then_inc(S("bcum"), 1)

            def gate_rows():
                pe.wait_ge(S("gate_cols"), 2)
                for what in range(2):
                    for tt in range(2):
                        m = nc.tensor.transpose(ps[0:4, 4, what * T + tt * P:what * T + tt * P + P],
                                                gl[:, 4 + what, tt * 4:tt * 4 + 4], C("ident"))
                m.then_inc(S("gate_rows"), 1)

            def mlstm():
                pe.wait_ge(S("row_max"), 3)
                pe.wait_ge(S("qk_ready"), 2)
                pe.wait_ge(*once("kc_ready"))
                pe.wait_ge(S("drained_a"), drained("a", G_EO - 1))

                def front(h):
                    b = 4 * (h % 2)
                    if h >= 2:
                        pe.wait_ge(S("mlstm_h"), h - 1)
                    one = C("pick", 512, 4)[:, h * P:(h + 1) * P]
                    mm(ps[:, b + 1, 0:T], one, rows4[:, 2, :], True, False)
                    mm(ps[:, b + 1, 0:P], ident_bf[:], before_bf[:], False, True)
                    mm(ps[:, b + 1, T:T + P], one, rows4[:, 2, P:T], True, False)
                    mm(ps[:, b + 1, T:T + P], ident_bf[:], before_bf[:], False, True)
                    mm(ps[:, b, 0:T], one, rows4[:, 3, :])
                    mm(ps[:, b + 2, 0:T], qk[:, 4 + h, 0:P], qk[:, h, :])
                    mm(ps[:, b + 2, T:T + P], qk[:, 4 + h, P:T], qk[:, h, P:T]).then_inc(S("mlstm_s"), 1)

                def back(h):
                    b = 4 * (h % 2)
                    pe.wait_ge(S("mlstm_st"), h + 1)
                    st = mST[:, h % 2, :]
                    for out, l0, l1 in ((0, vtok[:, 0, h * P:(h + 1) * P], vtok[:, 1, h * P:(h + 1) * P]),
                                        (T, C("ones"), C("ones"))):
                        mm(ps[:, b + 3, out:out + T], l0, st[:, 0:T], True, False)
                        m = mm(ps[:, b + 3, out + P:out + T], l1, st[:, T:T + P], False, True)
                    m.then_inc(S("mlstm_o"), 1)

                for h in range(5):
                    if h < 4:
                        front(h)
                    if h >= 1:
                        back(h - 1)
                pe.wait_ge(*once("mh_sq"))
                for j in range(2):
                    m = mm(ps[:, 4 + j, :], C("ones"), rs[:, 2 * j:2 * j + 2, :].rearrange("p a b -> p (a b)"))
                m.then_inc(S("mh_ss"), 1)

            def attention():
                pe.wait_ge(S("rope_done"), 4)
                pe.wait_ge(*once("mh_rs"))
                for qt in range(2):
                    for h in range(8):
                        i, g = h % 4, h // 4
                        m = mm(ps[:, 6 + g, (qt * 4 + i) * NCMP:(qt * 4 + i + 1) * NCMP],
                               nqk[64 * g:64 * g + 64, i, qt * P:(qt + 1) * P], kct[64 * g:64 * g + 64, 3, :])
                m.then_inc(S("cmp_s"), 1)

                def scores(n):
                    qt, g = n // 2, n % 2
                    nk = P * (qt + 1)
                    for i in range(4):
                        if n >= 1:
                            pe.wait_ge(S("att_exp"), 8 * (n - 1) + 2 * i + 2)
                        q = nqk[64 * g:64 * g + 64, i, qt * P:(qt + 1) * P]
                        for kind in range(2):
                            o = kind * T
                            mm(ps[:, i, o:o + nk], q, nqk[64 * g:64 * g + 64, 4 + kind, 0:nk], True, False)
                            m = mm(ps[:, i, o + nk - P:o + nk], ident_bf[:], later_bf[:], False, True)
                        m.then_inc(S("att_s"), 1)

                turn = [0]

                def outputs(n):
                    qt, g = n // 2, n % 2
                    pe.wait_ge(S("att_p"), 8 * n + 8)
                    pe.wait_ge(*once("cmp_p"))
                    parts = [(None, 0)] + [(kind, st) for kind in range(2) for st in range(qt + 1)]
                    if n >= 2:
                        pe.wait_ge(S("att_o"), n - 1)
                    for j, (kind, st) in enumerate(parts):
                        t = turn[0]
                        turn[0] += 1
                        if t >= 2:
                            pe.wait_ge(S("att_pt"), t - 1)
                        for i in range(4):
                            if kind is None:
                                m = nc.tensor.transpose(ps[0:NCMP, 4 + t % 2, i * P:(i + 1) * P],
                                                        pc[:, qt * 8 + 4 * g + i, :], C("ident"))
                            else:
                                m = nc.tensor.transpose(ps[:, 4 + t % 2, i * P:(i + 1) * P],
                                                        prob[:, n % 2, i, kind * T + st * P:kind * T + (st + 1) * P], C("ident"))
                        m.then_inc(S("att_tr"), 1)
                        pe.wait_ge(S("att_pt"), t + 1)
                        out = ps[64 * g:64 * g + 64, 6 + n % 2, :]
                        if kind is None:
                            m = mm(out, vct[:, 64 * g:64 * g + 64], pt[0:NCMP, t % 2, :], True, False)
                        else:
                            m = mm(out, vsw[:, kind, st, 64 * g:64 * g + 64], pt[:, t % 2, :], False, j == len(parts) - 1)
                    m.then_inc(S("att_av"), 1)

                for n in range(5):
                    if n < 4:
                        scores(n)
                    if n == 0:
                        pe.wait_ge(*once("cmp_e"))
                    if n >= 1:
                        outputs(n - 1)

            def project(u0, g0, nth, t0):
                if nth == 2:
                    pe.wait_ge(S("mix_split"), nth * KT + 5)
                for m in range(KT):
                    feature_tile(u0 + m, g0 + m, t0, ("mix_split", nth * KT))

            def hgrn_in():
                ready = ("norm_h", KT)
                for j in range(H_UNITS):
                    if H_OWNER[j] == "a":
                        feature_tile(U_H + j, G_H + j, TM, ready)
                    elif (j - H_IV) % 2 == 0:
                        token_pair(U_H + j, G_H + j, ready)

            def hgrn():
                pe.wait_ge(S("drained_a"), drained("a", G_HO - 1))
                for lev in range(9):
                    q = qkl[:, lev % 2, :].rearrange("p (h t w) -> p h t w", h=8, t=2)
                    pe.wait_ge(S("lev_qk"), 2 * lev + 2)
                    if lev < 8:
                        b0 = 4 * (lev % 2)
                        if lev >= 2:
                            pe.wait_ge(S("lev_a"), 4 * (lev - 1))
                        for j in range(16):
                            h, tt = j // 2, j % 2
                            key = q[:, h, tt, :] if lev else fK[:, h, tt * P:(tt + 1) * P]
                            query = q[:, h, tt, :] if lev else fQ[:, h, tt * P:(tt + 1) * P]
                            m = mm(ps[:, b0 + j // 4, (j % 4) * P:(j % 4 + 1) * P], key, query)
                            if j % 4 == 3:
                                m.then_inc(S("lev_s"), 1)
                    else:
                        pe.wait_ge(S("lev_a"), 4 * 7)
                        for h in range(8):
                            m = mm(ps[:, h // 4, (h % 4) * P:(h % 4 + 1) * P], q[:, h, 0, :], q[:, h, 1, :])
                            if h % 4 == 3:
                                m.then_inc(S("lev_s"), 1)
                pe.wait_ge(S("lev_a"), 4 * 8 + 2)
                for h in range(8):
                    o = ps[:, 4 + h // 2, (h % 2) * T:(h % 2 + 1) * T]
                    mm(o, ivt[:, 0, h * P:(h + 1) * P], hA[:, h, 0:2, :].rearrange("p a b -> p (a b)"), True, False)
                    m = mm(o[:, P:T], ivt[:, 1, h * P:(h + 1) * P], hA[:, h, 2, :], False, True)
                m.then_inc(S("hg_o"), 1)
                pe.wait_ge(*once("hg_sq"))
                for j in range(4):
                    m = mm(ps[:, j, :], C("ones"), dif[:, 0, j * 512:(j + 1) * 512])
                m.then_inc(S("hg_ss"), 1)

            def ffn(tag, u0, g0, first):
                d0 = drained("v", g0 - 1)

                def gate_up(it, f4, first_round=False):
                    for j in range(2 * f4, 2 * f4 + 2):
                        pe.wait_ge(S("w_split"), it * 8 + (u0 + j + 1))
                        pe.wait_ge(S("drained_v"), it * 8 + (d0 + j - 3))
                        s = (u0 + j) % SLOTS
                        for k in range(KT):
                            if first_round:
                                pe.wait_ge(S("norm_h"), NORMS.index(tag) * KT + k + 1)
                            at = slice(k * P, (k + 1) * P)
                            m = mm3(ps[:, (g0 + j) % MM_BANKS, 0:TT], whi[:, s, at], wlo[:, s, at], aH[:, k, :], aL[:, k, :],
                                    k == 0, k == KT - 1)
                        m.then_inc(S("w_used"), 1)

                for f4 in range(4):
                    gate_up(0, f4, f4 == 0)
                with pe.Fori(1, FT // 4) as it:
                    for f4 in range(4):
                        gate_up(it, f4)
                for f4 in range(FT % 4):
                    gate_up(FT // 4, f4)
                for m in range(KT):
                    b = bank(g0 + GU_UNITS + m)
                    for k in range(FT):
                        n = m * FT + k
                        u = u0 + GU_UNITS + n // KT
                        if n % KT == 0:
                            wh, wl = weights(u)
                        if m == 0:
                            pe.wait_ge(S("ffn_split"), first + k + 1)
                        last = mm3(ps[:, b, 0:TT], wh[:, n % KT, :], wl[:, n % KT, :], fH[:, k, :], fL[:, k, :],
                                   k == 0, k == FT - 1)
                        if n % KT == KT - 1:
                            last.then_inc(S("w_used"), 1)

            def mixer_in():
                for j in range(P_UNITS):
                    feature_tile(U_P + j, G_P + j, 0, ("norm_h", 3 * KT))

            def decays():
                pe.wait_ge(*once("lora_th"))
                low = pr[:, 12, 1:1 + TT]
                for j in range(4):
                    mm(ps[:, j, 0:TT], mat[0:32, MAT["wup"] + j * P:MAT["wup"] + (j + 1) * P], low[0:32])
                    m = mm(ps[:, 4 + j, 0:TT], mat[32:64, MAT["wup"] + j * P:MAT["wup"] + (j + 1) * P], low[32:64])
                m.then_inc(S("lora_up"), 1)
                pe.wait_ge(*once("kk_sq"))
                for j in range(4):
                    m = mm(ps[:, j, 0:TT], C("blk"), pT[:, j, :])
                m.then_inc(S("kk_ss"), 1)

            def sticks():
                pe.wait_ge(*once("kk_n2"))
                pe.wait_ge(S("sb_pad"), 2)
                for tt in range(3):
                    for j in range(4):
                        m = nc.tensor.transpose(ps[:, 4 + tt, j * P:(j + 1) * P], sbv[:, j, tt * P:(tt + 1) * P], C("ident"))
                m.then_inc(S("sb_vt"), 1)
                pe.wait_ge(*once("sb_v"))
                for h in range(10):
                    if h < 8:
                        a, j, b = 64 * (h % 2), h // 2, h % 4
                        if h >= 4:
                            pe.wait_ge(S("sb_ln"), h - 3)
                        mm(ps[:, b, 0:272], sbk[a:a + 64, j, 0:P], sbq[a:a + 64, j, :])
                        mm(ps[:, b, 272:416], sbk[a:a + 64, j, P:2 * P], sbq[a:a + 64, j, P:TT])
                        mm(ps[:, b, 416:432], sbk[a:a + 64, j, 2 * P:3 * P], sbq[a:a + 64, j, 2 * P:TT]).then_inc(S("sb_z"), 1)
                    if 1 <= h <= 8:
                        r, o = h - 1, ps[:, 4 + (h - 1) % 2, :]
                        pe.wait_ge(S("sb_sp"), r + 1)
                        if r >= 2:
                            pe.wait_ge(S("sb_arg"), r - 1)
                        s = zp[:, r % 2, :]
                        mm(o[:, 0:272], C("ge"), s[:, 0:272], True, False)
                        mm(o[:, 128:272], C("ones"), s[:, 272:416], False, False)
                        mm(o[:, 256:272], C("ones"), s[:, 416:432], False, False)
                        mm(o[:, 0:128], ident_bf[:], notyet_bf[:], False, True)
                        mm(o[:, 272:416], C("ge"), s[:, 272:416], True, False)
                        mm(o[:, 400:416], C("ones"), s[:, 416:432], False, False)
                        mm(o[:, 272:400], ident_bf[:], notyet_bf[:], False, True)
                        mm(o[:, 416:432], C("ge"), s[:, 416:432], True, False)
                        mm(o[:, 416:432], ident_bf[:], notyet_bf[:, 0:16], False, True).then_inc(S("sb_rest"), 1)
                    if h >= 2:
                        r = h - 2
                        a, o, A = 64 * (r % 2), ps[64 * (r % 2):64 * (r % 2) + 64, 6 + r % 2, :], zA[:, r % 2, :]
                        pe.wait_ge(S("sb_A"), r + 1)
                        if r >= 2:
                            pe.wait_ge(S("sb_out"), r - 1)
                        mm(o[:, 0:272], sbvt[:, 0, r * 64:r * 64 + 64], A[:, 0:272], True, False)
                        mm(o[:, 128:272], sbvt[:, 1, r * 64:r * 64 + 64], A[:, 272:416], False, False)
                        mm(o[:, 256:272], sbvt[:, 2, r * 64:r * 64 + 64], A[:, 416:432], False, True).then_inc(S("sb_av"), 1)

            def rwkv():
                pe.wait_ge(S("bk_ready"), 2)
                pe.wait_ge(S("sb_out"), 8)
                nth = [0]
                for tau, (t0, n) in enumerate(TILES2):
                    ar = lambda h: AR[64 * (h % 2):64 * (h % 2) + 64, h // 2, :, t0:t0 + n]
                    bk = lambda h, w: BK[64 * (h % 2):64 * (h % 2) + 64, h // 2, w, t0:t0 + n]
                    if tau:
                        pe.wait_ge(S("y_done"), tau)
                    for h in range(8):
                        m = mm(ps[0:n, 6 + h % 2, (h // 2) * n:(h // 2 + 1) * n], ar(h)[:, 0, :], bk(h, 0))
                    m.then_inc(S("r_ab"), 1)
                    for h in range(8):
                        b = h % 6
                        if h >= 6:
                            pe.wait_ge(S("r_mask"), 8 * tau + h - 5)
                        o = ps[0:n, b, 0:4 * n].rearrange("p (k w t) -> p k w t", k=2, w=2)
                        mm(o[:, 0], bk(h, 0), ar(h))
                        mm(o[:, 1], bk(h, 1), ar(h)).then_inc(S("r_mats"), 1)
                    for w in range(4):
                        b = 2 + w
                        pe.wait_ge(S("r_mask"), 8 * tau + b + 1)
                        for j in range(4):
                            src = (AR[:, j, 0, t0:t0 + n], BK[:, j, 0, t0:t0 + n], BK[:, j, 1, t0:t0 + n],
                                   pr[:, 8 + j, 1 + t0:1 + t0 + n])[w]
                            m = nc.tensor.transpose(ps[0:n, b, j * P:(j + 1) * P], src, C("ident"))
                        m.then_inc(S("r_tok"), 1)
                    pe.wait_ge(S("r_tokc"), 4 * tau + 4)
                    pe.wait_ge(S("r_mask"), 8 * tau + 8)
                    for h in range(8):
                        q = (h % 2) * 4 + h // 2
                        m = mm(ps[0:n, 6, h * 64:h * 64 + 64], rA[0:n, q, 2 * n:3 * n], tok[0:n, 2, h * 64:h * 64 + 64])
                    m.then_inc(S("r_w"), 1)
                    levels = [b for b in LEVELS[1:6] if b < n]
                    for lev in levels:
                        i = nth[0]
                        nth[0] += 2
                        for half in range(2):
                            pe.wait_ge(S("r_n"), i // 2 + 1)
                            if lev != levels[0]:
                                pe.wait_ge(S("r_g"), 2 * (i + half) - 3)
                            for k in range(4):
                                q = 4 * half + k
                                m = mm(ps[0:n, half, k * n:(k + 1) * n], rN[0:n, i // 2 % 2, q, 0:n], rG[0:n, q, 0:n])
                            m.then_inc(S("r_x"), 1)
                        for half in range(2):
                            pe.wait_ge(S("r_xc"), i + half + 1)
                            if lev != levels[0]:
                                pe.wait_ge(S("r_g"), 2 * (i + half) - 2)
                            for k in range(4):
                                q = 4 * half + k
                                m = mm(ps[0:n, 2 + half, k * n:(k + 1) * n], rI[0:n, q, 0:n], rX[0:n, q, 0:n])
                            if lev != levels[-1]:
                                for k in range(4):
                                    q = 4 * half + k
                                    m = mm(ps[0:n, 4 + half, k * n:(k + 1) * n], rX[0:n, q, 0:n], rI[0:n, q, 0:n])
                            m.then_inc(S("r_d"), 1)
                    pe.wait_ge(S("r_wc"), tau + 1)
                    pe.wait_ge(S("r_g"), 2 * nth[0])
                    for h in range(8):
                        q = (h % 2) * 4 + h // 2
                        m = mm(ps[0:n, h // 4, (h % 4) * P:(h % 4 + 1) * P], rG[0:n, q, 0:n], rWA[0:n, h, :])
                    m.then_inc(S("r_u"), 1)
                    pe.wait_ge(S("r_uc"), tau + 1)
                    for h in range(8):
                        q, a = (h % 2) * 4 + h // 2, 64 * (h % 2)
                        col = slice((h // 2) * n, (h // 2 + 1) * n)
                        mm(ps[a:a + 64, 2, col], rUM[0:n, h, 64:128], rA[0:n, q, n:2 * n])
                        mm(ps[a:a + 64, 3, col], rUM[0:n, h, 0:64], rA[0:n, q, n:2 * n], True, False)
                        m = mm(ps[a:a + 64, 3, col], tok[0:n, 2, h * 64:h * 64 + 64], rA[0:n, q, 3 * n:4 * n], False, True)
                    m.then_inc(S("r_y0"), 1)
                    chunks = [c for c, (s, _) in enumerate(RW_CHUNKS) if t0 <= s < t0 + n]
                    if tau < 2:
                        for c in chunks:
                            rows = slice(64 * (c % 2), 64 * (c % 2) + 64)
                            for h in range(8):
                                a, hh = 64 * (h % 2), slice(h * 64, h * 64 + 64)
                                o = slice((h // 2) * 64, (h // 2 + 1) * 64)
                                mm(ps[a:a + 64, 4 + c % 2, o], rUM[rows, h, 64:128], tok[rows, 0, hh])
                                o = slice(256 + (h // 2) * 64, 256 + (h // 2 + 1) * 64)
                                mm(ps[a:a + 64, 4 + c % 2, o], tok[rows, 0, hh], rUM[rows, h, 0:64], True, False)
                                m = mm(ps[a:a + 64, 4 + c % 2, o], tok[rows, 1, hh], tok[rows, 2, hh], False, True)
                            m.then_inc(S("r_phi"), 1)
                    for c in chunks:
                        cols = RW_CHUNKS[c]
                        if c >= 1:
                            pe.wait_ge(S("r_state"), c)
                            pe.wait_ge(S("r_r"), tau + 1)
                            for h in range(8):
                                a = 64 * (h % 2)
                                o = (h // 2) * n + cols[0] - t0
                                m = mm(ps[a:a + 64, 6 + h % 2, o:o + cols[1]], state[a:a + 64, c % 2, h // 2, :],
                                       rR[a:a + 64, h // 2, cols[0] - t0:cols[0] - t0 + cols[1]])
                            m.then_inc(S("r_ys"), 1)
                            if c < 4:
                                pe.wait_ge(S("r_phic"), c + 1)
                                for h in range(8):
                                    a = 64 * (h % 2)
                                    m = mm(ps[a:a + 64, h % 2, (h // 2) * 64:(h // 2 + 1) * 64],
                                           phi[a:a + 64, c % 2, h // 2, :], state[a:a + 64, c % 2, h // 2, :])
                                m.then_inc(S("r_s"), 1)
                pe.wait_ge(S("y_done"), 3)
                for j in range(4):
                    m = mm(ps[:, j, 0:TT], C("blk"), yT[:, j, :])
                m.then_inc(S("gn_mean"), 1)
                pe.wait_ge(*once("gn_sq"))
                for j in range(4):
                    m = mm(ps[:, 4 + j, 0:TT], C("blk"), pT[:, j, :])
                m.then_inc(S("gn_var"), 1)
                pe.wait_ge(*once("bonus_in"))
                for j in range(4):
                    m = mm(ps[:, j, 0:TT], C("blk"), pK[:, j, :])
                m.then_inc(S("bonus"), 1)
                pe.wait_ge(*once("g_in"))
                pe.wait_ge(*once("gn_rs"))
                for j in range(4):
                    m = mm(ps[:, 4 + j, 0:TT], mat[:, MAT["gup"] + j * P:MAT["gup"] + (j + 1) * P], pr[:, 13, 1:1 + TT])
                m.then_inc(S("g_out"), 1)

            norm("norm0", T)
            even_in()
            mlstm()
            attention()
            project(U_EO, G_EO, 0, TM)
            norm("norm1", T)
            hgrn_in()
            hgrn()
            project(U_HO, G_HO, 1, TM)
            norm("ffn1", TT)
            ffn("ffn1", U_F1, G_F1, 0)
            norm("mix", TT)
            mixer_in()
            decays()
            sticks()
            rwkv()
            project(U_PO, G_PO, 2, 0)
            norm("ffn2", TT)
            ffn("ffn2", U_F2, G_F2, FT)
            norm("final", TT)

        @block.scalar
        def _(act):
            step, act_n = in_order(act, "act_step")

            def func(out, in_, f, sem="act_step", **kw):
                step(nc.scalar.activation(out, in_, f, **kw), sem)

            LOG_EXP = "natural_log_exp_and_others"

            def square(tag, k, c0, n):
                if tag != "norm0":
                    act.wait_ge(S(before_norm[tag][0]), before_norm[tag][1] + k + 1)
                func(sq[:, k, 0:n], xT[:, k, c0:c0 + n], ACT.Square, "norm_sq")

            def norm(tag, n):
                act.wait_ge(S("norm_ss"), NORMS.index(tag) + 1)
                func(rstd[:, 0:n], ps[:, 7, 0:n], ACT.Ln, scale=1.0 / D, bias=eps[:, 0:1])
                func(rstd[:, 0:n], rstd[:, 0:n], ACT.Exp, "norm_rstd", scale=-0.5)

            def norm0():
                nc.scalar.preload_act_table_set(LOG_EXP)
                act.wait_ge(S("x_in"), 16)
                for k in range(KT):
                    square("norm0", k, TM, T)
                act.wait_ge(S("setup"), 4)
                act.wait_ge(S("early_in"), 32)
                norm("norm0", T)
                for u in range(SLOTS):
                    high(u)

            def squares_behind(tag, u0, n_units, g0, c0, n):
                nc.scalar.preload_act_table_set(LOG_EXP)
                k = 0
                for u in range(u0, u0 + n_units):
                    ahead(u)
                    while k < KT and used_by(g0 + k) <= u:
                        square(tag, k, c0, n)
                        k += 1
                for k in range(k, KT):
                    square(tag, k, c0, n)
                norm(tag, n)

            def ahead(u, it=0):
                if u + SLOTS >= N_UNITS:
                    return
                v = u + SLOTS
                act.wait_ge(S("w_used"), it * 8 + (u + 1))
                high(v, it)

            def high(v, it=0):
                act.wait_ge(S(f"w_ready{v % SLOTS}"), it * (8 // SLOTS * 16) + 16 * (v // SLOTS + 1))
                nc.scalar.activation(whi[:, v % SLOTS, :], ring[:, v % SLOTS, :], ACT.Copy).then_inc(S("w_high"), 1)

            def ahead_of(u0, n):
                for u in range(u0, u0 + n):
                    ahead(u)

            before_norm = {"norm1": ("drained_v", drained("v", G_EO - 1)), "ffn1": ("drained_v", drained("v", G_HO - 1)),
                           "mix": ("drained_v", drained("v", G_F1 + GU_UNITS - 1)), "ffn2": ("drained_v", drained("v", G_PO - 1)),
                           "final": ("drained_v", drained("v", G_F2 + GU_UNITS - 1))}

            def drain(g, out, width=T, bias=None, rows=P):
                act.wait_ge(S("w_used"), used_by(g))
                kw = {"bias": bias} if bias is not None else {}
                func(out, ps[0:rows, g % MM_BANKS, 0:width], ACT.Identity, "drained_a", **kw)

            def even_in():
                dst = {E_KC: kcvc[:, 0, :], E_KC + 1: kcvc[:, 1, :]}
                for j in range(6):
                    dst[E_NQK + j] = nqk[:, j, :]
                for j in range(8):
                    dst[E_QK + j] = qkpre[:, j, 3:3 + T]
                    dst[E_OZ + j] = oz[:, j, :]
                for j in range(4):
                    dst[E_NZ + j] = nz[:, j, :]
                between = {7: queries_sq, 13: queries_rs, C_AFTER - 1: hidden, 23: second_layer, 25: kc_rs, 27: forget_log}
                for j in range(E_UNITS):
                    if E_OWNER[j] == "a":
                        drain(G_E + j, dst[j], bias=V("ev_b", j))
                    ahead(even_unit(j))
                    if j in between:
                        between[j]()

            def queries_sq():
                func(rs[:], nqk[:], ACT.Square, "nqk_sq")

            def queries_rs():
                act.wait_ge(*once("nqk_ss"))
                for j, b in enumerate((4, 5, 7)):
                    func(rs[:, 2 * j:2 * j + 2, :], ps[:, b, :].rearrange("p (a b) -> p a b", a=2), ACT.Ln, scale=1.0 / 64, bias=eps[:, 0:1])
                func(rs[:], rs[:], ACT.Exp, "nqk_rs", scale=-0.5)

            def hidden():
                ahead_of(U_C, C_UNITS)
                act.wait_ge(*once("hx_x"))
                func(hx[:, 1, :], hx[:, 0, :], ACT.Square, "hx_sq")
                act.wait_ge(*once("hx_arg"))
                func(hx[:, 2, :], hx[:, 1, :], ACT.Tanh, "hx_th", scale=0.7978845608028654)

            def second_layer():
                act.wait_ge(*once("w2_done"))
                func(vct[:], ps[0:NCMP, 6, 128:256], ACT.Copy)
                func(kct[:, 0, :], ps[:, 6, 64:64 + NCMP], ACT.Copy)
                func(kct[:, 1, :], kct[:, 0, :], ACT.Square, "kc_sq")

            def kc_rs():
                act.wait_ge(*once("kc_ss"))
                func(kct[:, 3, :], ps[:, 6, 256:256 + NCMP], ACT.Ln, scale=1.0 / 64, bias=eps[:, 0:1])
                func(kct[:, 3, :], kct[:, 3, :], ACT.Exp, "kc_rs", scale=-0.5)

            def forget_log():
                act.wait_ge(S("fgate"), 2)
                func(gl[:, 1, :], gl[:, 0, :], ACT.Abs)
                func(gl[:, 1, :], gl[:, 1, :], ACT.Exp, scale=-1.0)
                func(gl[:, 2, :], gl[:, 1, :], ACT.Ln, "log1p", bias=eps[:, 2:3])

            def mlstm():
                func(small[:, :, 8:32], small[:, :, 8:32], ACT.Tanh, "gates_th", scale=0.5)
                act.wait_ge(S("conv"), 8)
                func(th[:], qk[:], ACT.Tanh, "qk_th", scale=0.5)
                for h in range(5):
                    if h < 4:
                        b = 4 * (h % 2)
                        act.wait_ge(S("mlstm_s"), h + 1)
                        if h >= 2:
                            act.wait_ge(S("mlstm_h"), h - 1)
                        func(mE[:, h % 2, 0:T], ps[:, b + 1, 0:T], ACT.Exp, scale=-1.0, bias=gl[:, 5, h:h + 1])
                        func(mE[:, h % 2, T:T + P], ps[:, b + 1, T:T + P], ACT.Exp, "mlstm_e", scale=-1.0,
                             bias=gl[:, 5, 4 + h:5 + h])
                        func(mem[:, h % 2, :], ps[:, b, 0:T], ACT.Exp, scale=-1.0)
                    if h >= 1:
                        act.wait_ge(S("mlstm_o"), h)
                        func(mad[:, (h - 1) % 2, :], ps[:, 4 * ((h - 1) % 2) + 3, T:2 * T], ACT.Abs, "mlstm_d")
                act.wait_ge(S("mlstm_h"), 4)
                func(rs[:, 0:4, :], hm[:], ACT.Square, "mh_sq")
                act.wait_ge(*once("mh_ss"))
                r = rs[:, 0:4, :].rearrange("p a b -> p (a b)").rearrange("p (a b) -> p a b", b=512)
                func(r, ps[:, 4:6, :], ACT.Ln, scale=1.0 / P, bias=eps[:, 0:1])
                func(rs[:, 0:4, :], rs[:, 0:4, :], ACT.Exp, "mh_rs", scale=-0.5)
                func(th[:], oz[:], ACT.Tanh, "oz_th", scale=0.5)
                act.wait_ge(S("m_out"), 4)
                func(th[:, 0:4, :], nz[:], ACT.Tanh, "nz_th", scale=0.5)

            def attention():
                act.wait_ge(*once("cmp_sub"))
                func(pc[:], pc[:], ACT.Exp, "cmp_e")
                turn = [0]
                for n in range(5):
                    if n < 4:
                        qt = n // 2
                        nk = P * (qt + 1)
                        for i in range(4):
                            act.wait_ge(S("att_max"), 4 * n + i + 1)
                            if n >= 2:
                                act.wait_ge(S("att_av"), n - 1)
                            for kind in range(2):
                                func(prob[:, n % 2, i, kind * T:kind * T + nk], ps[:, i, kind * T:kind * T + nk], ACT.Exp, "att_exp",
                                     bias=pst[:, n % 2, i, kind:kind + 1], accum_out=pst[:, n % 2, i, 2 + kind:3 + kind])
                    if n >= 1:
                        for j in range(1 + 2 * ((n - 1) // 2 + 1)):
                            t = turn[0]
                            turn[0] += 1
                            act.wait_ge(S("att_tr"), t + 1)
                            rows = NCMP if j == 0 else P
                            func(pt[0:rows, t % 2, :], ps[0:rows, 4 + t % 2, :], ACT.Copy, "att_pt")

            def hgrn_in():
                act.wait_ge(*once("lb_arg"))
                func(lbs[:, 0, :], lbs[:, 0, :], ACT.Tanh, "lb_th", scale=0.5)
                for j in range(H_UNITS):
                    if H_OWNER[j] == "a":
                        dst, bias, m = ((fF, "fp_b", j), (fQ, "qp_b", j - H_Q), (fZ, "z_b", j - H_Z0 - (8 if j > H_Z0 else 0)))[min(j // 8, 2)]
                        drain(G_H + j, dst[:, m, :], bias=V(bias, m))
                    ahead(U_H + j)
                    if H_OWNER[j] == "a":
                        if j == 7:
                            func(dif[:, 1, :].rearrange("p (a b) -> p a b", a=8), fF[:], ACT.Tanh, "f_th", scale=0.5)
                            act.wait_ge(S("f_ready"), 8)
                            func(fF[:], fF[:], ACT.Ln, "f_log")
                        if j == 15:
                            act.wait_ge(*once("f_read"))
                            func(dif[:, 1, :].rearrange("p (a b) -> p a b", a=8), fQ[:], ACT.Tanh, "q_th", scale=0.5)
                act.wait_ge(*once("q_ready"))
                func(qkl[:, 0, :].rearrange("p (a b) -> p a b", a=8), fZ, ACT.Tanh, "z_th", scale=0.5)

            def hgrn():
                for lev, b in enumerate(LEVELS + (P,)):
                    act.wait_ge(S("lev_d"), lev + 1)
                    d = dif[:, lev % 2, :].rearrange("p (n w) -> p n w", w=2 * b)
                    func(d[:, :, 0:b], d[:, :, 0:b], ACT.Exp, "lev_e", scale=-1.0)
                    func(d[:, :, b:], d[:, :, b:], ACT.Exp, "lev_e")
                act.wait_ge(*once("hg_o"))
                func(dif[:, 0, :], ps[:, 4:8, :].rearrange("p a b -> p (a b)"), ACT.Square, "hg_sq")
                act.wait_ge(*once("hg_ss"))
                func(dif[:, 1, :], ps[:, 0:4, :].rearrange("p a b -> p (a b)"), ACT.Ln, scale=1.0 / P, bias=eps[:, 0:1])
                func(dif[:, 1, :], dif[:, 1, :], ACT.Exp, "hg_rs", scale=-0.5)

            def ffn(u0, g0, first):
                d0 = drained("v", g0 - 1)

                def gate(it, f4):
                    act.wait_ge(S("w_used"), it * 8 + (u0 + 2 * f4 + 1))
                    act.wait_ge(S("drained_v"), it * 8 + (d0 + 2 * f4 + 1 - 8))
                    nc.scalar.activation(fth[:, f4, :], ps[:, (g0 + 2 * f4) % MM_BANKS, 0:TT], ACT.Tanh,
                                         scale=0.5).then_inc(S("ffn_th"), 1)
                    ahead(u0 + 2 * f4, it)
                    ahead(u0 + 2 * f4 + 1, it)

                with act.Fori(0, FT // 4) as it:
                    for f4 in range(4):
                        gate(it, f4)
                for f4 in range(FT % 4):
                    gate(FT // 4, f4)
                act.wait_ge(S("ffn_th"), first + FT)

            def mixer_in():
                for j in range(P_UNITS):
                    if j < 12:
                        dst = (sbq, sbk, sbv)[j // 4][:, j % 4, 0:TT]
                        act.wait_ge(S("w_used"), used_by(G_P + j))
                        func(dst, ps[:, (G_P + j) % MM_BANKS, 0:TT], ACT.Copy, "drained_a", scale=0.125 if j < 4 else 1.0)
                    else:
                        drain(G_P + j, pr[:, j - 12, 1:1 + TT], TT)
                    ahead(U_P + j)
                act.wait_ge(S("shifted"), 14)
                func(pr[0:32, 12, 1:1 + TT], pr[0:32, 12, 1:1 + TT], ACT.Tanh, "lora_th")
                func(pr[:, 13, 1:1 + TT], pr[:, 13, 1:1 + TT], ACT.Tanh, "g_th", scale=0.5)
                act.wait_ge(*once("lora_up"))
                for j in range(4):
                    func(pD[:, j, :], ps[:, j, 0:TT], ACT.Tanh, "decay_th" if j == 3 else "act_step", scale=0.5, bias=V("w0", j))
                for j in range(4):
                    func(pA[:, j, :], ps[:, 4 + j, 0:TT], ACT.Tanh, "a_th" if j == 3 else "act_step", scale=0.5, bias=V("a0", j))
                nc.scalar.preload_act_table_set(LOG_EXP)
                act.wait_ge(S("kk_raw"), 4)
                func(pT[:], pK[:], ACT.Square, "kk_sq")
                act.wait_ge(*once("kk_n2"))
                func(pT[:], pT[:], ACT.Ln, scale=2.0 ** 20)
                func(pT[:], pT[:], ACT.Exp, "kk_rs", scale=-0.5, bias=eps[:, 3:4])
                act.wait_ge(*once("cum"))
                func(pT[:], pC[:], ACT.Exp, "e_c")
                act.wait_ge(*once("cum_x"))
                func(pD[:], pD[:], ACT.Exp, "e_cx")
                func(pC[:], pC[:], ACT.Exp, "e_nc", scale=-1.0)

            def sticks():
                act.wait_ge(*once("sb_vt"))
                func(sbvt[:], ps[:, 4:7, :], ACT.Copy, "sb_v")
                for h in range(10):
                    if h < 8:
                        p = h % 2
                        act.wait_ge(S("sb_z"), h + 1)
                        if h >= 2:
                            act.wait_ge(S("sb_arg"), h - 1)
                        z = ps[:, h % 4, 0:432]
                        func(zs[:, p, :], z, ACT.Copy)
                        func(zl[:, p, :], z, ACT.Abs)
                        func(zl[:, p, :], zl[:, p, :], ACT.Exp, scale=-1.0)
                        func(zl[:, p, :], zl[:, p, :], ACT.Ln, "sb_ln", bias=eps[:, 2:3])
                    if 1 <= h <= 8:
                        r = h - 1
                        act.wait_ge(S("sb_arg"), r + 1)
                        if r >= 2:
                            act.wait_ge(S("sb_av"), r - 1)
                        func(zA[:, r % 2, :], zs[:, r % 2, :], ACT.Exp, "sb_A")
                    if h >= 2:
                        r = h - 2
                        a = 64 * (r % 2)
                        act.wait_ge(S("sb_av"), r + 1)
                        func(mixT[a:a + 64, r // 2, :], ps[a:a + 64, 6 + r % 2, 0:TT], ACT.Copy, "sb_out")

            def rwkv():
                nth = [0]
                for tau, (t0, n) in enumerate(TILES2):
                    for w in range(4):
                        act.wait_ge(S("r_tok"), 4 * tau + w + 1)
                        src = ps[0:n, 2 + w, :]
                        if w == 0:
                            func(rWA[0:n, :, 64:128], src.rearrange("p (h j) -> p h j", j=64), ACT.Copy, "r_tokc")
                        else:
                            func(tok[0:n, w - 1, :], src, ACT.Copy, "r_tokc")
                    act.wait_ge(S("r_w"), tau + 1)
                    func(rWA[0:n, :, 0:64], ps[0:n, 6, :].rearrange("p (h j) -> p h j", j=64), ACT.Copy, "r_wc")
                    for _ in [b for b in LEVELS[1:6] if b < n]:
                        for q in range(2):
                            nth[0] += 1
                            act.wait_ge(S("r_x"), nth[0])
                            func(rX[0:n, 4 * q:4 * q + 4, 0:n], ps[0:n, q, 0:4 * n].rearrange("p (q t) -> p q t", q=4), ACT.Copy, "r_xc")
                    act.wait_ge(S("r_u"), tau + 1)
                    for q in range(2):
                        func(rUM[0:n, 4 * q:4 * q + 4, :], ps[0:n, q, :].rearrange("p (q t) -> p q t", q=4), ACT.Copy,
                             "r_uc" if q else "act_step", scale=-1.0)
                    act.wait_ge(S("r_y0"), tau + 1)
                    func(yT[:, :, t0:t0 + n], ps[:, 3, 0:4 * n].rearrange("p (q t) -> p q t", q=4), ACT.Copy, "r_y0c")
                act.wait_ge(S("gn_d"), 4)
                func(pT[:], yT[:], ACT.Square, "gn_sq")
                act.wait_ge(*once("gn_var"))
                nc.scalar.preload_act_table_set(LOG_EXP)
                func(pT[:], ps[:, 4:8, 0:TT], ACT.Ln, scale=1.0 / 64, bias=eps[:, 1:2])
                func(pT[:], pT[:], ACT.Exp, "gn_rs", scale=-0.5)

            norm0()
            even_in()
            mlstm()
            attention()
            squares_behind("norm1", U_EO, KT, G_EO, TM, T)
            hgrn_in()
            hgrn()
            squares_behind("ffn1", U_HO, KT, G_HO, 0, TT)
            ffn(U_F1, G_F1, 0)
            squares_behind("mix", U_F1 + GU_UNITS, DN_UNITS, G_F1 + GU_UNITS, 0, TT)
            mixer_in()
            sticks()
            rwkv()
            squares_behind("ffn2", U_PO, KT, G_PO, 0, TT)
            ffn(U_F2, G_F2, FT)
            squares_behind("final", U_F2 + GU_UNITS, DN_UNITS, G_F2 + GU_UNITS, 0, TT)

        @block.vector
        def _(dve):
            step, dve_n = in_order(dve, "dve_step")

            def tt(out, a, b, op, sem="dve_step"):
                step(nc.vector.tensor_tensor(out, a, b, op), sem)

            def ts(out, a, s1, s2, op0, op1=None, sem="dve_step"):
                if op1 is None:
                    step(nc.vector.tensor_scalar(out, a, s1, s2, op0), sem)
                else:
                    step(nc.vector.tensor_scalar(out, a, s1, s2, op0, op1), sem)

            def stt(out, a, s, b, op0, op1, sem="dve_step"):
                step(nc.vector.scalar_tensor_tensor(out=out, in0=a, scalar=s, in1=b, op0=op0, op1=op1), sem)

            def add_square(tag, k, n):
                dve.wait_ge(S("norm_sq"), NORMS.index(tag) * KT + k + 1)
                tt(sq[:, 0, 0:n], sq[:, 0, 0:n], sq[:, k, 0:n], ALU.add, "norm_sum")

            def norm(tag, c0, n, w):
                i = NORMS.index(tag) * KT
                if tag == "norm0":
                    for k in range(1, KT - 1):
                        add_square(tag, k, n)
                dve.wait_ge(S("norm_rstd"), NORMS.index(tag) + 1)
                if tag == "norm0":
                    dve.wait_ge(S("early_in"), 32)
                split = tag != "final"
                for j in range(KT + 2):
                    if j < KT:
                        nc.vector.scalar_tensor_tensor(out=hT[:, j, c0:c0 + n], in0=xT[:, j, c0:c0 + n], scalar=V(w, j),
                                                       in1=rstd[:, 0:n], op0=ALU.mult, op1=ALU.mult)\
                            .then_inc(S("norm_x" if split else "norm_h"), 1)
                    if split and 1 <= j <= KT:
                        k = j - 1
                        dve.wait_ge(S("norm_x"), i + k + 1)
                        nc.vector.tensor_copy(aH[:, k, c0:c0 + n], hT[:, k, c0:c0 + n]).then_inc(S("norm_hi"), 1)
                    if split and j >= 2:
                        k = j - 2
                        dve.wait_ge(S("norm_hi"), i + k + 1)
                        nc.vector.tensor_tensor(aL[:, k, c0:c0 + n], hT[:, k, c0:c0 + n], aH[:, k, c0:c0 + n].bitcast(F32),
                                                ALU.subtract).then_inc(S("norm_h"), 1)
                dve.wait_ge(S("norm_h"), i + KT)

            def mix_split(k, c0):
                step(nc.vector.tensor_copy(aH[:, k, c0:TT], mixT[:, k, c0:TT]))
                tt(aL[:, k, c0:TT], mixT[:, k, c0:TT], aH[:, k, c0:TT].bitcast(F32), ALU.subtract, "mix_split")

            def setup():
                for j, v in enumerate((EPS, LNX_EPS, 1.0, 10 * float(np.log(2.0)))):
                    step(nc.vector.memset(eps[:, j:j + 1], v), "setup")
                step(nc.vector.memset(qkpre[:, :, 0:3], 0.0), "setup")

            def masks():
                dve.wait_ge(S("consts_in"), 64)
                step(nc.vector.tensor_copy(ident_bf[:], C("ident")), "setup")
                ts(before_bf[:], C("gt"), BIG, None, ALU.mult, sem="setup")
                ts(notyet_bf[:], C("ge"), BIG, None, ALU.mult, sem="setup")
                ts(later_bf[:], C("ge"), 1.0, BIG, ALU.subtract, ALU.mult, sem="setup")
                ts(vec[:, VEC["w0"]:VEC["w0"] + 8], vec[:, VEC["w0"]:VEC["w0"] + 8], 0.5, None, ALU.mult, sem="setup")
                ts(vec[:, VEC["nqk"]:VEC["nqk"] + 4], vec[:, VEC["nqk"]:VEC["nqk"] + 4], 0.125, None, ALU.mult, sem="setup")

            def drain_pair(g, outs, off):
                dve.wait_ge(S("w_used"), used_by(g + 1))
                for j, out in enumerate(outs):
                    src = ps[:, (g + 1) % MM_BANKS, :].rearrange("p (t u n) -> p t u n", t=2, u=2)[:, :, j, :]
                    tt(out, src, mid(row[:, off + j * P:off + (j + 1) * P], 2), ALU.add, "drained_v")

            def convolved(j):
                dve.wait_ge(S("drained_a"), drained("a", G_E + E_QK + j))
                c = lambda tap: V("conv_w", 4 * j + tap)
                ts(qk[:, j, :], qkpre[:, j, 0:T], c(0), V("conv_b", j), ALU.mult, ALU.add)
                for tap in range(1, 4):
                    stt(qk[:, j, :], qkpre[:, j, tap:tap + T], c(tap), qk[:, j, :], ALU.mult, ALU.add,
                        "conv" if tap == 3 else "dve_step")

            def even_in():
                drain_pair(G_E + E_VSW, [vsw[:, 0], vsw[:, 1]], ROW["vs"])
                for j in range(3):
                    convolved(j)
                dve.wait_ge(*once("nqk_rs"))
                for j in range(6):
                    stt(nqk[:, j, :], nqk[:, j, :], V("nqk", j), rs[:, j, :], ALU.mult, ALU.mult, "nqk_n")
                for j in range(3, 5):
                    convolved(j)
                dve.wait_ge(*once("nqk_rot"))
                for j, b in enumerate((4, 5, 7)):
                    tt(rs[:, 2 * j:2 * j + 2, :], ps[:, b, :].rearrange("p (a b) -> p a b", a=2), mid(C("sin", T), 2), ALU.mult, "rope_done")
                tt(nqk[:], nqk[:], mid(C("cos", T), 6), ALU.mult)
                tt(nqk[:], nqk[:], rs[:], ALU.add, "rope_done")
                for j in range(5, 8):
                    convolved(j)
                compress()
                for j in (0, 2):
                    drain_pair(G_E + E_V + j, [vtok[:, :, (j + i) * P:(j + i + 1) * P] for i in range(2)], ROW["v"] + j * P)
                hidden()
                dve.wait_ge(S("w_used"), used_by(G_E + E_SMALL))
                tt(small[:], ps[:, (G_E + E_SMALL) % MM_BANKS, 0:T].rearrange("p (t n) -> p t n", t=2)[:, :, 0:32],
                   mid(row[:, ROW["small"]:ROW["small"] + 32], 2), ALU.add, "drained_v")
                for j in range(2):
                    tt(gl[:, 0, 4 * j:4 * j + 4], small[:, j, 4:8], row[:, ROW["fbias"]:ROW["fbias"] + 4], ALU.add, "fgate")
                dve.wait_ge(*once("kc_rs"))
                stt(kct[:, 2, :], kct[:, 0, :], V("kcn"), kct[:, 3, :], ALU.mult, ALU.mult, "kc_n")
                dve.wait_ge(*once("log1p"))
                stt(gl[:, 3, :], gl[:, 0, :], 0.0, gl[:, 2, :], ALU.min, ALU.subtract, "logf")
                dve.wait_ge(*once("kc_rot"))
                tt(kct[:, 0, :], ps[:, 6, 288:288 + NCMP], C("sinc", NCMP), ALU.mult)
                tt(kct[:, 3, :], kct[:, 2, :], C("cosc", NCMP), ALU.mult)
                tt(kct[:, 3, :], kct[:, 3, :], kct[:, 0, :], ALU.add, "kc_ready")

            def compress():
                dve.wait_ge(*once("dup_done"))
                for kind in range(2):
                    d = ps[:, 4 + kind, :].rearrange("p (g t) -> p g t", g=2)
                    step(nc.vector.tensor_copy(kc2[0:64, kind, :, :], d[0:64]))
                    step(nc.vector.tensor_copy(kc2[64:128, kind, :, 0:T - 1], d[64:128, :, 1:T]))
                for kind in range(2):
                    for g in range(2):
                        for a in range(2):
                            pos = vec[:, VEC[("kpos", "vpos")[kind]] + 8 * a:VEC[("kpos", "vpos")[kind]] + 8 * a + 8]
                            v = kc2[:, kind, g, :].rearrange("p (n j two) -> p j n two", n=16, two=2)[:, :, a:a + NCMP, 0]
                            tt(xc[:, kind, 8 * a:8 * a + 8, g * NCMP:(g + 1) * NCMP], v, end(pos, NCMP), ALU.add, "xc_ready")
                step(nc.vector.tensor_copy(xcH[:], xc[:]), "xc_ready")
                tt(xcL[:], xc[:], xcH[:].bitcast(F32), ALU.subtract, "xc_ready")

            def hidden():
                dve.wait_ge(S("w_used"), U_C + C_UNITS)
                h4 = ps[:, 6, 0:64].rearrange("p (k n) -> p k n", k=2)[:, :, 0:30]
                step(nc.vector.tensor_copy(hx[:, 0, :].rearrange("p (k n) -> p k n", k=2), h4), "hx_x")
                dve.wait_ge(*once("hx_sq"))
                ts(hx[:, 1, :], hx[:, 1, :], 0.044715, 1.0, ALU.mult, ALU.add)
                tt(hx[:, 1, :], hx[:, 1, :], hx[:, 0, :], ALU.mult, "hx_arg")
                dve.wait_ge(*once("hx_th"))
                ts(hx[:, 2, :], hx[:, 2, :], 0.5, 0.5, ALU.mult, ALU.add)
                tt(hx[:, 0, :], hx[:, 2, :], hx[:, 0, :], ALU.mult, "gelu_ready")

            def mlstm():
                dve.wait_ge(*once("bcum"))
                step(nc.vector.tensor_copy(gl[:, 4, :], ps[:, 4, 0:8]), "gate_cols")
                tt(gl[:, 5, :].rearrange("p (a b) -> p a b", a=2), small[:, :, 0:4], gl[:, 4, :].rearrange("p (a b) -> p a b", a=2),
                   ALU.subtract, "gate_cols")
                dve.wait_ge(*once("gate_rows"))
                step(nc.vector.tensor_copy(rows4[:, 0:2, :].rearrange("p a b -> p (a b)"), ps[0:4, 4, :]), "row_max")
                step(nc.vector.tensor_tensor_scan(rows4[:, 2, :], rows4[:, 1, :], rows4[:, 1, :], 0.0, ALU.max, ALU.max), "row_max")
                tt(rows4[:, 3, :], rows4[:, 2, :], rows4[:, 0, :], ALU.add, "row_max")
                dve.wait_ge(*once("qk_th"))
                for j in range(2):
                    stt(qk[:, 4 * j:4 * j + 4, :], th[:, 4 * j:4 * j + 4, :], 1.0, qk[:, 4 * j:4 * j + 4, :], ALU.add, ALU.mult, "qk_ready")
                for h in range(5):
                    if h < 4:
                        dve.wait_ge(S("mlstm_e"), h + 1)
                        stt(mST[:, h % 2, :], ps[:, 4 * (h % 2) + 2, 0:384], 0.25 * P ** -0.5, mE[:, h % 2, :], ALU.mult, ALU.mult, "mlstm_st")
                    if h >= 1:
                        j = (h - 1) % 2
                        dve.wait_ge(S("mlstm_d"), h)
                        tt(mad[:, j, :], mad[:, j, :], mem[:, j, :], ALU.max)
                        step(nc.vector.reciprocal(mad[:, j, :], mad[:, j, :]))
                        tt(hm[:, h - 1, :], ps[:, 4 * j + 3, 0:T], mad[:, j, :], ALU.mult, "mlstm_h")
                dve.wait_ge(*once("mh_rs"))
                tt(hm[:], hm[:], rs[:, 0:4, :], ALU.mult)
                dve.wait_ge(*once("oz_th"))
                stt(hm[:], th[:, 0:4, :], 1.0, hm[:], ALU.add, ALU.mult)
                stt(oz[:, 4:8, :], th[:, 4:8, :], 1.0, oz[:, 4:8, :], ALU.add, ALU.mult)
                tt(hm[:], hm[:], oz[:, 4:8, :], ALU.mult)
                for h in range(4):
                    ts(mixT[:, h, TM:TT], hm[:, h, :], V("mnorm", h), 0.25, ALU.mult, ALU.mult, "m_out")
                for k in range(4):
                    mix_split(k, TM)

            def attention():
                dve.wait_ge(*once("cmp_s"))
                for qt in range(2):
                    for g in range(2):
                        s = ps[:, 6 + g, qt * 4 * NCMP:(qt + 1) * 4 * NCMP].rearrange("p (i n) -> p i n", i=4)
                        tt(pc[:, qt * 8 + 4 * g:qt * 8 + 4 * g + 4, :], s, mid(C("cneg", 2 * NCMP)[:, qt * NCMP:(qt + 1) * NCMP], 4), ALU.add)
                step(nc.vector.tensor_reduce(cs[:, 0, :], pc[:], AX.X, ALU.max))
                tt(pc[:], pc[:], end(cs[:, 0, :], NCMP), ALU.subtract, "cmp_sub")
                dve.wait_ge(*once("cmp_e"))
                step(nc.vector.tensor_reduce(cs[:, 1, :], pc[:], AX.X, ALU.add))
                for qt in range(2):
                    tt(pc[:, qt * 8:qt * 8 + 8, :], pc[:, qt * 8:qt * 8 + 8, :],
                       mid(C("cok", 2 * NCMP)[:, qt * NCMP:(qt + 1) * NCMP], 8), ALU.mult)
                step(nc.vector.reciprocal(cs[:, 1, :], cs[:, 1, :]))
                dve.wait_ge(*once("gates_th"))
                gates = small[:, :, 8:32]
                ts(gates, gates, 0.5, 0.5, ALU.mult, ALU.add)
                g3 = small[:, :, 8:32].rearrange("p t (h b) -> p t h b", b=3)
                tt(cs[:, 2, :].rearrange("p (t h) -> p t h", t=2), cs[:, 1, :].rearrange("p (t h) -> p t h", t=2), g3[:, :, :, 0], ALU.mult)
                tt(pc[:], pc[:], end(cs[:, 2, :], NCMP), ALU.mult, "cmp_p")
                dve.wait_ge(*once("nz_th"))
                stt(nz[:], th[:, 0:4, :], 1.0, nz[:], ALU.add, ALU.mult)
                for n in range(5):
                    if n < 4:
                        qt, g = n // 2, n % 2
                        nk = P * (qt + 1)
                        for i in range(4):
                            dve.wait_ge(S("att_s"), 4 * n + i + 1)
                            s = ps[:, i, :].rearrange("p (k n) -> p k n", k=2)[:, :, 0:nk]
                            step(nc.vector.tensor_reduce(pst[:, n % 2, i, 0:2], s, AX.X, ALU.max, negate=True), "att_max")
                        for i in range(4):
                            dve.wait_ge(S("att_exp"), 8 * n + 2 * i + 2)
                            r = pst[:, n % 2, i, 2:4]
                            step(nc.vector.reciprocal(r, r))
                            tt(r, r, g3[:, qt, 4 * g + i, 1:3], ALU.mult)
                            for kind in range(2):
                                p = prob[:, n % 2, i, kind * T:kind * T + nk]
                                ts(p, p, pst[:, n % 2, i, 2 + kind:3 + kind], None, ALU.mult, sem="att_p")
                    if n >= 1:
                        qt, g = (n - 1) // 2, (n - 1) % 2
                        dve.wait_ge(S("att_av"), n)
                        rows = slice(64 * g, 64 * g + 64)
                        stt(mixT[rows, 4:8, TM + qt * P:TM + (qt + 1) * P],
                            ps[rows, 6 + (n - 1) % 2, :].rearrange("p (i q) -> p i q", i=4), 0.5,
                            nz[rows, :, qt * P:(qt + 1) * P], ALU.mult, ALU.mult, "att_o")
                for k in range(4, 8):
                    mix_split(k, TM)

            def residual(tag, g0, c0, scale=1.0):
                for m in range(KT):
                    if m >= 2:
                        add_square(tag, m - 1, TT - (TM if tag == "norm1" else 0))
                    dve.wait_ge(S("w_used"), used_by(g0 + m))
                    stt(xT[:, m, c0:TT], ps[:, (g0 + m) % MM_BANKS, 0:TT - c0], scale, xT[:, m, c0:TT], ALU.mult, ALU.add, "drained_v")

            def hgrn_in():
                lb = lambda j: lbs[:, j, :]
                l0, l1 = vec[:, VEC["lb0"]:VEC["lb0"] + 8], vec[:, VEC["lb1"]:VEC["lb1"] + 8]
                tt(lb(0), l0, l1, ALU.subtract, "lb_arg")
                dve.wait_ge(*once("lb_th"))
                ts(lb(1), lb(0), -0.25, 0.25, ALU.mult, ALU.add)
                ts(lb(2), lb(1), -1.0, 1.0, ALU.mult, ALU.add)
                ts(lb(3), lb(1), 0.5, None, ALU.mult)
                ts(lb(4), lb(1), -0.5, None, ALU.mult)
                step(nc.vector.memset(dif[:, 0, :], 1.0))
                step(nc.vector.memset(dif[:, 0, :].rearrange("p (n w) -> p n w", w=P)[:, :, 0:1], 0.0))
                dve.wait_ge(*once("f_th"))
                t8 = dif[:, 1, :].rearrange("p (a b) -> p a b", a=8)
                for h in range(8):
                    ts(fF[:, h, :], t8[:, h, :], lbs[:, 1, h:h + 1], lbs[:, 2, h:h + 1], ALU.mult, ALU.add, "f_ready")
                for h in range(8):
                    ts(fK[:, h, :], t8[:, h, :], lbs[:, 4, h:h + 1], lbs[:, 3, h:h + 1], ALU.mult, ALU.add,
                       "f_read" if h == 7 else "dve_step")
                dve.wait_ge(*once("f_log"))
                step(nc.vector.tensor_tensor_scan(fC, dif[:, 0, :], fF[:].rearrange("p a b -> p (a b)"),
                                                  0.0, ALU.mult, ALU.add))
                dve.wait_ge(*once("q_th"))
                stt(fQ[:], t8, 1.0, fQ[:], ALU.add, ALU.mult, "q_ready")
                for j in range(0, 8, 2):
                    drain_pair(G_H + H_IV + j, [ivt[:, :, (j + i) * P:(j + i + 1) * P] for i in range(2)], ROW["iv"] + j * P)

            def hgrn():
                blocks = lambda ap: ap.rearrange("p (h t w) -> p h t w", h=2, t=2)

                def banks_of(lev):
                    for j in range(4):
                        dve.wait_ge(S("lev_s"), 4 * lev + j + 1)
                        out = hA[:, 2 * j:2 * j + 2, 0:3:2, :]
                        src = blocks(ps[:, 4 * (lev % 2) + j, :])
                        if lev == 0:
                            m = C("ident")
                        else:
                            m = C("hlev", 7 * P)[:, (lev - 1) * P:lev * P]
                        m = m.unsqueeze(1).unsqueeze(1).broadcast_to([P, 2, 2, P])
                        if lev == 0:
                            for t in range(2):
                                tt(out[:, :, t, :], src[:, :, t, :], m[:, :, t, :], ALU.mult, "lev_a" if t else "dve_step")
                        else:
                            step(nc.vector.copy_predicated(out, m.bitcast(U32), src), "lev_a")

                def scaled(lev):
                    b = (LEVELS + (P,))[lev - 1]
                    cv = fC.rearrange("p (n w) -> p n w", w=2 * b)
                    d = dif[:, (lev - 1) % 2, :].rearrange("p (n w) -> p n w", w=2 * b)
                    n = 8 * T // (2 * b)
                    if lev < 8:
                        tt(d, cv, cv[:, :, b - 1:b].broadcast_to([P, n, 2 * b]), ALU.subtract, "lev_d")
                    else:
                        tt(d[:, :, 0:b], cv[:, :, 0:b], cv[:, :, b - 1:b].broadcast_to([P, n, b]), ALU.subtract)
                        step(nc.vector.tensor_copy(d[:, :, b:], cv[:, :, b:]), "lev_d")

                def products(lev):
                    b = (LEVELS + (P,))[lev - 1]
                    view = lambda ap: ap.rearrange("p (n w) -> p n w", w=2 * b)
                    d, o = view(dif[:, (lev - 1) % 2, :]), view(qkl[:, lev % 2, :])
                    flat = lambda t: view(t[:].rearrange("p a b -> p (a b)"))
                    dve.wait_ge(S("lev_e"), 2 * lev)
                    if lev >= 3:
                        dve.wait_ge(S("lev_s"), 4 * (lev - 1))
                    tt(o[:, :, 0:b], d[:, :, 0:b], flat(fK)[:, :, 0:b], ALU.mult, "lev_qk")
                    tt(o[:, :, b:], d[:, :, b:], flat(fQ)[:, :, b:], ALU.mult, "lev_qk")

                dve.wait_ge(*once("z_th"))
                dve.wait_ge(S("drained_a"), drained("a", G_HO - 1))
                stt(fZ, qkl[:, 0, :].rearrange("p (a b) -> p a b", a=8), 1.0, fZ, ALU.add, ALU.mult)
                for j in range(2):
                    step(nc.vector.memset(lbs[:, 5, j:j + 1], 0.0), "lev_qk")
                scaled(1)
                for lev in range(1, 9):
                    if lev < 8:
                        scaled(lev + 1)
                    products(lev)
                    banks_of(lev - 1)
                for j in range(2):
                    dve.wait_ge(S("lev_s"), 4 * 8 + j + 1)
                    step(nc.vector.tensor_copy(hA[:, 4 * j:4 * j + 4, 1, :], ps[:, j, :].rearrange("p (h w) -> p h w", h=4)), "lev_a")
                dve.wait_ge(*once("hg_rs"))
                tt(dif[:, 1, :], dif[:, 1, :], ps[:, 4:8, :].rearrange("p a b -> p (a b)"), ALU.mult)
                for h in range(8):
                    ts(dif[:, 1, h * T:(h + 1) * T], dif[:, 1, h * T:(h + 1) * T], V("hnorm", h), 0.5, ALU.mult, ALU.mult)
                    tt(mixT[:, h, TM:TT], dif[:, 1, h * T:(h + 1) * T], fZ[:, h, :], ALU.mult)
                    mix_split(h, TM)

            def ffn(u0, g0, first):
                d0 = drained("v", g0 - 1)

                def pair(it, f4, f):
                    half, prod = fhalf[:], fact[:, f4 % 2, :]
                    dve.wait_ge(S("ffn_th"), it * 4 + (first + f4 + 1))
                    dve.wait_ge(S("drained_v"), it * 8 + (d0 + 2 * f4))
                    nc.vector.scalar_tensor_tensor(out=half, in0=fth[:, f4, :], scalar=1.0,
                                                   in1=ps[:, (g0 + 2 * f4) % MM_BANKS, 0:TT], op0=ALU.add,
                                                   op1=ALU.mult).then_inc(S("drained_v"), 1)
                    dve.wait_ge(S("drained_v"), it * 8 + (d0 + 2 * f4 + 1))
                    dve.wait_ge(S("w_used"), it * 8 + (u0 + 2 * f4 + 2))
                    nc.vector.tensor_tensor(prod, half, ps[:, (g0 + 2 * f4 + 1) % MM_BANKS, 0:TT],
                                            ALU.mult).then_inc(S("drained_v"), 1)
                    dve.wait_ge(S("drained_v"), it * 8 + (d0 + 2 * f4 + 2))
                    nc.vector.tensor_copy(fH[:, f, :], prod).then_inc(S("ffn_hi"), 1)
                    dve.wait_ge(S("ffn_hi"), it * 4 + (first + f4 + 1))
                    nc.vector.tensor_tensor(fL[:, f, :], prod, fH[:, f, :].bitcast(F32),
                                            ALU.subtract).then_inc(S("ffn_split"), 1)
                    dve.wait_ge(S("ffn_split"), it * 4 + (first + f4 + 1))

                with dve.Fori(0, FT // 4) as it:
                    for f4 in range(4):
                        pair(it, f4, it * 4 + f4)
                for f4 in range(FT % 4):
                    pair(FT // 4, f4, FT - FT % 4 + f4)
                dve.wait_ge(S("drained_v"), d0 + GU_UNITS)
                dve_n["drained_v"] += GU_UNITS
                residual("mix" if first == 0 else "final", g0 + GU_UNITS, 0, 0.25)

            def mixer_in():
                step(nc.vector.memset(pr[:, :, 0:1], 0.0))
                step(nc.vector.memset(sbk[:, :, TT:], 0.0), "sb_pad")
                step(nc.vector.memset(sbv[:, :, TT:], 0.0), "sb_pad")
                for j in range(14):
                    dve.wait_ge(S("drained_a"), drained("a", G_P + 12 + j))
                    tmp = pT[:, j % 4, :]
                    tt(tmp, pr[:, j, 0:TT], pr[:, j, 1:1 + TT], ALU.subtract)
                    stt(pr[:, j, 1:1 + TT], tmp, V("mu", j), pr[:, j, 1:1 + TT], ALU.mult, ALU.add, "shifted")
                k = pr[:, 4:8, 1:1 + TT]
                for j in range(4):
                    ts(pK[:, j, :], k[:, j, :], V("k_k", j), None, ALU.mult, sem="kk_raw")
                dve.wait_ge(*once("decay_th"))
                ts(pD[:], pD[:], -0.5 * DECAY, -0.5 * DECAY, ALU.mult, ALU.add)
                dve.wait_ge(*once("a_th"))
                ts(pA[:], pA[:], 0.5, 0.5, ALU.mult, ALU.add)
                dve.wait_ge(*once("kk_ss"))
                ts(pT[:], ps[:, 0:4, 0:TT], 1e-24, None, ALU.max, sem="kk_n2")
                dve.wait_ge(*once("kk_rs"))
                tt(pK[:], pK[:], pT[:], ALU.mult)
                for j in range(4):
                    ts(pT[:, j, :], pA[:, j, :], 1.0, V("k_a", j), ALU.subtract, ALU.mult)
                stt(k, pT[:], 1.0, k, ALU.add, ALU.mult)
                tt(pA[:], pA[:], pK[:], ALU.mult)
                step(nc.vector.memset(pT[:], 1.0))
                step(nc.vector.memset(pT[:, :, 0:TT:RW_CHUNK], 0.0))
                flat = lambda t: t[:].rearrange("p a b -> p (a b)")
                step(nc.vector.tensor_tensor_scan(flat(pC), flat(pT), flat(pD), 0.0, ALU.mult, ALU.add), "cum")
                tt(pD[:], pC[:], pD[:], ALU.subtract, "cum_x")
                dve.wait_ge(*once("e_c"))
                step(nc.vector.tensor_copy(eL[:, :, 0:4], pT[:, :, RW_CHUNK - 1:4 * RW_CHUNK:RW_CHUNK]))
                tt(AR[:, :, 1, :], pr[:, 0:4, 1:1 + TT], pT[:], ALU.mult)
                dve.wait_ge(*once("e_cx"))
                tt(AR[:, :, 0, :], pK[:], pD[:], ALU.mult)
                dve.wait_ge(*once("e_nc"))
                tt(BK[:, :, 0, :], pA[:], pC[:], ALU.mult, "bk_ready")
                tt(BK[:, :, 1, :], k, pC[:], ALU.mult, "bk_ready")

            def sticks():
                for h in range(9):
                    if h < 8:
                        p = h % 2
                        dve.wait_ge(S("sb_ln"), h + 1)
                        stt(zl[:, p, :], zs[:, p, :], 0.0, zl[:, p, :], ALU.max, ALU.add)
                        tt(zp[:, p, :], zl[:, p, :], C("sbok", 432), ALU.mult, "sb_sp")
                    if h >= 1:
                        r = h - 1
                        dve.wait_ge(S("sb_rest"), r + 1)
                        tt(zs[:, r % 2, :], zs[:, r % 2, :], ps[:, 4 + r % 2, 0:432], ALU.subtract, "sb_arg")

            def rwkv():
                dve.wait_ge(S("sb_out"), 8)
                for k in range(4):
                    mix_split(k, 0)
                nth = [0]
                for tau, (t0, n) in enumerate(TILES2):
                    q8 = lambda ap: mid(ap, 8)
                    part = lambda t: t[0:n, :, 0:n]
                    rl = lambda j: C("rlev", 6 * P)[0:n, j * P:j * P + n]
                    dve.wait_ge(S("r_ab"), tau + 1)
                    for q in range(2):
                        step(nc.vector.tensor_copy(rN0[0:n, 4 * q:4 * q + 4, 0:n], ps[0:n, 6 + q, 0:4 * n].rearrange("p (q t) -> p q t", q=4)))
                    mask = C("rwmask", 512)[0:n].rearrange("p (k t) -> p k t", k=4)[:, :, 0:n]
                    for h in range(8):
                        dve.wait_ge(S("r_mats"), 8 * tau + h + 1)
                        q = (h % 2) * 4 + h // 2
                        tt(rA[0:n, q, 0:4 * n].rearrange("p (k t) -> p k t", k=4),
                           ps[0:n, h % 6, 0:4 * n].rearrange("p (k t) -> p k t", k=4), mask, ALU.mult, "r_mask")
                    tt(part(rG), rA[0:n, :, 0:n], q8(C("rlevt")[0:n, 0:n]), ALU.mult)
                    tt(part(rG), q8(C("ident")[0:n, 0:n]), part(rG), ALU.subtract)
                    tt(part(rI), part(rN0), q8(rl(0)), ALU.mult)
                    tt(part(rI), q8(C("ident")[0:n, 0:n]), part(rI), ALU.subtract)
                    levels = [j for j in range(1, 6) if LEVELS[j] < n]
                    def level_part(j):
                        nth[0] += 1
                        tt(rN[0:n, (nth[0] - 1) % 2, :, 0:n], part(rN0), q8(rl(j)), ALU.mult, "r_n")

                    level_part(levels[0])
                    for j in levels:
                        i = 2 * nth[0] - 2
                        if j != levels[-1]:
                            level_part(j + 1)
                        for q in range(2):
                            dve.wait_ge(S("r_d"), i + q + 1)
                            for dst, b in ((rG, 2), (rI, 4)):
                                if b == 4 and j == levels[-1]:
                                    dve.sem_inc(S("r_g"), 1)
                                    dve_n["r_g"] += 1
                                    continue
                                d = dst[0:n, 4 * q:4 * q + 4, 0:n]
                                tt(d, d, ps[0:n, b + q, 0:4 * n].rearrange("p (q t) -> p q t", q=4), ALU.subtract, "r_g")
                    dve.wait_ge(S("r_y0"), tau + 1)
                    tt(rR[:, :, 0:n], ps[:, 2, 0:4 * n].rearrange("p (q t) -> p q t", q=4), AR[:, :, 1, t0:t0 + n], ALU.add, "r_r")
                    dve.wait_ge(S("r_y0c"), tau + 1)
                    if tau < 2:
                        for c in (2 * tau, 2 * tau + 1):
                            dve.wait_ge(S("r_phi"), c + 1)
                            v = ps[:, 4 + c % 2, :].rearrange("p (w q i) -> p w q i", w=2, q=4)
                            tt(psi[:, c % 2], v[:, 1], end(eL[:, :, c], 64), ALU.mult)
                            tt(phi[:, c % 2], v[:, 0], mid(C("istack", 64), 4), ALU.add, "r_phic")
                    for c in [c for c, (s, _) in enumerate(RW_CHUNKS) if t0 <= s < t0 + n]:
                        start, width = RW_CHUNKS[c]
                        if c >= 1:
                            dve.wait_ge(S("r_ys"), c)
                            for a in range(2):
                                rows = slice(64 * a, 64 * a + 64)
                                o = ps[rows, 6 + a, 0:4 * n].rearrange("p (q t) -> p q t", q=4)[:, :, start - t0:start - t0 + width]
                                tt(yT[rows, :, start:start + width], yT[rows, :, start:start + width], o, ALU.add)
                        if c == 0:
                            step(nc.vector.tensor_copy(state[:, 1], psi[:, 0]), "r_state")
                        elif c < 4:
                            dve.wait_ge(S("r_s"), c)
                            for a in range(2):
                                rows = slice(64 * a, 64 * a + 64)
                                s = state[rows, (c + 1) % 2]
                                tt(s, ps[rows, a, 0:256].rearrange("p (q i) -> p q i", q=4), end(eL[rows, :, c], 64), ALU.mult)
                            tt(state[:, (c + 1) % 2], state[:, (c + 1) % 2], psi[:, c % 2], ALU.add, "r_state")
                    step(nc.vector.memset(rstd[:, 0:1], 0.0), "y_done")
                for j in range(4):
                    if j == 0:
                        dve.wait_ge(*once("gn_mean"))
                    stt(yT[:, j, :], ps[:, j, 0:TT], -1.0 / 64, yT[:, j, :], ALU.mult, ALU.add, "gn_d")
                for j in range(4):
                    ts(pK[:, j, :], pr[:, j, 1:1 + TT], V("r_k", j), None, ALU.mult)
                tt(pK[:], pK[:], pr[:, 4:8, 1:1 + TT], ALU.mult, "bonus_in")
                dve.wait_ge(*once("g_th"))
                ts(pr[:, 13, 1:1 + TT], pr[:, 13, 1:1 + TT], 0.5, 0.5, ALU.mult, ALU.add, "g_in")
                dve.wait_ge(*once("gn_rs"))
                tt(yT[:], yT[:], pT[:], ALU.mult)
                for j in range(4):
                    ts(yT[:, j, :], yT[:, j, :], V("lnx_w", j), V("lnx_b", j), ALU.mult, ALU.add)
                dve.wait_ge(*once("bonus"))
                tt(pT[:], ps[:, 0:4, 0:TT], pr[:, 8:12, 1:1 + TT], ALU.mult)
                tt(yT[:], yT[:], pT[:], ALU.add)
                dve.wait_ge(*once("g_out"))
                for j in range(4):
                    tt(mixT[:, 4 + j, :], yT[:, j, :], ps[:, 4 + j, 0:TT], ALU.mult)
                    mix_split(4 + j, 0)

            setup()
            norm("norm0", TM, T, "norm0")
            masks()
            even_in()
            mlstm()
            attention()
            residual("norm1", G_EO, TM)
            norm("norm1", TM, T, "norm1")
            hgrn_in()
            hgrn()
            residual("ffn1", G_HO, TM)
            norm("ffn1", 0, TT, "ffn1")
            ffn(U_F1, G_F1, 0)
            norm("mix", 0, TT, "mix")
            mixer_in()
            sticks()
            rwkv()
            residual("ffn2", G_PO, 0)
            norm("ffn2", 0, TT, "ffn2")
            ffn(U_F2, G_F2, FT)
            norm("final", 0, TT, "final")


_ORDER = ("stream", "vec", "row", "mat", "cst", "x")


def kernel(**inputs):
    import concourse.bacc as bacc
    from concourse.bass_utils import run_bass_kernel_spmd

    packed = pack(inputs)
    nc = bacc.Bacc("TRN2", target_bir_lowering=False, num_devices=1)
    arrays = {"in_" + n: packed[n] for n in _ORDER}
    args = [nc.dram_tensor("in_" + n, packed[n].shape, F32, kind="ExternalInput").ap() for n in _ORDER]
    out = nc.dram_tensor("out", (P, KT, T), F32, kind="ExternalOutput").ap()
    program(nc, *args, out)
    r = run_bass_kernel_spmd(nc, [arrays], core_ids=[0])
    got = np.asarray(r.results[0]["out"])
    return np.ascontiguousarray(got.transpose(2, 1, 0).reshape(1, T, D))
```

```python
from contextlib import ExitStack

import numpy as np
import concourse.bass as bass
from concourse import mybir

F32 = mybir.dt.float32
F32R = mybir.dt.float32r
BF16 = mybir.dt.bfloat16
U32 = mybir.dt.uint32
ALU = mybir.AluOpType
ACT = mybir.ActivationFunctionType
AX = mybir.AxisListType

P = 128
D = 1024
KT = D // P
T = 256
TM = 16
TT = T + TM
EPS = 1e-6
LNX_EPS = 64e-5
BIG = 1e30
NCMP = 15
FF = 2816
FT = FF // P
SLOTS = 4
LEVELS = (1, 2, 4, 8, 16, 32, 64)
RW_CHUNK = 64
RW_CHUNKS = [(c, min(RW_CHUNK, TT - c)) for c in range(0, TT, RW_CHUNK)]
TILES2 = [(0, 128), (128, 128), (256, 16)]
DECAY = float(np.exp(-0.5))

E_UNITS = 35
C_UNITS = 4
H_UNITS = 32
GU_UNITS = 2 * FT
DN_UNITS = FT
P_UNITS = 26
U_E = 0
C_AFTER = 22
U_C = U_E + C_AFTER
U_EO = U_E + E_UNITS + C_UNITS
U_H = U_EO + KT
U_HO = U_H + H_UNITS
U_F1 = U_HO + KT
U_P = U_F1 + GU_UNITS + DN_UNITS
U_PO = U_P + P_UNITS
U_F2 = U_PO + KT
N_UNITS = U_F2 + GU_UNITS + DN_UNITS

E_KC, E_NQK, E_VSW, E_QK, E_V, E_SMALL, E_OZ, E_NZ = 0, 2, 8, 10, 18, 22, 23, 31
E_OWNER = "a" * 8 + "vv" + "a" * 8 + "vvvv" + "a" * 13
H_F, H_Q, H_Z0, H_IV, H_Z1 = 0, 8, 16, 17, 25
H_OWNER = "a" * 17 + "v" * 8 + "a" * 7
G_E = 0
G_EO = G_E + E_UNITS
G_H = G_EO + KT
G_HO = G_H + H_UNITS
G_F1 = G_HO + KT
G_P = G_F1 + GU_UNITS + KT
G_PO = G_P + P_UNITS
G_F2 = G_PO + KT
OWNER = (E_OWNER + "v" * KT + H_OWNER + "v" * KT + "v" * (GU_UNITS + KT) + "a" * P_UNITS
         + "v" * KT + "v" * (GU_UNITS + KT))
MM_BANKS = 4


def drained(owner, g):
    return OWNER[:g + 1].count(owner)


def even_unit(j):
    return U_E + j + (C_UNITS if j >= C_AFTER else 0)


def _offsets(parts):
    at, out = 0, {}
    for name, n in parts:
        out[name] = at
        at += n
    return out, at


VEC, NVEC = _offsets([
    ("norm0", 8), ("norm1", 8), ("ffn1", 8), ("mix", 8), ("ffn2", 8), ("final", 8),
    ("ev_b", 35), ("conv_w", 32), ("conv_b", 8), ("mnorm", 4), ("nqk", 6), ("kcn", 1),
    ("fp_b", 8), ("qp_b", 8), ("z_b", 8), ("lb0", 8), ("lb1", 8), ("hnorm", 8),
    ("mu", 14), ("w0", 4), ("a0", 4), ("k_k", 4), ("k_a", 4), ("r_k", 4), ("lnx_w", 4), ("lnx_b", 4),
    ("kpos", 16), ("vpos", 16)])
ROW, NROW = _offsets([("fbias", 4), ("vs", 128), ("vw", 128), ("v", 512), ("iv", 1024)])
MAT, NMAT = _offsets([("w2k", 64), ("w2v", 64), ("wup", 512), ("gup", 512)])
CST, NCST = _offsets([
    ("ident", 128), ("ones", 128), ("blk", 128), ("ge", 128),
    ("sbok", 432), ("rwmask", 512), ("rlev", 6 * 128), ("rlevt", 128), ("istack", 64),
    ("le", 128), ("gt", 128), ("cos", 256), ("sin", 256), ("rot", 128), ("dup0", 128), ("dup1", 128),
    ("pick", 512), ("cosc", NCMP), ("sinc", NCMP), ("cneg", 2 * NCMP), ("cok", 2 * NCMP), ("hlev", 7 * 128)])
CST1 = CST["le"]


def constants():
    c = np.zeros((P, NCST), np.float32)

    def put(name, a):
        c[:a.shape[0], CST[name]:CST[name] + a.shape[1]] = a

    i = np.arange(P)
    row, col = i[:, None], i[None, :]
    put("ident", np.eye(P))
    put("ones", np.ones((P, P)))
    put("blk", (row // 64 == col // 64) * 1.0)
    put("ge", (row >= col) * 1.0)
    put("le", (row <= col) * 1.0)
    put("gt", (row > col) * 1.0)

    def rope(pos):
        half = 8
        inv = (500000.0 ** (-np.arange(half, dtype=np.float32) / np.float32(half))).astype(np.float32)
        ang = pos.astype(np.float32)[None, :] * inv[:, None]
        cos, sin = np.ones((P, len(pos))), np.zeros((P, len(pos)))
        for g in range(2):
            for s in range(2):
                cos[64 * g + 8 * s:64 * g + 8 * s + 8] = np.cos(ang)
                sin[64 * g + 8 * s:64 * g + 8 * s + 8] = np.sin(ang)
        return cos, sin

    cos, sin = rope(np.arange(T))
    put("cos", cos)
    put("sin", sin)
    cos, sin = rope(np.arange(NCMP) * 16 + 31)
    put("cosc", cos)
    put("sinc", sin)
    rot = np.zeros((P, P))
    for g in range(2):
        for k in range(8):
            rot[64 * g + 8 + k, 64 * g + k] = -1.0
            rot[64 * g + k, 64 * g + 8 + k] = 1.0
    put("rot", rot)
    for g in range(2):
        dup = np.zeros((P, P))
        for d in range(64):
            dup[64 * g + d, d] = dup[64 * g + d, 64 + d] = 1.0
        put(f"dup{g}", dup)
    pick = np.zeros((4, 4, P))
    for h in range(4):
        pick[h, h] = 1.0
    put("pick", pick.reshape(4, 512))
    ok = (np.arange(NCMP)[None, None, :] * 16 + 31 <= (np.arange(2)[None, :, None] * P + i[:, None, None]))
    put("cok", ok.reshape(P, -1) * 1.0)
    put("cneg", np.where(ok, 0.0, -BIG).reshape(P, -1))
    lev = [((row // (2 * b) == col // (2 * b)) & (row % (2 * b) < b) & (col % (2 * b) >= b)) for b in LEVELS]
    put("hlev", np.concatenate(lev, 1) * 1.0)
    put("rlev", np.concatenate([m.T for m in lev[:6]], 1) * 1.0)
    put("rlevt", lev[0] * 1.0)
    strict, incl = (row < col), (row <= col)
    put("sbok", np.concatenate([strict, np.ones((P, 144)), strict, np.ones((P, 16)), strict[:, :16]], 1) * 1.0)
    same = row // RW_CHUNK == col // RW_CHUNK
    put("rwmask", np.concatenate([strict & same, incl & same] * 2, 1) * 1.0)
    put("istack", (row % 64 == np.arange(64)[None, :]) * 1.0)
    return c


def pack(i):
    f = {k: np.asarray(v) for k, v in i.items()}
    ev_w, ev_b = f["ev_w_in"][0], f["ev_b_in"][0]
    nsa = 2568
    r = np.arange
    pair = [np.concatenate([r(64) + 64 * j, r(64) + 64 * (4 + j)]) for j in range(4)]
    ev_cols = [nsa + 512 + r(128), nsa + 640 + r(128)]
    ev_cols += [nsa + pair[j] for j in range(4)]
    ev_cols += [nsa + 768 + r(128), nsa + 1024 + r(128), nsa + 896 + r(128), nsa + 1152 + r(128)]
    ev_cols += [r(128) + 128 * j for j in range(12)]
    ev_cols += [np.concatenate([r(2560, 2568), nsa + 1280 + r(24)])]
    ev_cols += [r(128) + 128 * j for j in range(12, 20)]
    ev_cols += [nsa + 1304 + pair[j] for j in range(4)]
    assert len(ev_cols) == E_UNITS
    stream = np.zeros((N_UNITS, P, KT * P), np.float32)
    at = [0]

    def unit(w):
        k, n = w.shape[0] // P, w.shape[1]
        stream[at[0]].reshape(P, KT, P)[:, :k, :n] = w.reshape(k, P, n).transpose(1, 0, 2)
        at[0] += 1

    def units(w):
        for m in range(w.shape[1] // P):
            unit(w[:, m * P:(m + 1) * P])

    def ffn(gate, up, down):
        for m in range(FT):
            unit(gate[:, m * P:(m + 1) * P])
            unit(up[:, m * P:(m + 1) * P])
        blocks = down.reshape(FT, P, KT, P).transpose(2, 0, 1, 3).reshape(FT, KT, P, P)
        for u in range(FT):
            stream[at[0]].reshape(P, KT, P)[:] = blocks[u].transpose(1, 0, 2)
            at[0] += 1

    for c in ev_cols[:C_AFTER]:
        unit(ev_w[:, c])
    for w1 in (f["cmp_k_w1"][0], f["cmp_v_w1"][0]):
        unit(w1[:1024])
        unit(w1[1024:])
    for c in ev_cols[C_AFTER:]:
        unit(ev_w[:, c])
    rows = np.concatenate([r(512)] + [512 + pair[j] for j in range(4)])
    units(f["ev_w_out"][0][rows])
    od = f["od_w_in"][0]
    for lo, hi in ((0, D), (2 * D, 3 * D), (3 * D, 3 * D + P), (D, 2 * D), (3 * D + P, 4 * D)):
        units(od[:, lo:hi])
    units(f["od_w_out"][0])
    ffn(f["ffn1_w_gate_2"][0], f["ffn1_w_up_2"][0], f["ffn1_w_down_2"][0])
    w_in = f["w_in_2"][0]
    units(w_in[:, :3072])
    unit(w_in[:, 3072:3136])
    unit(w_in[:, 3136:3232])
    units(f["w_out_2"][0])
    ffn(f["ffn2_w_gate_2"][0], f["ffn2_w_up_2"][0], f["ffn2_w_down_2"][0])
    assert at[0] == N_UNITS

    vec = np.zeros((P, NVEC), np.float32)

    def col(name, v):
        v = v.reshape(-1, P).T
        vec[:, VEC[name]:VEC[name] + v.shape[1]] = v

    col("norm0", f["norm_w"][0])
    col("norm1", f["norm_w"][1])
    for name, key in (("ffn1", "ffn1_norm_2"), ("mix", "mix_norm_2"), ("ffn2", "ffn2_norm_2"), ("final", "final_norm_2"),
                      ("conv_b", "mlstm_conv_b"), ("mnorm", "mlstm_head_norm"), ("hnorm", "hgrn_head_norm"),
                      ("w0", "rwkv_w0_2"), ("a0", "rwkv_a0_2"), ("k_k", "rwkv_k_k_2"), ("k_a", "rwkv_k_a_2"),
                      ("r_k", "rwkv_r_k_2"), ("lnx_w", "rwkv_lnx_w_2"), ("lnx_b", "rwkv_lnx_b_2")):
        col(name, f[key])
    for m, c in enumerate(ev_cols):
        vec[:len(c), VEC["ev_b"] + m] = ev_b[c]
    vec[:, VEC["conv_w"]:VEC["conv_w"] + 32] = f["mlstm_conv_w"][0].reshape(4, 8, P).transpose(2, 1, 0).reshape(P, 32)
    qn, kn = f["nsa_q_norm"][0], f["nsa_k_norm"][0]
    for m, v in enumerate([qn] * 4 + [kn[1], kn[2]]):
        vec[:64, VEC["nqk"] + m] = vec[64:, VEC["nqk"] + m] = v
    vec[:64, VEC["kcn"]] = vec[64:, VEC["kcn"]] = kn[0]
    ob = f["od_b_in"][0]
    col("fp_b", ob[:D])
    col("qp_b", ob[2 * D:3 * D])
    col("z_b", ob[3 * D:])
    col("lb0", f["hgrn_lb_logits"][0])
    col("lb1", f["hgrn_lb_logits"][1])
    mu = f["rwkv_mu_2"][0]
    col("mu", mu[:1536])
    vec[:64, VEC["mu"] + 12] = mu[1536:1600]
    vec[:96, VEC["mu"] + 13] = mu[1600:]
    col("kpos", f["cmp_k_pos"][0].reshape(16, P))
    col("vpos", f["cmp_v_pos"][0].reshape(16, P))

    row = np.zeros((1, NROW), np.float32)
    for name, v in (("fbias", f["mlstm_f_bias"][0]), ("vs", ev_b[ev_cols[E_VSW]]),
                    ("vw", ev_b[ev_cols[E_VSW + 1]]), ("v", ev_b[1024:1536]), ("iv", ob[D:2 * D])):
        row[0, ROW[name]:ROW[name] + len(v)] = v
    mat = np.zeros((P, NMAT), np.float32)
    mat[:, MAT["w2k"]:MAT["w2k"] + 64] = f["cmp_k_w2"][0]
    mat[:, MAT["w2v"]:MAT["w2v"] + 64] = f["cmp_v_w2"][0]
    mat[0:32, MAT["wup"]:MAT["wup"] + 512] = f["rwkv_w_up_2"][0]
    mat[32:64, MAT["wup"]:MAT["wup"] + 512] = f["rwkv_a_up_2"][0]
    mat[0:96, MAT["gup"]:MAT["gup"] + 512] = f["rwkv_g_up_2"][0]
    x_t = f["x"][0].T.reshape(KT, P, T).transpose(1, 0, 2)
    meta_t = f["meta_tokens_2"].T.reshape(KT, P, TM).transpose(1, 0, 2)
    x_in = np.concatenate([meta_t, x_t], 2)
    return {"stream": stream, "vec": vec, "row": row, "mat": mat, "cst": constants(),
            "x": np.ascontiguousarray(x_in, np.float32)}


ONCE = {
    "TensorE": (
        "nqk_ss", "nqk_rot", "dup_done", "small_t", "hx_t", "w2_done", "kc_ss", "kc_rot", "bcum", "gate_rows",
        "cmp_s", "mh_ss", "hg_o", "hg_o2", "hg_ss", "hg_ss2", "sb_vt", "lora_up", "kk_ss", "kk_ss2", "gn_mean", "bonus", "gn_var", "g_out"),
    "ScalarE": (
        "nqk_sq", "nqk_rs", "hx_sq", "hx_th", "hx_f", "kc_sq", "kc_rs", "log1p", "gates_th", "qk_th", "nz_th", "oz_th",
        "mh_sq", "cmp_e", "mh_rs", "lb_th", "f_th", "f_log", "q_th", "z_th", "hg_sq", "hg_sq2", "hg_rs", "hg_rs2",
        "sb_v", "lora_th", "g_th", "decay_th", "a_th", "kk_sq", "kk_rs", "e_c", "e_cx", "e_nc", "gn_sq",
        "gn_rs"),
    "VectorE": (
        "hx_x", "hx_arg", "gelu_ready", "kc_n", "logf", "kc_ready", "cmp_sub", "cmp_p", "lb_arg", "f_read",
        "q_ready", "kk_n2", "kk_n2b", "cum", "cum_x", "bonus_in", "g_in", "bonus_out"),
}
NORMS = ("norm0", "norm1", "ffn1", "mix", "ffn2", "final")


def used_by(g):
    if G_E <= g < G_E + E_UNITS:
        return even_unit(g - G_E) + 1
    for g0, u0, n in ((G_EO, U_EO, KT), (G_H, U_H, H_UNITS), (G_HO, U_HO, KT),
                      (G_F1, U_F1, GU_UNITS), (G_P, U_P, P_UNITS), (G_PO, U_PO, KT), (G_F2, U_F2, GU_UNITS)):
        if g0 <= g < g0 + n:
            return u0 + (g - g0) + 1
    g0, u0 = (G_F1, U_F1) if g < G_P else (G_F2, U_F2)
    m = g - g0 - GU_UNITS
    return u0 + GU_UNITS + (FT * (m + 1) - 1) // KT + 1


def program(nc, stream, vec_d, row_d, mat_d, cst_d, x_d, out_d):
    with ExitStack() as ctx:
        def sb(name, shape, dt=F32, at=ctx):
            return at.enter_context(nc.sbuf_tensor(name, shape, dt))

        sems = {}

        def S(name):
            for engine, names in ONCE.items():
                if name in names:
                    name = engine + "_once"
            if name not in sems:
                sems[name] = ctx.enter_context(nc.semaphore(name))
            return sems[name]

        def once(name):
            for names in ONCE.values():
                if name in names:
                    return S(name), names.index(name) + 1

        ring = sb("ring", [P, SLOTS, KT * P])
        whi = sb("whi", [P, SLOTS, KT * P], F32R)
        wlo = sb("wlo", [P, SLOTS, KT * P], F32R)
        aH = sb("aH", [P, KT, TT], F32R)
        aL = sb("aL", [P, KT, TT], F32R)
        xT = sb("xT", [P, KT, TT])
        hT = sb("hT", [P, KT, TT])
        mixT = sb("mixT", [P, KT, TT])
        sq = sb("sq", [P, KT, TT])
        vec = sb("vec", [P, NVEC])
        mat = sb("mat", [P, NMAT])
        cst = sb("cst", [P, CST1])
        eps = sb("eps", [P, 4])
        ident_bf = sb("ident_bf", [P, P], BF16)
        later_bf = sb("later_bf", [P, P], BF16)
        before_bf = sb("before_bf", [P, P], BF16)
        notyet_bf = sb("notyet_bf", [P, P], BF16)
        rstd = sb("rstd", [P, TT])
        ps = ctx.enter_context(nc.psum_tensor("ps", [P, 8, 512], F32))

        b1 = ExitStack()
        row = sb("row", [P, NROW], at=b1)
        cst1 = sb("cst1", [P, NCST - CST1], at=b1)

        ev = ExitStack()
        small = sb("small", [P, 2, 32], at=ev)
        smallT = sb("smallT", [P, T], at=ev)
        kcvc = sb("kcvc", [P, 2, T], at=ev)
        nqk = sb("nqk", [P, 6, T], at=ev)
        nz = sb("nz", [P, 4, T], at=ev)
        vsw = sb("vsw", [P, 2, 2, P], at=ev)
        qkpre = sb("qkpre", [P, 8, 3 + T], at=ev)
        flat_sq = sq[:].rearrange("p a b -> p (a b)")[:, 0:8 * T]
        oz = flat_sq.rearrange("p (a b) -> p a b", b=T)
        vtok = sb("vtok", [P, 2, 512], at=ev)
        th = qkpre[:, :, 3:3 + T]
        gl = sb("gl", [P, 6, 8], at=ev)
        rows4 = sb("rows4", [4, 4, T], at=ev)
        rs = sb("rs", [P, 6, T], at=ev)
        kct = sb("kct", [P, 4, NCMP], at=ev)
        vct = sb("vct", [NCMP, P], at=ev)
        pc = sb("pc", [P, 16, NCMP], at=ev)
        cs = sb("cs", [P, 3, 16], at=ev)
        pst = sb("pst", [P, 2, 4, 4], at=ev)
        mem = sb("mem", [P, 4, T], at=ev)
        hm = sb("hm", [P, 4, T], at=ev)
        ml = ExitStack()
        qk = sb("qk", [P, 8, T], at=ml)
        cmp = ExitStack()
        kc2 = sb("kc2", [P, 2, 2, T], at=cmp)
        xc = sb("xc", [P, 2, 16, 2 * NCMP], at=cmp)
        xcH = sb("xcH", [P, 2, 16, 2 * NCMP], F32R, at=cmp)
        xcL = sb("xcL", [P, 2, 16, 2 * NCMP], F32R, at=cmp)
        hx = sb("hx", [2 * NCMP, 3, 2 * P], at=cmp)
        hf = sb("hf", [P, 2, 32], at=cmp)
        cmp.close()
        mE = sb("mE", [P, 2, 384], at=ml)
        mST = sb("mST", [P, 2, 384], at=ml)
        mad = sb("mad", [P, 4, T], at=ml)
        ml.close()
        prob = sb("prob", [P, 2, 4, 512], at=ev)
        pt = sb("pt", [P, 2, 512], at=ev)
        ev.close()

        hg = ExitStack()
        early = ExitStack()
        fF = sb("fF", [P, 8, T], at=early)
        early.close()
        hA = sb("hA", [P, 8, 2, P], at=hg)
        fK = sb("fK", [P, 8, T], at=hg)
        fQ = sb("fQ", [P, 8, T], at=hg)
        fZ = mixT[:, :, TM:TT]
        fC = flat_sq
        ivt = sb("ivt", [P, 2, D], at=hg)
        dif = sb("dif", [P, 2, 8 * T], at=hg)
        qkl = sb("qkl", [P, 2, 8 * T], at=hg)
        lbs = sb("lbs", [P, 6, 8], at=hg)
        hX = sb("hX", [P, 8, P], at=hg)
        hg.close()
        b1.close()

        ff = ExitStack()
        fact = sb("fact", [P, 2, TT], at=ff)
        fH = sb("fH", [P, FT, TT], F32R, at=ff)
        fL = sb("fL", [P, FT, TT], F32R, at=ff)
        fth = sb("fth", [P, 4, TT], at=ff)
        fhalf = sb("fhalf", [P, TT], at=ff)
        ff.close()

        mx = ExitStack()
        pr = sb("pr", [P, 14, 1 + TT], at=mx)
        pA = sb("pA", [P, 4, TT], at=mx)
        pK = sb("pK", [P, 4, TT], at=mx)
        pT = sb("pT", [P, 4, TT], at=mx)
        yT = sb("yT", [P, 4, TT], at=mx)
        eL = sb("eL", [P, 4, 5], at=mx)
        state = sb("state", [P, 2, 4, 64], at=mx)
        AR = hT[:].rearrange("p (m w) t -> p m w t", w=2)
        BK = sq[:].rearrange("p (m w) t -> p m w t", w=2)
        att = ExitStack()
        pC = sb("pC", [P, 4, TT], at=att)
        pD = sb("pD", [P, 4, TT], at=att)
        sbq = sb("sbq", [P, 4, TT], at=att)
        sbk = sb("sbk", [P, 4, 3 * P], at=att)
        sbv = sb("sbv", [P, 4, 3 * P], at=att)
        sbvt = sb("sbvt", [P, 3, 512], at=att)
        zs = sb("zs", [P, 4, 432], at=att)
        zl = sb("zl", [P, 2, 432], at=att)
        zp = sb("zp", [P, 3, 432], at=att)
        zA = sb("zA", [P, 2, 432], at=att)
        att.close()
        rw = ExitStack()
        rA = sb("rA", [P, 8, 512], at=rw)
        rN0 = sb("rN0", [P, 8, P], at=rw)
        rG = sb("rG", [P, 8, P], at=rw)
        rI = sb("rI", [P, 8, P], at=rw)
        rN = sb("rN", [P, 2, 8, P], at=rw)
        rX = sb("rX", [P, 8, P], at=rw)
        rWA = sb("rWA", [P, 8, P], at=rw)
        rUM = rX
        tok = sb("tok", [P, 3, 512], at=rw)
        phi = sb("phi", [P, 2, 4, 64], at=rw)
        psi = sb("psi", [P, 2, 4, 64], at=rw)
        rR = sb("rR", [P, 4, P], at=rw)
        rw.close()
        mx.close()

        def V(name, i=0):
            return vec[:, VEC[name] + i:VEC[name] + i + 1]

        def C(name, n=P, rows=P):
            at = CST[name]
            return cst[0:rows, at:at + n] if at < CST1 else cst1[0:rows, at - CST1:at - CST1 + n]

        def mid(ap, n):
            return ap.unsqueeze(1).broadcast_to([ap.shape[0], n, ap.shape[-1]])

        def end(ap, n):
            return ap.unsqueeze(2).broadcast_to([ap.shape[0], ap.shape[1], n])

        def in_order(eng, own):
            n = {}

            def step(ins, sem=own):
                key = next((e for e, names in ONCE.items() if sem in names), sem)
                n[key] = n.get(key, 0) + 1
                assert key == sem or once(sem)[1] == n[key], sem
                ins.then_inc(S(sem), 1)
                eng.wait_ge(S(sem), n[key])
            return step, n

        block = ctx.enter_context(nc.Block())

        @block.sync
        def _(sp):
            sp.dma_start(xT[:], x_d).then_inc(S("x_in"), 16)
            sp.dma_start(vec[:], vec_d).then_inc(S("early_in"), 16)
            sp.dma_start(cst[:, 0:2 * P], cst_d[:, 0:2 * P]).then_inc(S("early_in"), 16)
            for s in range(SLOTS):
                sp.dma_start(ring[:, s, :], stream[s]).then_inc(S(f"w_ready{s}"), 16)
            sp.dma_start(row[:], row_d.broadcast_to([P, NROW])).then_inc(S("consts_in"), 16)
            sp.dma_start(cst[:, 2 * P:], cst_d[:, 2 * P:CST1]).then_inc(S("consts_in"), 16)
            sp.dma_start(cst1[:], cst_d[:, CST1:NCST]).then_inc(S("consts_in"), 16)
            sp.dma_start(mat[:], mat_d).then_inc(S("consts_in"), 16)
            rounds = N_UNITS // SLOTS
            with sp.Fori(1, rounds) as it:
                for s in range(SLOTS):
                    sp.wait_ge(S("w_split"), it * SLOTS + (s + 1 - SLOTS))
                    sp.dma_start(ring[:, s, :], stream[it * SLOTS + s]).then_inc(S(f"w_ready{s}"), 16)
            for u in range(rounds * SLOTS, N_UNITS):
                sp.wait_ge(S("w_split"), u - SLOTS + 1)
                sp.dma_start(ring[:, u % SLOTS, :], stream[u]).then_inc(S(f"w_ready{u % SLOTS}"), 16)
            sp.wait_ge(S("norm_h"), len(NORMS) * KT)
            sp.dma_start(out_d, hT[:, :, TM:TT]).then_inc(S("out_done"), 16)
            sp.wait_ge(S("out_done"), 16)

        @block.gpsimd
        def _(pool):
            def low(s, u):
                pool.wait_ge(S("w_high"), u + 1)
                nc.gpsimd.tensor_tensor(wlo[:, s, :], ring[:, s, :], whi[:, s, :].bitcast(F32),
                                        ALU.subtract).then_inc(S("w_split"), 1)

            def lows(u0, u1):
                r0, r1 = -(-u0 // SLOTS), u1 // SLOTS
                for u in range(u0, r0 * SLOTS):
                    low(u % SLOTS, u)
                if r1 > r0:
                    with pool.Fori(r0, r1) as it:
                        for s in range(SLOTS):
                            low(s, it * SLOTS + s)
                for u in range(r1 * SLOTS, u1):
                    low(u % SLOTS, u)

            def decays(lev):
                b = (LEVELS + (P,))[lev - 1]
                n = 8 * T // (2 * b)
                cv = fC.rearrange("p (n w) -> p n w", w=2 * b)
                d = dif[:, (lev - 1) % 2, :].rearrange("p (n w) -> p n w", w=2 * b)
                if lev >= 3:
                    pool.wait_ge(S("lev_qk"), 2 * lev - 2)
                if lev < 8:
                    nc.gpsimd.tensor_tensor(d, cv, cv[:, :, b - 1:b].broadcast_to([P, n, 2 * b]), ALU.subtract).then_inc(S("lev_d"), 1)
                else:
                    nc.gpsimd.tensor_tensor(d[:, :, 0:b], cv[:, :, 0:b], cv[:, :, b - 1:b].broadcast_to([P, n, b]),
                                            ALU.subtract).then_inc(S("lev_d"), 1)
                    nc.gpsimd.tensor_copy(d[:, :, b:], cv[:, :, b:]).then_inc(S("lev_d"), 1)

            lows(0, U_H + H_IV + 6)
            pool.wait_ge(*once("q_ready"))
            decays(1)
            lows(U_H + H_IV + 6, U_HO)
            decays(2)
            lows(U_HO, U_HO + SLOTS)
            for lev in range(3, 9):
                decays(lev)
            lows(U_HO + SLOTS, N_UNITS)

        @block.tensor
        def _(pe):
            def mm(out, lhsT, rhs, start=True, stop=True):
                return nc.tensor.matmul(out, lhsT, rhs, start=start, stop=stop, skip_group_check=True)

            def mm3(out, l_high, l_low, r_high, r_low, start, stop):
                mm(out, l_high, r_high, start, False)
                mm(out, l_high, r_low, False, False)
                return mm(out, l_low, r_high, False, stop)

            def weights(u):
                pe.wait_ge(S("w_split"), u + 1)
                return [w[:, u % SLOTS, :].rearrange("p (k n) -> p k n", n=P) for w in (whi, wlo)]

            def bank(g):
                if g >= MM_BANKS:
                    who = OWNER[g - MM_BANKS]
                    pe.wait_ge(S("drained_" + who), drained(who, g - MM_BANKS))
                return g % MM_BANKS

            def feature_tile(u, g, t0, ready):
                (wh, wl), b = weights(u), bank(g)
                for k in range(KT):
                    pe.wait_ge(S(ready[0]), ready[1] + k + 1)
                    m = mm3(ps[:, b, 0:TT - t0], wh[:, k, :], wl[:, k, :], aH[:, k, t0:TT], aL[:, k, t0:TT],
                            k == 0, k == KT - 1)
                m.then_inc(S("w_used"), 1)

            def feature_pair(u, g, t0, ready):
                parts = [weights(u + j) + [bank(g + j)] for j in range(2)]
                for k in range(KT):
                    pe.wait_ge(S(ready[0]), ready[1] + k + 1)
                    for wh, wl, b in parts:
                        m = mm3(ps[:, b, 0:TT - t0], wh[:, k, :], wl[:, k, :], aH[:, k, t0:TT], aL[:, k, t0:TT],
                                k == 0, k == KT - 1)
                        if k == KT - 1:
                            m.then_inc(S("w_used"), 1)

            def token_pair(u, g, ready):
                pe.wait_ge(S("w_split"), u + 2)
                assert u % SLOTS + 1 < SLOTS
                b = bank(g + 1)
                wh, wl = [w[:, u % SLOTS:u % SLOTS + 2, :] for w in (whi, wlo)]
                for tt in range(2):
                    for k in range(KT):
                        pe.wait_ge(S(ready[0]), ready[1] + k + 1)
                        tok, at = slice(TM + tt * P, TM + tt * P + P), slice(k * P, (k + 1) * P)
                        m = mm3(ps[:, b, tt * T:(tt + 1) * T], aH[:, k, tok], aL[:, k, tok],
                                wh[:, :, at], wl[:, :, at], k == 0, k == KT - 1)
                m.then_inc(S("w_used"), 2)

            def norm(tag, n):
                i = NORMS.index(tag)
                if i == 0:
                    pe.wait_ge(S("early_in"), 32)
                pe.wait_ge(S("norm_sum"), (KT - 2) * (i + 1))
                mm(ps[:, 7, 0:n], C("ones"), sq[:, 0, 0:n], True, False)
                pe.wait_ge(S("norm_sq"), KT * (i + 1))
                mm(ps[:, 7, 0:n], C("ones"), sq[:, KT - 1, 0:n], False, True).then_inc(S("norm_ss"), 1)

            def even_in():
                ready = ("norm_h", 0)
                between = {13: queries_ss, 15: queries_rot, 17: doubled, C_AFTER - 1: compress, 23: transposed,
                           24: second_layer, 26: kc_ss, 28: kc_rot, 30: forget_sums, 32: gate_rows}
                feature_pair(U_E, G_E, TM, ready)
                for j in range(2, E_UNITS):
                    if j in (E_VSW, E_V, E_V + 2):
                        token_pair(even_unit(j), G_E + j, ready)
                    elif E_OWNER[j] == "a":
                        feature_tile(even_unit(j), G_E + j, TM, ready)
                    if j in between:
                        between[j]()

            def queries_ss():
                pe.wait_ge(S("consts_in"), 64)
                pe.wait_ge(*once("nqk_sq"))
                for j, b in enumerate((4, 5, 7)):
                    m = mm(ps[:, b, :], C("blk"), rs[:, 2 * j:2 * j + 2, :].rearrange("p a b -> p (a b)"))
                m.then_inc(S("nqk_ss"), 1)

            def queries_rot():
                pe.wait_ge(S("nqk_n"), 6)
                for j, b in enumerate((4, 5, 7)):
                    m = mm(ps[:, b, :], C("rot"), nqk[:, 2 * j:2 * j + 2, :].rearrange("p a b -> p (a b)"))
                m.then_inc(S("nqk_rot"), 1)

            def doubled():
                pe.wait_ge(S("rope_done"), 3)
                for kind in range(2):
                    for g in range(2):
                        m = mm(ps[:, 4 + kind, g * T:(g + 1) * T], C(f"dup{g}"), kcvc[:, kind, :])
                m.then_inc(S("dup_done"), 1)

            def compress():
                pe.wait_ge(S("xc_ready"), 10)
                for kind in range(2):
                    for half in range(2):
                        wh, wl = weights(U_C + 2 * kind + half)
                        for j in range(8):
                            at = 8 * half + j
                            m = mm3(ps[0:2 * NCMP, 6, kind * P:(kind + 1) * P], xcH[:, kind, at, :], xcL[:, kind, at, :],
                                    wh[:, j, :], wl[:, j, :], at == 0, at == 15)
                        m.then_inc(S("w_used"), 1)

            def transposed():
                pe.wait_ge(S("drained_a"), drained("a", G_E + E_SMALL))
                for tt in range(2):
                    m = nc.tensor.transpose(ps[:, 5, tt * 32:tt * 32 + 32], smallT[0:32, tt * P:(tt + 1) * P], C("ident")[0:32, 0:32])
                m.then_inc(S("small_t"), 1)
                pe.wait_ge(*once("gelu_ready"))
                for kind in range(2):
                    m = nc.tensor.transpose(ps[:, 6, 320 + 32 * kind:320 + 32 * kind + 2 * NCMP],
                                            hx[:, 0, kind * P:(kind + 1) * P], C("ident")[0:2 * NCMP, 0:2 * NCMP])
                m.then_inc(S("hx_t"), 1)

            def second_layer():
                pe.wait_ge(*once("hx_f"))
                for g in range(2):
                    mm(ps[64 * g:64 * g + 64, 6, 64:64 + NCMP], mat[:, MAT["w2k"]:MAT["w2k"] + 64], hf[:, 0, g * NCMP:(g + 1) * NCMP])
                    m = mm(ps[0:NCMP, 6, 128 + 64 * g:192 + 64 * g], hf[:, 1, g * NCMP:(g + 1) * NCMP],
                           mat[:, MAT["w2v"]:MAT["w2v"] + 64])
                m.then_inc(S("w2_done"), 1)

            def kc_ss():
                pe.wait_ge(*once("kc_sq"))
                mm(ps[:, 6, 256:256 + NCMP], C("blk"), kct[:, 1, :]).then_inc(S("kc_ss"), 1)

            def kc_rot():
                pe.wait_ge(*once("kc_n"))
                mm(ps[:, 6, 288:288 + NCMP], C("rot"), kct[:, 2, :]).then_inc(S("kc_rot"), 1)

            def forget_sums():
                pe.wait_ge(*once("logf"))
                mm(ps[:, 4, 0:4], C("le"), gl[:, 3, 0:4])
                mm(ps[:, 4, 4:8], C("le"), gl[:, 3, 4:8], True, False)
                mm(ps[:, 4, 4:8], C("ones"), gl[:, 3, 0:4], False, True).then_inc(S("bcum"), 1)

            def gate_rows():
                pe.wait_ge(S("gate_cols"), 2)
                for what in range(2):
                    for tt in range(2):
                        m = nc.tensor.transpose(ps[0:4, 4, what * T + tt * P:what * T + tt * P + P],
                                                gl[:, 4 + what, tt * 4:tt * 4 + 4], C("ident"))
                m.then_inc(S("gate_rows"), 1)

            def mlstm():
                pe.wait_ge(S("row_max"), 3)
                pe.wait_ge(S("qk_ready"), 2)
                pe.wait_ge(*once("kc_ready"))
                pe.wait_ge(S("drained_a"), drained("a", G_EO - 1))

                def front(h):
                    b = 4 * (h % 2)
                    if h >= 2:
                        pe.wait_ge(S("mlstm_st"), h - 1)
                    one = C("pick", 512, 4)[:, h * P:(h + 1) * P]
                    mm(ps[:, b + 1, 0:T], one, rows4[:, 2, :], True, False)
                    mm(ps[:, b + 1, 0:P], ident_bf[:], before_bf[:], False, True)
                    mm(ps[:, b + 1, T:T + P], one, rows4[:, 2, P:T], True, False)
                    mm(ps[:, b + 1, T:T + P], ident_bf[:], before_bf[:], False, True)
                    mm(ps[:, b, 0:T], one, rows4[:, 3, :])
                    mm(ps[:, b + 2, 0:T], qk[:, 4 + h, 0:P], qk[:, h, :])
                    mm(ps[:, b + 2, T:T + P], qk[:, 4 + h, P:T], qk[:, h, P:T]).then_inc(S("mlstm_s"), 1)

                def back(h):
                    b = 4 * (h % 2)
                    pe.wait_ge(S("mlstm_st"), h + 1)
                    if h >= 2:
                        pe.wait_ge(S("mlstm_h"), h - 1)
                    st = mST[:, h % 2, :]
                    for out, l0, l1 in ((0, vtok[:, 0, h * P:(h + 1) * P], vtok[:, 1, h * P:(h + 1) * P]),
                                        (T, C("ones"), C("ones"))):
                        mm(ps[:, b + 3, out:out + T], l0, st[:, 0:T], True, False)
                        m = mm(ps[:, b + 3, out + P:out + T], l1, st[:, T:T + P], False, True)
                    m.then_inc(S("mlstm_o"), 1)

                for h in range(5):
                    if h < 4:
                        front(h)
                    if h >= 1:
                        back(h - 1)

            def attention():
                pe.wait_ge(S("rope_done"), 4)
                pe.wait_ge(S("mlstm_h"), 4)
                for qt in range(2):
                    for h in range(8):
                        i, g = h % 4, h // 4
                        m = mm(ps[:, 6 + g, (qt * 4 + i) * NCMP:(qt * 4 + i + 1) * NCMP],
                               nqk[64 * g:64 * g + 64, i, qt * P:(qt + 1) * P], kct[64 * g:64 * g + 64, 3, :])
                m.then_inc(S("cmp_s"), 1)

                def scores(n):
                    qt, g = n // 2, n % 2
                    nk = P * (qt + 1)
                    for i in range(4):
                        if n >= 1:
                            pe.wait_ge(S("att_exp"), 8 * (n - 1) + 2 * i + 2)
                        q = nqk[64 * g:64 * g + 64, i, qt * P:(qt + 1) * P]
                        for kind in range(2):
                            o = kind * T
                            mm(ps[:, i, o:o + nk], q, nqk[64 * g:64 * g + 64, 4 + kind, 0:nk], True, False)
                            m = mm(ps[:, i, o + nk - P:o + nk], ident_bf[:], later_bf[:], False, True)
                        m.then_inc(S("att_s"), 1)

                turn = [0]

                def outputs(n):
                    qt, g = n // 2, n % 2
                    pe.wait_ge(S("att_p"), 8 * n + 8)
                    pe.wait_ge(*once("cmp_p"))
                    parts = [(None, 0)] + [(kind, st) for kind in range(2) for st in range(qt + 1)]
                    if n >= 2:
                        pe.wait_ge(S("att_o"), n - 1)
                    first = turn[0]
                    turn[0] += len(parts)
                    for j in range(len(parts) + 1):
                        if j < len(parts):
                            (kind, st), t = parts[j], first + j
                            if t >= 2:
                                pe.wait_ge(S("att_pt"), t - 1)
                            for i in range(4):
                                if kind is None:
                                    m = nc.tensor.transpose(ps[0:NCMP, 4 + t % 2, i * P:(i + 1) * P],
                                                            pc[:, qt * 8 + 4 * g + i, :], C("ident"))
                                else:
                                    m = nc.tensor.transpose(ps[:, 4 + t % 2, i * P:(i + 1) * P],
                                                            prob[:, n % 2, i, kind * T + st * P:kind * T + (st + 1) * P], C("ident"))
                            m.then_inc(S("att_tr"), 1)
                        if j >= 1:
                            (kind, st), t = parts[j - 1], first + j - 1
                            pe.wait_ge(S("att_pt"), t + 1)
                            out = ps[64 * g:64 * g + 64, 6 + n % 2, :]
                            if kind is None:
                                m = mm(out, vct[:, 64 * g:64 * g + 64], pt[0:NCMP, t % 2, :], True, False)
                            else:
                                m = mm(out, vsw[:, kind, st, 64 * g:64 * g + 64], pt[:, t % 2, :], False, j == len(parts))
                    m.then_inc(S("att_av"), 1)

                for n in range(5):
                    if n < 4:
                        scores(n)
                    if n == 0:
                        pe.wait_ge(*once("mh_sq"))
                        for j in range(2):
                            m = mm(ps[:, 4 + j, :], C("ones"), rs[:, 2 * j:2 * j + 2, :].rearrange("p a b -> p (a b)"))
                        m.then_inc(S("mh_ss"), 1)
                    if n == 1:
                        pe.wait_ge(*once("mh_rs"))
                    if n >= 1:
                        outputs(n - 1)

            def project(u0, g0, nth, t0):
                feature_pair(u0, g0, t0, ("mix_split", nth * KT))
                for m in range(2, KT):
                    feature_tile(u0 + m, g0 + m, t0, ("mix_split", nth * KT))

            def hgrn_in():
                ready = ("norm_h", KT)
                feature_pair(U_H, G_H, TM, ready)
                for j in range(2, H_UNITS):
                    if H_OWNER[j] == "a":
                        feature_tile(U_H + j, G_H + j, TM, ready)
                    elif (j - H_IV) % 2 == 0:
                        token_pair(U_H + j, G_H + j, ready)

            def hgrn():
                for lev in range(9):
                    q = qkl[:, lev % 2, :].rearrange("p (h t w) -> p h t w", h=8, t=2)
                    pe.wait_ge(S("lev_qk"), 2 * lev + 2)
                    if lev < 8:
                        b0 = 4 * ((lev + 1) % 2)
                        if lev == 1:
                            pe.wait_ge(S("drained_a"), drained("a", G_HO - 1))
                            pe.wait_ge(S("drained_v"), drained("v", G_HO - 1))
                        if lev >= 2:
                            pe.wait_ge(S("lev_a"), 4 * (lev - 1))
                        for j in range(16):
                            h, tt = j // 2, j % 2
                            key = q[:, h, tt, :] if lev else fK[:, h, tt * P:(tt + 1) * P]
                            query = q[:, h, tt, :] if lev else fQ[:, h, tt * P:(tt + 1) * P]
                            m = mm(ps[:, b0 + j // 4, (j % 4) * P:(j % 4 + 1) * P], key, query)
                            if j % 4 == 3:
                                m.then_inc(S("lev_s"), 1)
                    else:
                        pe.wait_ge(S("lev_a"), 4 * 7)
                        for h in range(8):
                            m = mm(ps[:, 4 + h // 4, (h % 4) * P:(h % 4 + 1) * P], q[:, h, 0, :], q[:, h, 1, :])
                            if h % 4 == 3:
                                m.then_inc(S("lev_s"), 1)
                pe.wait_ge(S("lev_a"), 4 * 8 + 2)
                for h in range(8):
                    o = ps[:, 4 + h // 2, (h % 2) * T:(h % 2 + 1) * T]
                    v0, v1 = [ivt[:, tt, h * P:(h + 1) * P] for tt in range(2)]
                    mm(o[:, 0:P], v0, hA[:, h, 0, :])
                    mm(o[:, P:T], v0, hX[:, h, :], True, False)
                    m = mm(o[:, P:T], v1, hA[:, h, 1, :], False, True)
                    if h == 3:
                        m.then_inc(S("hg_o"), 1)
                m.then_inc(S("hg_o2"), 1)
                for j in range(4):
                    if j % 2 == 0:
                        pe.wait_ge(*once(("hg_sq", "hg_sq2")[j // 2]))
                    m = mm(ps[:, j, :], C("ones"), dif[:, 0, j * 512:(j + 1) * 512])
                    if j == 1:
                        m.then_inc(S("hg_ss"), 1)
                m.then_inc(S("hg_ss2"), 1)

            def ffn(tag, u0, g0, first):
                d0 = drained("v", g0 - 1)

                def gate_up(it, f4):
                    for j in range(2 * f4, 2 * f4 + 2):
                        pe.wait_ge(S("w_split"), it * 8 + (u0 + j + 1))
                        pe.wait_ge(S("drained_v"), it * 8 + (d0 + j - 3))
                        s = (u0 + j) % SLOTS
                        for k in range(KT):
                            at = slice(k * P, (k + 1) * P)
                            m = mm3(ps[:, (g0 + j) % MM_BANKS, 0:TT], whi[:, s, at], wlo[:, s, at], aH[:, k, :], aL[:, k, :],
                                    k == 0, k == KT - 1)
                        m.then_inc(S("w_used"), 1)

                feature_pair(u0, g0, 0, ("norm_h", NORMS.index(tag) * KT))
                for f4 in range(1, 4):
                    gate_up(0, f4)
                with pe.Fori(1, FT // 4) as it:
                    for f4 in range(4):
                        gate_up(it, f4)
                for f4 in range(FT % 4):
                    gate_up(FT // 4, f4)
                for m in range(KT):
                    b = bank(g0 + GU_UNITS + m)
                    for k in range(FT):
                        n = m * FT + k
                        u = u0 + GU_UNITS + n // KT
                        if n % KT == 0:
                            wh, wl = weights(u)
                        if m == 0:
                            pe.wait_ge(S("ffn_split"), first + k + 1)
                        last = mm3(ps[:, b, 0:TT], wh[:, n % KT, :], wl[:, n % KT, :], fH[:, k, :], fL[:, k, :],
                                   k == 0, k == FT - 1)
                        if n % KT == KT - 1:
                            last.then_inc(S("w_used"), 1)

            def mixer_in():
                feature_pair(U_P, G_P, 0, ("norm_h", 3 * KT))
                for j in range(2, P_UNITS):
                    feature_tile(U_P + j, G_P + j, 0, ("norm_h", 3 * KT))
                    if j == 15:
                        pe.wait_ge(S("drained_a"), drained("a", G_P + 11))
                        pe.wait_ge(S("sb_pad"), 2)
                        for tt in range(3):
                            for jj in range(4):
                                m = nc.tensor.transpose(ps[:, 4 + tt, jj * P:(jj + 1) * P], sbv[:, jj, tt * P:(tt + 1) * P], C("ident"))
                        m.then_inc(S("sb_vt"), 1)

            def decays():
                pe.wait_ge(*once("lora_th"))
                pe.wait_ge(*once("sb_v"))
                low = pr[:, 12, 1:1 + TT]
                for j in range(4):
                    mm(ps[:, j, 0:TT], mat[0:32, MAT["wup"] + j * P:MAT["wup"] + (j + 1) * P], low[0:32])
                    m = mm(ps[:, 4 + j, 0:TT], mat[32:64, MAT["wup"] + j * P:MAT["wup"] + (j + 1) * P], low[32:64])
                m.then_inc(S("lora_up"), 1)

            def sticks():
                pe.wait_ge(*once("a_th"))
                for h in range(11):
                    if h < 8:
                        a, j, b = 64 * (h % 2), h // 2, h % 2
                        if h >= 2:
                            pe.wait_ge(S("sb_ln"), h - 1)
                        mm(ps[:, b, 0:272], sbk[a:a + 64, j, 0:P], sbq[a:a + 64, j, :])
                        mm(ps[:, b, 272:416], sbk[a:a + 64, j, P:2 * P], sbq[a:a + 64, j, P:TT])
                        mm(ps[:, b, 416:432], sbk[a:a + 64, j, 2 * P:3 * P], sbq[a:a + 64, j, 2 * P:TT]).then_inc(S("sb_z"), 1)
                    if h == 0:
                        pe.wait_ge(*once("kk_sq"))
                        for j in range(2):
                            m = mm(ps[:, 2 + j, 0:TT], C("blk"), pT[:, j, :])
                        m.then_inc(S("kk_ss"), 1)
                    if h == 1:
                        pe.wait_ge(*once("kk_n2"))
                        for j in range(2):
                            m = mm(ps[:, 2 + j, 0:TT], C("blk"), pT[:, 2 + j, :])
                        m.then_inc(S("kk_ss2"), 1)
                    if 2 <= h <= 9:
                        r, o = h - 2, ps[:, 4 + h % 2, :]
                        pe.wait_ge(S("sb_sp"), r + 1)
                        if r >= 2:
                            pe.wait_ge(S("sb_arg"), r - 1)
                        s = zp[:, r % 3, :]
                        mm(o[:, 0:272], C("ge"), s[:, 0:272], True, False)
                        mm(o[:, 128:272], C("ones"), s[:, 272:416], False, False)
                        mm(o[:, 256:272], C("ones"), s[:, 416:432], False, False)
                        mm(o[:, 0:128], ident_bf[:], notyet_bf[:], False, True)
                        mm(o[:, 272:416], C("ge"), s[:, 272:416], True, False)
                        mm(o[:, 400:416], C("ones"), s[:, 416:432], False, False)
                        mm(o[:, 272:400], ident_bf[:], notyet_bf[:], False, True)
                        mm(o[:, 416:432], C("ge"), s[:, 416:432], True, False)
                        mm(o[:, 416:432], ident_bf[:], notyet_bf[:, 0:16], False, True).then_inc(S("sb_rest"), 1)
                    if h >= 3:
                        r = h - 3
                        a, o, A = 64 * (r % 2), ps[64 * (r % 2):64 * (r % 2) + 64, 6 + r % 2, :], zA[:, r % 2, :]
                        pe.wait_ge(S("sb_A"), r + 1)
                        if r >= 2:
                            pe.wait_ge(S("sb_out"), r - 1)
                        mm(o[:, 0:272], sbvt[:, 0, r * 64:r * 64 + 64], A[:, 0:272], True, False)
                        mm(o[:, 128:272], sbvt[:, 1, r * 64:r * 64 + 64], A[:, 272:416], False, False)
                        mm(o[:, 256:272], sbvt[:, 2, r * 64:r * 64 + 64], A[:, 416:432], False, True).then_inc(S("sb_av"), 1)

            def rwkv():
                pe.wait_ge(S("bk_ready"), 2)
                pe.wait_ge(S("sb_out"), 8)
                nth = [0]
                for tau, (t0, n) in enumerate(TILES2):
                    ar = lambda h: AR[64 * (h % 2):64 * (h % 2) + 64, h // 2, :, t0:t0 + n]
                    bk = lambda h, w: BK[64 * (h % 2):64 * (h % 2) + 64, h // 2, w, t0:t0 + n]
                    if tau:
                        pe.wait_ge(S("y_done"), tau)
                    for h in range(8):
                        m = mm(ps[0:n, 6 + h % 2, (h // 2) * n:(h // 2 + 1) * n], ar(h)[:, 0, :], bk(h, 0))
                    m.then_inc(S("r_ab"), 1)
                    for h in range(8):
                        b = h % 6
                        if h >= 6:
                            pe.wait_ge(S("r_mask"), 8 * tau + h - 5)
                        o = ps[0:n, b, 0:4 * n].rearrange("p (k w t) -> p k w t", k=2, w=2)
                        mm(o[:, 0], bk(h, 0), ar(h))
                        mm(o[:, 1], bk(h, 1), ar(h)).then_inc(S("r_mats"), 1)
                    for w in range(4):
                        b = 2 + w
                        pe.wait_ge(S("r_mask"), 8 * tau + b + 1)
                        for j in range(4):
                            src = (AR[:, j, 0, t0:t0 + n], BK[:, j, 0, t0:t0 + n], BK[:, j, 1, t0:t0 + n],
                                   pr[:, 8 + j, 1 + t0:1 + t0 + n])[w]
                            m = nc.tensor.transpose(ps[0:n, b, j * P:(j + 1) * P], src, C("ident"))
                        m.then_inc(S("r_tok"), 1)
                    pe.wait_ge(S("r_tokc"), 4 * tau + 4)
                    pe.wait_ge(S("r_mask"), 8 * tau + 8)
                    for h in range(8):
                        q = (h % 2) * 4 + h // 2
                        m = mm(ps[0:n, 6, h * 64:h * 64 + 64], rA[0:n, q, 2 * n:3 * n], tok[0:n, 2, h * 64:h * 64 + 64])
                    m.then_inc(S("r_w"), 1)
                    levels = [b for b in LEVELS[1:6] if b < n]
                    for lev in levels:
                        i = nth[0]
                        nth[0] += 2
                        for half in range(2):
                            pe.wait_ge(S("r_n"), i // 2 + 1)
                            if lev != levels[0]:
                                pe.wait_ge(S("r_g"), 2 * (i + half) - 3)
                            for k in range(4):
                                q = 4 * half + k
                                m = mm(ps[0:n, half, k * n:(k + 1) * n], rN[0:n, i // 2 % 2, q, 0:n], rG[0:n, q, 0:n])
                            m.then_inc(S("r_x"), 1)
                        for half in range(2):
                            pe.wait_ge(S("r_xc"), i + half + 1)
                            if lev != levels[0]:
                                pe.wait_ge(S("r_g"), 2 * (i + half) - 2)
                            for k in range(4):
                                q = 4 * half + k
                                m = mm(ps[0:n, 2 + half, k * n:(k + 1) * n], rI[0:n, q, 0:n], rX[0:n, q, 0:n])
                            if lev != levels[-1]:
                                for k in range(4):
                                    q = 4 * half + k
                                    m = mm(ps[0:n, 4 + half, k * n:(k + 1) * n], rX[0:n, q, 0:n], rI[0:n, q, 0:n])
                            m.then_inc(S("r_d"), 1)
                    pe.wait_ge(S("r_wc"), tau + 1)
                    pe.wait_ge(S("r_g"), 2 * nth[0])
                    for h in range(8):
                        q = (h % 2) * 4 + h // 2
                        m = mm(ps[0:n, h // 4, (h % 4) * P:(h % 4 + 1) * P], rG[0:n, q, 0:n], rWA[0:n, h, :])
                    m.then_inc(S("r_u"), 1)
                    pe.wait_ge(S("r_uc"), tau + 1)
                    for h in range(8):
                        q, a = (h % 2) * 4 + h // 2, 64 * (h % 2)
                        col = slice((h // 2) * n, (h // 2 + 1) * n)
                        mm(ps[a:a + 64, 2, col], rUM[0:n, h, 64:128], rA[0:n, q, n:2 * n])
                        mm(ps[a:a + 64, 3, col], rUM[0:n, h, 0:64], rA[0:n, q, n:2 * n], True, False)
                        m = mm(ps[a:a + 64, 3, col], tok[0:n, 2, h * 64:h * 64 + 64], rA[0:n, q, 3 * n:4 * n], False, True)
                    m.then_inc(S("r_y0"), 1)
                    chunks = [c for c, (s, _) in enumerate(RW_CHUNKS) if t0 <= s < t0 + n]
                    if tau < 2:
                        for c in chunks:
                            rows = slice(64 * (c % 2), 64 * (c % 2) + 64)
                            for h in range(8):
                                a, hh = 64 * (h % 2), slice(h * 64, h * 64 + 64)
                                o = slice((h // 2) * 64, (h // 2 + 1) * 64)
                                mm(ps[a:a + 64, 4 + c % 2, o], rUM[rows, h, 64:128], tok[rows, 0, hh])
                                o = slice(256 + (h // 2) * 64, 256 + (h // 2 + 1) * 64)
                                mm(ps[a:a + 64, 4 + c % 2, o], tok[rows, 0, hh], rUM[rows, h, 0:64], True, False)
                                m = mm(ps[a:a + 64, 4 + c % 2, o], tok[rows, 1, hh], tok[rows, 2, hh], False, True)
                            m.then_inc(S("r_phi"), 1)
                    for c in chunks:
                        cols = RW_CHUNKS[c]
                        if c >= 1:
                            pe.wait_ge(S("r_state"), c)
                            pe.wait_ge(S("r_r"), tau + 1)
                            for h in range(8):
                                a = 64 * (h % 2)
                                o = (h // 2) * n + cols[0] - t0
                                m = mm(ps[a:a + 64, 6 + h % 2, o:o + cols[1]], state[a:a + 64, c % 2, h // 2, :],
                                       rR[a:a + 64, h // 2, cols[0] - t0:cols[0] - t0 + cols[1]])
                            m.then_inc(S("r_ys"), 1)
                            if c < 4:
                                pe.wait_ge(S("r_phic"), c + 1)
                                for h in range(8):
                                    a = 64 * (h % 2)
                                    m = mm(ps[a:a + 64, h % 2, (h // 2) * 64:(h // 2 + 1) * 64],
                                           phi[a:a + 64, c % 2, h // 2, :], state[a:a + 64, c % 2, h // 2, :])
                                m.then_inc(S("r_s"), 1)
                pe.wait_ge(S("y_done"), 3)
                for j in range(4):
                    m = mm(ps[:, j, 0:TT], C("blk"), yT[:, j, :])
                m.then_inc(S("gn_mean"), 1)
                pe.wait_ge(*once("bonus_in"))
                for j in range(4):
                    m = mm(ps[:, 4 + j, 0:TT], C("blk"), pK[:, j, :])
                m.then_inc(S("bonus"), 1)
                pe.wait_ge(*once("gn_sq"))
                for j in range(4):
                    m = mm(ps[:, j, 0:TT], C("blk"), pT[:, j, :])
                m.then_inc(S("gn_var"), 1)
                pe.wait_ge(*once("bonus_out"))
                for j in range(4):
                    m = mm(ps[:, 4 + j, 0:TT], mat[:, MAT["gup"] + j * P:MAT["gup"] + (j + 1) * P], pr[:, 13, 1:1 + TT])
                m.then_inc(S("g_out"), 1)
                pe.wait_ge(*once("gn_rs"))

            norm("norm0", T)
            even_in()
            mlstm()
            attention()
            project(U_EO, G_EO, 0, TM)
            norm("norm1", T)
            hgrn_in()
            hgrn()
            project(U_HO, G_HO, 1, TM)
            norm("ffn1", TT)
            ffn("ffn1", U_F1, G_F1, 0)
            norm("mix", TT)
            mixer_in()
            decays()
            sticks()
            rwkv()
            project(U_PO, G_PO, 2, 0)
            norm("ffn2", TT)
            ffn("ffn2", U_F2, G_F2, FT)
            norm("final", TT)

        @block.scalar
        def _(act):
            step, act_n = in_order(act, "act_step")

            def func(out, in_, f, sem="act_step", **kw):
                step(nc.scalar.activation(out, in_, f, **kw), sem)

            LOG_EXP = "natural_log_exp_and_others"

            def square(tag, k, c0, n):
                if tag != "norm0":
                    act.wait_ge(S(before_norm[tag][0]), before_norm[tag][1] + k + 1)
                func(sq[:, k, 0:n], xT[:, k, c0:c0 + n], ACT.Square, "norm_sq")

            def norm(tag, n):
                act.wait_ge(S("norm_ss"), NORMS.index(tag) + 1)
                func(rstd[:, 0:n], ps[:, 7, 0:n], ACT.Ln, scale=1.0 / D, bias=eps[:, 0:1])
                func(rstd[:, 0:n], rstd[:, 0:n], ACT.Exp, "norm_rstd", scale=-0.5)
                if tag != "final":
                    for k in range(KT):
                        act.wait_ge(S("norm_x"), NORMS.index(tag) * KT + k + 1)
                        func(aH[:, k, TT - n:TT], hT[:, k, TT - n:TT], ACT.Copy, "norm_hi")

            def mix_high(ready, seen, tiles, c0):
                for i, k in enumerate(tiles):
                    act.wait_ge(S(ready), seen + i + 1)
                    func(aH[:, k, c0:TT], mixT[:, k, c0:TT], ACT.Copy, "mix_hi")

            def norm0():
                nc.scalar.preload_act_table_set(LOG_EXP)
                act.wait_ge(S("x_in"), 16)
                for k in range(KT):
                    square("norm0", k, TM, T)
                for u in range(2):
                    high(u)
                act.wait_ge(S("setup"), 4)
                act.wait_ge(S("early_in"), 32)
                norm("norm0", T)
                for u in range(2, SLOTS):
                    high(u)

            def squares_behind(tag, u0, n_units, g0, c0, n):
                nc.scalar.preload_act_table_set(LOG_EXP)
                k = 0
                for u in range(u0, u0 + n_units):
                    ahead(u)
                    while k < KT and used_by(g0 + k) <= u:
                        square(tag, k, c0, n)
                        k += 1
                for k in range(k, KT):
                    square(tag, k, c0, n)
                norm(tag, n)

            def ahead(u, it=0):
                if u + SLOTS >= N_UNITS:
                    return
                v = u + SLOTS
                act.wait_ge(S("w_used"), it * 8 + (u + 1))
                high(v, it)

            def high(v, it=0):
                act.wait_ge(S(f"w_ready{v % SLOTS}"), it * (8 // SLOTS * 16) + 16 * (v // SLOTS + 1))
                nc.scalar.activation(whi[:, v % SLOTS, :], ring[:, v % SLOTS, :], ACT.Copy).then_inc(S("w_high"), 1)

            def ahead_of(u0, n):
                for u in range(u0, u0 + n):
                    ahead(u)

            before_norm = {"norm1": ("drained_v", drained("v", G_EO - 1)), "ffn1": ("drained_v", drained("v", G_HO - 1)),
                           "mix": ("drained_v", drained("v", G_F1 + GU_UNITS - 1)), "ffn2": ("drained_v", drained("v", G_PO - 1)),
                           "final": ("drained_v", drained("v", G_F2 + GU_UNITS - 1))}

            def drain(g, out, width=T, bias=None, rows=P):
                act.wait_ge(S("w_used"), used_by(g))
                kw = {"bias": bias} if bias is not None else {}
                func(out, ps[0:rows, g % MM_BANKS, 0:width], ACT.Identity, "drained_a", **kw)

            def even_in():
                dst = {E_KC: kcvc[:, 0, :], E_KC + 1: kcvc[:, 1, :], E_SMALL: smallT[:]}
                for j in range(6):
                    dst[E_NQK + j] = nqk[:, j, :]
                for j in range(8):
                    dst[E_QK + j] = qkpre[:, j, 3:3 + T]
                    dst[E_OZ + j] = oz[:, j, :]
                for j in range(4):
                    dst[E_NZ + j] = nz[:, j, :]
                between = {7: queries_sq, 13: queries_rs, C_AFTER - 1: hidden, 23: by_feature, 24: second_layer,
                           26: kc_rs, 28: forget_log, 31: silu}
                for j in range(E_UNITS):
                    if E_OWNER[j] == "a":
                        drain(G_E + j, dst[j], bias=V("ev_b", j))
                    ahead(even_unit(j))
                    if j in between:
                        between[j]()

            def queries_sq():
                func(rs[:], nqk[:], ACT.Square, "nqk_sq")

            def queries_rs():
                act.wait_ge(*once("nqk_ss"))
                for j, b in enumerate((4, 5, 7)):
                    func(rs[:, 2 * j:2 * j + 2, :], ps[:, b, :].rearrange("p (a b) -> p a b", a=2), ACT.Ln, scale=1.0 / 64, bias=eps[:, 0:1])
                func(rs[:], rs[:], ACT.Exp, "nqk_rs", scale=-0.5)

            def hidden():
                ahead_of(U_C, C_UNITS)
                act.wait_ge(*once("hx_x"))
                func(hx[:, 1, :], hx[:, 0, :], ACT.Square, "hx_sq")
                act.wait_ge(*once("hx_arg"))
                func(hx[:, 2, :], hx[:, 1, :], ACT.Tanh, "hx_th", scale=0.7978845608028654)

            def by_feature():
                act.wait_ge(*once("hx_t"))
                func(hf[:, :, 0:2 * NCMP], ps[:, 6, 320:384].rearrange("p (k n) -> p k n", k=2)[:, :, 0:2 * NCMP], ACT.Copy, "hx_f")

            def second_layer():
                act.wait_ge(*once("w2_done"))
                func(vct[:], ps[0:NCMP, 6, 128:256], ACT.Copy)
                func(kct[:, 0, :], ps[:, 6, 64:64 + NCMP], ACT.Copy)
                func(kct[:, 1, :], kct[:, 0, :], ACT.Square, "kc_sq")

            def kc_rs():
                act.wait_ge(*once("kc_ss"))
                func(kct[:, 3, :], ps[:, 6, 256:256 + NCMP], ACT.Ln, scale=1.0 / 64, bias=eps[:, 0:1])
                func(kct[:, 3, :], kct[:, 3, :], ACT.Exp, "kc_rs", scale=-0.5)

            def forget_log():
                act.wait_ge(S("fgate"), 2)
                func(gl[:, 1, :], gl[:, 0, :], ACT.Abs)
                func(gl[:, 1, :], gl[:, 1, :], ACT.Exp, scale=-1.0)
                func(gl[:, 2, :], gl[:, 1, :], ACT.Ln, "log1p", bias=eps[:, 2:3])

            def silu():
                func(small[:, :, 8:32], small[:, :, 8:32], ACT.Tanh, "gates_th", scale=0.5)
                act.wait_ge(S("conv"), 8)
                func(th[:], qk[:], ACT.Tanh, "qk_th", scale=0.5)

            def mlstm():
                func(rs[:, 0:4, :], nz[:], ACT.Tanh, "nz_th", scale=0.5)
                act.wait_ge(S("qk_ready"), 2)
                func(th[:], oz[:], ACT.Tanh, "oz_th", scale=0.5)
                nc.scalar.preload_act_table_set(LOG_EXP)
                for h in range(5):
                    if h < 4:
                        b = 4 * (h % 2)
                        act.wait_ge(S("mlstm_s"), h + 1)
                        if h >= 2:
                            act.wait_ge(S("mlstm_st"), h - 1)
                        func(mem[:, h, :], ps[:, b, 0:T], ACT.Exp, scale=-1.0)
                        func(mE[:, h % 2, 0:T], ps[:, b + 1, 0:T], ACT.Exp, scale=-1.0, bias=gl[:, 5, h:h + 1])
                        func(mE[:, h % 2, T:T + P], ps[:, b + 1, T:T + P], ACT.Exp, "mlstm_e", scale=-1.0,
                             bias=gl[:, 5, 4 + h:5 + h])
                    if h >= 1:
                        act.wait_ge(S("mlstm_o"), h)
                        func(mad[:, h - 1, :], ps[:, 4 * ((h - 1) % 2) + 3, T:2 * T], ACT.Abs, "mlstm_d")
                act.wait_ge(S("mlstm_h"), 4)
                func(rs[:, 0:4, :], hm[:], ACT.Square, "mh_sq")

            def heads():
                act.wait_ge(*once("mh_ss"))
                r = rs[:, 0:4, :].rearrange("p a b -> p (a b)").rearrange("p (a b) -> p a b", b=512)
                func(r, ps[:, 4:6, :], ACT.Ln, scale=1.0 / P, bias=eps[:, 0:1])
                func(rs[:, 0:4, :], rs[:, 0:4, :], ACT.Exp, "mh_rs", scale=-0.5)

            def attention():
                act.wait_ge(*once("cmp_sub"))
                func(pc[:], pc[:], ACT.Exp, "cmp_e")
                turn = [0]
                for n in range(5):
                    if n < 4:
                        qt = n // 2
                        nk = P * (qt + 1)
                        for i in range(4):
                            act.wait_ge(S("att_max"), 4 * n + i + 1)
                            if n >= 2:
                                act.wait_ge(S("att_av"), n - 1)
                            for kind in range(2):
                                func(prob[:, n % 2, i, kind * T:kind * T + nk], ps[:, i, kind * T:kind * T + nk], ACT.Exp, "att_exp",
                                     bias=pst[:, n % 2, i, kind:kind + 1], accum_out=pst[:, n % 2, i, 2 + kind:3 + kind])
                    if n == 0:
                        heads()
                    if n >= 1:
                        for j in range(1 + 2 * ((n - 1) // 2 + 1)):
                            t = turn[0]
                            turn[0] += 1
                            act.wait_ge(S("att_tr"), t + 1)
                            rows = NCMP if j == 0 else P
                            func(pt[0:rows, t % 2, :], ps[0:rows, 4 + t % 2, :], ACT.Copy, "att_pt")
                mix_high("mix_x", 0, range(4, KT), TM)

            def hgrn_in():
                act.wait_ge(*once("lb_arg"))
                func(lbs[:, 0, :], lbs[:, 0, :], ACT.Tanh, "lb_th", scale=0.5)
                for j in range(H_UNITS):
                    if H_OWNER[j] == "a":
                        dst, bias, m = ((fF, "fp_b", j), (fQ, "qp_b", j - H_Q), (fZ, "z_b", j - H_Z0 - (8 if j > H_Z0 else 0)))[min(j // 8, 2)]
                        drain(G_H + j, dst[:, m, :], bias=V(bias, m))
                    ahead(U_H + j)
                    if H_OWNER[j] == "a":
                        if j == 7:
                            func(dif[:, 1, :].rearrange("p (a b) -> p a b", a=8), fF[:], ACT.Tanh, "f_th", scale=0.5)
                            act.wait_ge(S("f_ready"), 8)
                            func(fF[:], fF[:], ACT.Ln, "f_log")
                        if j == 15:
                            act.wait_ge(*once("f_read"))
                            func(dif[:, 1, :].rearrange("p (a b) -> p a b", a=8), fQ[:], ACT.Tanh, "q_th", scale=0.5)
                        if j == H_UNITS - 2:
                            powers((0,))

            def powers(levels):
                for lev in levels:
                    b = (LEVELS + (P,))[lev]
                    act.wait_ge(S("lev_d"), lev + (1 if lev < 7 else 2))
                    d = dif[:, lev % 2, :].rearrange("p (n w) -> p n w", w=2 * b)
                    func(d[:, :, 0:b], d[:, :, 0:b], ACT.Exp, "lev_e", scale=-1.0)
                    func(d[:, :, b:], d[:, :, b:], ACT.Exp, "lev_e")

            def hgrn():
                powers(range(1, 8))
                act.wait_ge(S("lev_s"), 4 * 8)
                func(qkl[:, 1, :].rearrange("p (a b) -> p a b", a=8), fZ, ACT.Tanh, "z_th", scale=0.5)
                nc.scalar.preload_act_table_set(LOG_EXP)
                for i in range(2):
                    act.wait_ge(*once(("hg_o", "hg_o2")[i]))
                    func(dif[:, 0, i * 1024:(i + 1) * 1024], ps[:, 4 + 2 * i:6 + 2 * i, :].rearrange("p a b -> p (a b)"), ACT.Square,
                         ("hg_sq", "hg_sq2")[i])
                for i in range(2):
                    act.wait_ge(*once(("hg_ss", "hg_ss2")[i]))
                    r = dif[:, 1, i * 1024:(i + 1) * 1024]
                    func(r, ps[:, 2 * i:2 * i + 2, :].rearrange("p a b -> p (a b)"), ACT.Ln, scale=1.0 / P, bias=eps[:, 0:1])
                    func(r, r, ACT.Exp, ("hg_rs", "hg_rs2")[i], scale=-0.5)
                mix_high("mix_x", 4, range(KT), TM)

            def ffn(u0, g0, first):
                d0 = drained("v", g0 - 1)

                def gate(it, f4):
                    act.wait_ge(S("w_used"), it * 8 + (u0 + 2 * f4 + 1))
                    act.wait_ge(S("drained_v"), it * 8 + (d0 + 2 * f4 + 1 - 8))
                    nc.scalar.activation(fth[:, f4, :], ps[:, (g0 + 2 * f4) % MM_BANKS, 0:TT], ACT.Tanh,
                                         scale=0.5).then_inc(S("ffn_th"), 1)
                    ahead(u0 + 2 * f4, it)
                    ahead(u0 + 2 * f4 + 1, it)

                with act.Fori(0, FT // 4) as it:
                    for f4 in range(4):
                        gate(it, f4)
                for f4 in range(FT % 4):
                    gate(FT // 4, f4)
                act.wait_ge(S("ffn_th"), first + FT)

            def mixer_in():
                for j in range(P_UNITS):
                    if j < 12:
                        dst = (sbq, sbk, sbv)[j // 4][:, j % 4, 0:TT]
                        act.wait_ge(S("w_used"), used_by(G_P + j))
                        func(dst, ps[:, (G_P + j) % MM_BANKS, 0:TT], ACT.Copy, "drained_a", scale=0.125 if j < 4 else 1.0)
                    else:
                        drain(G_P + j, pr[:, j - 12, 1:1 + TT], TT)
                    ahead(U_P + j)
                    if j == 16:
                        act.wait_ge(*once("sb_vt"))
                        func(sbvt[:], ps[:, 4:7, :], ACT.Copy, "sb_v")
                act.wait_ge(S("shifted"), 14)
                func(pr[0:32, 12, 1:1 + TT], pr[0:32, 12, 1:1 + TT], ACT.Tanh, "lora_th")
                func(pr[:, 13, 1:1 + TT], pr[:, 13, 1:1 + TT], ACT.Tanh, "g_th", scale=0.5)
                act.wait_ge(*once("lora_up"))
                for j in range(4):
                    func(pD[:, j, :], ps[:, j, 0:TT], ACT.Tanh, "decay_th" if j == 3 else "act_step", scale=0.5, bias=V("w0", j))
                for j in range(4):
                    func(pA[:, j, :], ps[:, 4 + j, 0:TT], ACT.Tanh, "a_th" if j == 3 else "act_step", scale=0.5, bias=V("a0", j))
                nc.scalar.preload_act_table_set(LOG_EXP)
                act.wait_ge(S("kk_raw"), 4)
                func(pT[:], pK[:], ACT.Square, "kk_sq")

            def sticks():
                def lengths():
                    act.wait_ge(*once("kk_n2b"))
                    func(pT[:], pT[:], ACT.Ln, scale=2.0 ** 20)
                    func(pT[:], pT[:], ACT.Exp, "kk_rs", scale=-0.5, bias=eps[:, 3:4])

                def decay_products():
                    act.wait_ge(*once("cum"))
                    func(pT[:], pC[:], ACT.Exp, "e_c")

                def decay_quotients():
                    act.wait_ge(*once("cum_x"))
                    func(pD[:], pD[:], ACT.Exp, "e_cx")
                    func(pC[:], pC[:], ACT.Exp, "e_nc", scale=-1.0)

                between = {2: lengths, 6: decay_products, 7: decay_quotients}
                for h in range(12):
                    if h < 8:
                        act.wait_ge(S("sb_z"), h + 1)
                        if h >= 2:
                            act.wait_ge(S("sb_sp"), h - 1)
                        z = ps[:, h % 2, 0:432]
                        func(zs[:, h % 4, :], z, ACT.Copy)
                        func(zl[:, h % 2, :], z, ACT.Abs)
                        func(zl[:, h % 2, :], zl[:, h % 2, :], ACT.Exp, scale=-1.0)
                        func(zl[:, h % 2, :], zl[:, h % 2, :], ACT.Ln, "sb_ln", bias=eps[:, 2:3])
                    if 3 <= h <= 10:
                        r = h - 3
                        act.wait_ge(S("sb_arg"), r + 1)
                        if r >= 2:
                            act.wait_ge(S("sb_av"), r - 1)
                        func(zA[:, r % 2, :], zs[:, r % 4, :], ACT.Exp, "sb_A")
                    if h >= 4:
                        r = h - 4
                        a = 64 * (r % 2)
                        act.wait_ge(S("sb_av"), r + 1)
                        func(mixT[a:a + 64, r // 2, :], ps[a:a + 64, 6 + r % 2, 0:TT], ACT.Copy, "sb_out")
                    if h in between:
                        between[h]()

            def rwkv():
                nth = [0]
                for tau, (t0, n) in enumerate(TILES2):
                    for w in range(4):
                        act.wait_ge(S("r_tok"), 4 * tau + w + 1)
                        src = ps[0:n, 2 + w, :]
                        if w == 0:
                            func(rWA[0:n, :, 64:128], src.rearrange("p (h j) -> p h j", j=64), ACT.Copy, "r_tokc")
                        else:
                            func(tok[0:n, w - 1, :], src, ACT.Copy, "r_tokc")
                    act.wait_ge(S("r_w"), tau + 1)
                    func(rWA[0:n, :, 0:64], ps[0:n, 6, :].rearrange("p (h j) -> p h j", j=64), ACT.Copy, "r_wc")
                    for _ in [b for b in LEVELS[1:6] if b < n]:
                        for q in range(2):
                            nth[0] += 1
                            act.wait_ge(S("r_x"), nth[0])
                            func(rX[0:n, 4 * q:4 * q + 4, 0:n], ps[0:n, q, 0:4 * n].rearrange("p (q t) -> p q t", q=4), ACT.Copy, "r_xc")
                    act.wait_ge(S("r_u"), tau + 1)
                    for q in range(2):
                        func(rUM[0:n, 4 * q:4 * q + 4, :], ps[0:n, q, :].rearrange("p (q t) -> p q t", q=4), ACT.Copy,
                             "r_uc" if q else "act_step", scale=-1.0)
                    act.wait_ge(S("r_y0"), tau + 1)
                    func(yT[:, :, t0:t0 + n], ps[:, 3, 0:4 * n].rearrange("p (q t) -> p q t", q=4), ACT.Copy, "r_y0c")
                act.wait_ge(S("gn_d"), 4)
                func(pT[:], yT[:], ACT.Square, "gn_sq")
                act.wait_ge(*once("gn_var"))
                nc.scalar.preload_act_table_set(LOG_EXP)
                func(pT[:], ps[:, 0:4, 0:TT], ACT.Ln, scale=1.0 / 64, bias=eps[:, 1:2])
                func(pT[:], pT[:], ACT.Exp, "gn_rs", scale=-0.5)
                mix_high("mix_x", 4 + KT, range(4, KT), 0)

            norm0()
            even_in()
            mlstm()
            attention()
            squares_behind("norm1", U_EO, KT, G_EO, TM, T)
            hgrn_in()
            hgrn()
            squares_behind("ffn1", U_HO, KT, G_HO, 0, TT)
            ffn(U_F1, G_F1, 0)
            squares_behind("mix", U_F1 + GU_UNITS, DN_UNITS, G_F1 + GU_UNITS, 0, TT)
            mixer_in()
            sticks()
            rwkv()
            squares_behind("ffn2", U_PO, KT, G_PO, 0, TT)
            ffn(U_F2, G_F2, FT)
            squares_behind("final", U_F2 + GU_UNITS, DN_UNITS, G_F2 + GU_UNITS, 0, TT)

        @block.vector
        def _(dve):
            step, dve_n = in_order(dve, "dve_step")

            def tt(out, a, b, op, sem="dve_step"):
                step(nc.vector.tensor_tensor(out, a, b, op), sem)

            def ts(out, a, s1, s2, op0, op1=None, sem="dve_step"):
                if op1 is None:
                    step(nc.vector.tensor_scalar(out, a, s1, s2, op0), sem)
                else:
                    step(nc.vector.tensor_scalar(out, a, s1, s2, op0, op1), sem)

            def stt(out, a, s, b, op0, op1, sem="dve_step"):
                step(nc.vector.scalar_tensor_tensor(out=out, in0=a, scalar=s, in1=b, op0=op0, op1=op1), sem)

            def add_square(tag, k, n):
                dve.wait_ge(S("norm_sq"), NORMS.index(tag) * KT + k + 1)
                tt(sq[:, 0, 0:n], sq[:, 0, 0:n], sq[:, k, 0:n], ALU.add, "norm_sum")

            def norm(tag, c0, n, w):
                i = NORMS.index(tag) * KT
                if tag == "norm0":
                    for k in range(1, KT - 1):
                        add_square(tag, k, n)
                dve.wait_ge(S("norm_rstd"), NORMS.index(tag) + 1)
                if tag == "norm0":
                    dve.wait_ge(S("early_in"), 32)
                split = tag != "final"
                for j in range(KT + 2):
                    if j < KT:
                        nc.vector.scalar_tensor_tensor(out=hT[:, j, c0:c0 + n], in0=xT[:, j, c0:c0 + n], scalar=V(w, j),
                                                       in1=rstd[:, 0:n], op0=ALU.mult, op1=ALU.mult)\
                            .then_inc(S("norm_x" if split else "norm_h"), 1)
                    if split and j >= 2:
                        k = j - 2
                        dve.wait_ge(S("norm_hi"), i + k + 1)
                        nc.vector.tensor_tensor(aL[:, k, c0:c0 + n], hT[:, k, c0:c0 + n], aH[:, k, c0:c0 + n].bitcast(F32),
                                                ALU.subtract).then_inc(S("norm_h"), 1)
                dve.wait_ge(S("norm_h"), i + KT)

            def mix_low(n, k, c0):
                dve.wait_ge(S("mix_hi"), n)
                tt(aL[:, k, c0:TT], mixT[:, k, c0:TT], aH[:, k, c0:TT].bitcast(F32), ALU.subtract, "mix_split")

            def mix_split(k, c0):
                step(nc.vector.tensor_copy(aH[:, k, c0:TT], mixT[:, k, c0:TT]))
                tt(aL[:, k, c0:TT], mixT[:, k, c0:TT], aH[:, k, c0:TT].bitcast(F32), ALU.subtract, "mix_split")

            def setup():
                for j, v in enumerate((EPS, LNX_EPS, 1.0, 10 * float(np.log(2.0)))):
                    step(nc.vector.memset(eps[:, j:j + 1], v), "setup")
                step(nc.vector.memset(qkpre[:, :, 0:3], 0.0), "setup")

            def masks():
                dve.wait_ge(S("consts_in"), 64)
                step(nc.vector.tensor_copy(ident_bf[:], C("ident")), "setup")
                ts(before_bf[:], C("gt"), BIG, None, ALU.mult, sem="setup")
                ts(notyet_bf[:], C("ge"), BIG, None, ALU.mult, sem="setup")
                ts(later_bf[:], C("ge"), 1.0, BIG, ALU.subtract, ALU.mult, sem="setup")
                ts(vec[:, VEC["w0"]:VEC["w0"] + 8], vec[:, VEC["w0"]:VEC["w0"] + 8], 0.5, None, ALU.mult, sem="setup")
                ts(vec[:, VEC["mnorm"]:VEC["mnorm"] + 4], vec[:, VEC["mnorm"]:VEC["mnorm"] + 4], 0.25, None, ALU.mult, sem="setup")
                ts(vec[:, VEC["hnorm"]:VEC["hnorm"] + 8], vec[:, VEC["hnorm"]:VEC["hnorm"] + 8], 0.5, None, ALU.mult, sem="setup")
                ts(vec[:, VEC["nqk"]:VEC["nqk"] + 4], vec[:, VEC["nqk"]:VEC["nqk"] + 4], 0.125, None, ALU.mult, sem="setup")

            def drain_pair(g, outs, off):
                dve.wait_ge(S("w_used"), used_by(g + 1))
                for j, out in enumerate(outs):
                    src = ps[:, (g + 1) % MM_BANKS, :].rearrange("p (t u n) -> p t u n", t=2, u=2)[:, :, j, :]
                    tt(out, src, mid(row[:, off + j * P:off + (j + 1) * P], 2), ALU.add, "drained_v")

            def convolved(j):
                dve.wait_ge(S("drained_a"), drained("a", G_E + E_QK + j))
                c = lambda tap: V("conv_w", 4 * j + tap)
                ts(qk[:, j, :], qkpre[:, j, 0:T], c(0), V("conv_b", j), ALU.mult, ALU.add)
                for tap in range(1, 4):
                    stt(qk[:, j, :], qkpre[:, j, tap:tap + T], c(tap), qk[:, j, :], ALU.mult, ALU.add,
                        "conv" if tap == 3 else "dve_step")

            def even_in():
                drain_pair(G_E + E_VSW, [vsw[:, 0], vsw[:, 1]], ROW["vs"])
                for j in range(3):
                    convolved(j)
                dve.wait_ge(*once("nqk_rs"))
                for j in range(6):
                    stt(nqk[:, j, :], nqk[:, j, :], V("nqk", j), rs[:, j, :], ALU.mult, ALU.mult, "nqk_n")
                for j in range(3, 5):
                    convolved(j)
                dve.wait_ge(*once("nqk_rot"))
                for j, b in enumerate((4, 5, 7)):
                    tt(rs[:, 2 * j:2 * j + 2, :], ps[:, b, :].rearrange("p (a b) -> p a b", a=2), mid(C("sin", T), 2), ALU.mult, "rope_done")
                tt(nqk[:], nqk[:], mid(C("cos", T), 6), ALU.mult)
                tt(nqk[:], nqk[:], rs[:], ALU.add, "rope_done")
                for j in range(5, 8):
                    convolved(j)
                compress()
                for j in (0, 2):
                    drain_pair(G_E + E_V + j, [vtok[:, :, (j + i) * P:(j + i + 1) * P] for i in range(2)], ROW["v"] + j * P)
                hidden()
                dve.wait_ge(*once("small_t"))
                step(nc.vector.tensor_copy(small[:], ps[:, 5, 0:64].rearrange("p (t n) -> p t n", t=2)))
                for j in range(2):
                    tt(gl[:, 0, 4 * j:4 * j + 4], small[:, j, 4:8], row[:, ROW["fbias"]:ROW["fbias"] + 4], ALU.add, "fgate")
                dve.wait_ge(*once("kc_rs"))
                stt(kct[:, 2, :], kct[:, 0, :], V("kcn"), kct[:, 3, :], ALU.mult, ALU.mult, "kc_n")
                dve.wait_ge(*once("log1p"))
                stt(gl[:, 3, :], gl[:, 0, :], 0.0, gl[:, 2, :], ALU.min, ALU.subtract, "logf")
                dve.wait_ge(*once("kc_rot"))
                tt(kct[:, 0, :], ps[:, 6, 288:288 + NCMP], C("sinc", NCMP), ALU.mult)
                tt(kct[:, 3, :], kct[:, 2, :], C("cosc", NCMP), ALU.mult)
                tt(kct[:, 3, :], kct[:, 3, :], kct[:, 0, :], ALU.add, "kc_ready")

            def compress():
                dve.wait_ge(*once("dup_done"))
                for kind in range(2):
                    d = ps[:, 4 + kind, :].rearrange("p (g t) -> p g t", g=2)
                    step(nc.vector.tensor_copy(kc2[0:64, kind, :, :], d[0:64]))
                    step(nc.vector.tensor_copy(kc2[64:128, kind, :, 0:T - 1], d[64:128, :, 1:T]))
                for kind in range(2):
                    for g in range(2):
                        for a in range(2):
                            pos = vec[:, VEC[("kpos", "vpos")[kind]] + 8 * a:VEC[("kpos", "vpos")[kind]] + 8 * a + 8]
                            v = kc2[:, kind, g, :].rearrange("p (n j two) -> p j n two", n=16, two=2)[:, :, a:a + NCMP, 0]
                            tt(xc[:, kind, 8 * a:8 * a + 8, g * NCMP:(g + 1) * NCMP], v, end(pos, NCMP), ALU.add, "xc_ready")
                step(nc.vector.tensor_copy(xcH[:], xc[:]), "xc_ready")
                tt(xcL[:], xc[:], xcH[:].bitcast(F32), ALU.subtract, "xc_ready")

            def hidden():
                dve.wait_ge(S("w_used"), U_C + C_UNITS)
                step(nc.vector.tensor_copy(hx[:, 0, :], ps[0:2 * NCMP, 6, 0:2 * P]), "hx_x")
                dve.wait_ge(*once("hx_sq"))
                ts(hx[:, 1, :], hx[:, 1, :], 0.044715, 1.0, ALU.mult, ALU.add)
                tt(hx[:, 1, :], hx[:, 1, :], hx[:, 0, :], ALU.mult, "hx_arg")
                dve.wait_ge(*once("hx_th"))
                ts(hx[:, 2, :], hx[:, 2, :], 0.5, 0.5, ALU.mult, ALU.add)
                tt(hx[:, 0, :], hx[:, 2, :], hx[:, 0, :], ALU.mult, "gelu_ready")

            def mlstm():
                dve.wait_ge(*once("bcum"))
                step(nc.vector.tensor_copy(gl[:, 4, :], ps[:, 4, 0:8]), "gate_cols")
                tt(gl[:, 5, :].rearrange("p (a b) -> p a b", a=2), small[:, :, 0:4], gl[:, 4, :].rearrange("p (a b) -> p a b", a=2),
                   ALU.subtract, "gate_cols")
                dve.wait_ge(*once("gate_rows"))
                step(nc.vector.tensor_copy(rows4[:, 0:2, :].rearrange("p a b -> p (a b)"), ps[0:4, 4, :]), "row_max")
                step(nc.vector.tensor_tensor_scan(rows4[:, 2, :], rows4[:, 1, :], rows4[:, 1, :], 0.0, ALU.max, ALU.max), "row_max")
                tt(rows4[:, 3, :], rows4[:, 2, :], rows4[:, 0, :], ALU.add, "row_max")
                dve.wait_ge(*once("qk_th"))
                for j in range(2):
                    stt(qk[:, 4 * j:4 * j + 4, :], th[:, 4 * j:4 * j + 4, :], 1.0, qk[:, 4 * j:4 * j + 4, :], ALU.add, ALU.mult, "qk_ready")
                for h in range(5):
                    if h < 4:
                        dve.wait_ge(S("mlstm_e"), h + 1)
                        stt(mST[:, h % 2, :], ps[:, 4 * (h % 2) + 2, 0:384], 0.25 * P ** -0.5, mE[:, h % 2, :], ALU.mult, ALU.mult, "mlstm_st")
                    if h == 1:
                        dve.wait_ge(*once("nz_th"))
                        stt(nz[:], rs[:, 0:4, :], 1.0, nz[:], ALU.add, ALU.mult)
                        dve.wait_ge(*once("oz_th"))
                        stt(oz[:, 4:8, :], th[:, 4:8, :], 1.0, oz[:, 4:8, :], ALU.add, ALU.mult)
                    if h >= 1:
                        j = (h - 1) % 2
                        dve.wait_ge(S("mlstm_d"), h)
                        d = mad[:, h - 1, :]
                        tt(d, d, mem[:, h - 1, :], ALU.max)
                        step(nc.vector.reciprocal(d, d))
                        tt(hm[:, h - 1, :], ps[:, 4 * j + 3, 0:T], d, ALU.mult, "mlstm_h")

            def heads(n):
                if n == 0:
                    dve.wait_ge(*once("mh_rs"))
                    tt(hm[:], hm[:], rs[:, 0:4, :], ALU.mult)
                    stt(hm[:], th[:, 0:4, :], 1.0, hm[:], ALU.add, ALU.mult)
                if n == 1:
                    for h in range(4):
                        stt(mixT[:, h, TM:TT], hm[:, h, :], V("mnorm", h), oz[:, 4 + h, :], ALU.mult, ALU.mult)
                if n == 2:
                    for k in range(4):
                        mix_split(k, TM)

            def attention():
                dve.wait_ge(*once("cmp_s"))
                for qt in range(2):
                    for g in range(2):
                        s = ps[:, 6 + g, qt * 4 * NCMP:(qt + 1) * 4 * NCMP].rearrange("p (i n) -> p i n", i=4)
                        tt(pc[:, qt * 8 + 4 * g:qt * 8 + 4 * g + 4, :], s, mid(C("cneg", 2 * NCMP)[:, qt * NCMP:(qt + 1) * NCMP], 4), ALU.add)
                step(nc.vector.tensor_reduce(cs[:, 0, :], pc[:], AX.X, ALU.max))
                tt(pc[:], pc[:], end(cs[:, 0, :], NCMP), ALU.subtract, "cmp_sub")
                dve.wait_ge(*once("cmp_e"))
                step(nc.vector.tensor_reduce(cs[:, 1, :], pc[:], AX.X, ALU.add))
                for qt in range(2):
                    tt(pc[:, qt * 8:qt * 8 + 8, :], pc[:, qt * 8:qt * 8 + 8, :],
                       mid(C("cok", 2 * NCMP)[:, qt * NCMP:(qt + 1) * NCMP], 8), ALU.mult)
                step(nc.vector.reciprocal(cs[:, 1, :], cs[:, 1, :]))
                dve.wait_ge(*once("gates_th"))
                gates = small[:, :, 8:32]
                ts(gates, gates, 0.5, 0.5, ALU.mult, ALU.add)
                g3 = small[:, :, 8:32].rearrange("p t (h b) -> p t h b", b=3)
                tt(cs[:, 2, :].rearrange("p (t h) -> p t h", t=2), cs[:, 1, :].rearrange("p (t h) -> p t h", t=2), g3[:, :, :, 0], ALU.mult)
                tt(pc[:], pc[:], end(cs[:, 2, :], NCMP), ALU.mult, "cmp_p")
                for n in range(5):
                    if n < 4:
                        qt, g = n // 2, n % 2
                        nk = P * (qt + 1)
                        for i in range(4):
                            dve.wait_ge(S("att_s"), 4 * n + i + 1)
                            s = ps[:, i, :].rearrange("p (k n) -> p k n", k=2)[:, :, 0:nk]
                            step(nc.vector.tensor_reduce(pst[:, n % 2, i, 0:2], s, AX.X, ALU.max, negate=True), "att_max")
                        for i in range(4):
                            dve.wait_ge(S("att_exp"), 8 * n + 2 * i + 2)
                            r = pst[:, n % 2, i, 2:4]
                            step(nc.vector.reciprocal(r, r))
                            tt(r, r, g3[:, qt, 4 * g + i, 1:3], ALU.mult)
                            for kind in range(2):
                                p = prob[:, n % 2, i, kind * T:kind * T + nk]
                                ts(p, p, pst[:, n % 2, i, 2 + kind:3 + kind], None, ALU.mult, sem="att_p")
                        heads(n)
                    if n >= 1:
                        qt, g = (n - 1) // 2, (n - 1) % 2
                        dve.wait_ge(S("att_av"), n)
                        rows = slice(64 * g, 64 * g + 64)
                        stt(mixT[rows, 4:8, TM + qt * P:TM + (qt + 1) * P],
                            ps[rows, 6 + (n - 1) % 2, :].rearrange("p (i q) -> p i q", i=4), 0.5,
                            nz[rows, :, qt * P:(qt + 1) * P], ALU.mult, ALU.mult, "att_o")
                        if n == 4:
                            dve.sem_inc(S("mix_x"), 4)
                            dve_n["mix_x"] = 4
                for k in range(4, KT):
                    mix_low(k - 3, k, TM)

            def residual(tag, g0, c0, scale=1.0):
                for m in range(KT):
                    if m >= 2:
                        add_square(tag, m - 1, TT - (TM if tag == "norm1" else 0))
                    dve.wait_ge(S("w_used"), used_by(g0 + m))
                    stt(xT[:, m, c0:TT], ps[:, (g0 + m) % MM_BANKS, 0:TT - c0], scale, xT[:, m, c0:TT], ALU.mult, ALU.add, "drained_v")

            def hgrn_in():
                lb = lambda j: lbs[:, j, :]
                l0, l1 = vec[:, VEC["lb0"]:VEC["lb0"] + 8], vec[:, VEC["lb1"]:VEC["lb1"] + 8]
                tt(lb(0), l0, l1, ALU.subtract, "lb_arg")
                dve.wait_ge(*once("lb_th"))
                ts(lb(1), lb(0), -0.25, 0.25, ALU.mult, ALU.add)
                ts(lb(2), lb(1), -1.0, 1.0, ALU.mult, ALU.add)
                ts(lb(3), lb(1), 0.5, None, ALU.mult)
                ts(lb(4), lb(1), -0.5, None, ALU.mult)
                step(nc.vector.memset(dif[:, 0, :], 1.0))
                step(nc.vector.memset(dif[:, 0, :].rearrange("p (n w) -> p n w", w=P)[:, :, 0:1], 0.0))
                dve.wait_ge(*once("f_th"))
                t8 = dif[:, 1, :].rearrange("p (a b) -> p a b", a=8)
                for h in range(8):
                    ts(fF[:, h, :], t8[:, h, :], lbs[:, 1, h:h + 1], lbs[:, 2, h:h + 1], ALU.mult, ALU.add, "f_ready")
                for h in range(8):
                    ts(fK[:, h, :], t8[:, h, :], lbs[:, 4, h:h + 1], lbs[:, 3, h:h + 1], ALU.mult, ALU.add,
                       "f_read" if h == 7 else "dve_step")
                dve.wait_ge(*once("f_log"))
                step(nc.vector.tensor_tensor_scan(fC, dif[:, 0, :], fF[:].rearrange("p a b -> p (a b)"),
                                                  0.0, ALU.mult, ALU.add))
                dve.wait_ge(*once("q_th"))
                stt(fQ[:], t8, 1.0, fQ[:], ALU.add, ALU.mult, "q_ready")
                dve.sem_inc(S("lev_qk"), 2)
                dve_n["lev_qk"] = 2
                for j in range(0, 8, 2):
                    drain_pair(G_H + H_IV + j, [ivt[:, :, (j + i) * P:(j + i + 1) * P] for i in range(2)], ROW["iv"] + j * P)

            def hgrn():
                def banks_of(lev):
                    for j in range(4):
                        dve.wait_ge(S("lev_s"), 4 * lev + j + 1)
                        out = hA[:, 2 * j:2 * j + 2].rearrange("p h t w -> p (h t w)")
                        src = ps[:, 4 * ((lev + 1) % 2) + j, :]
                        if lev == 0:
                            v = lambda ap: ap.rearrange("p (n w) -> p n w", n=4)
                            tt(v(out), v(src), mid(C("ident"), 4), ALU.mult, "lev_a")
                        else:
                            b = LEVELS[lev - 1]
                            v = lambda ap, n: ap.rearrange("p (n m w) -> p n m w", n=n, w=2 * b)[:, :, :, b:]
                            m = v(C("hlev", 7 * P)[:, (lev - 1) * P:lev * P], 1).broadcast_to([P, 4, P // (2 * b), b])
                            step(nc.vector.copy_predicated(v(out, 4), m.bitcast(U32), v(src, 4)), "lev_a")

                def products(lev):
                    b = (LEVELS + (P,))[lev - 1]
                    view = lambda ap: ap.rearrange("p (n w) -> p n w", w=2 * b)
                    d, o = view(dif[:, (lev - 1) % 2, :]), view(qkl[:, lev % 2, :])
                    flat = lambda t: view(t[:].rearrange("p a b -> p (a b)"))
                    dve.wait_ge(S("lev_e"), 2 * lev)
                    if lev >= 3:
                        dve.wait_ge(S("lev_s"), 4 * (lev - 1))
                    tt(o[:, :, 0:b], d[:, :, 0:b], flat(fK)[:, :, 0:b], ALU.mult, "lev_qk")
                    tt(o[:, :, b:], d[:, :, b:], flat(fQ)[:, :, b:], ALU.mult, "lev_qk")

                for lev in range(1, 9):
                    products(lev)
                    banks_of(lev - 1)
                for j in range(2):
                    dve.wait_ge(S("lev_s"), 4 * 8 + j + 1)
                    step(nc.vector.tensor_copy(hX[:, 4 * j:4 * j + 4, :], ps[:, 4 + j, :].rearrange("p (h w) -> p h w", h=4)), "lev_a")
                dve.wait_ge(*once("z_th"))
                stt(fZ, qkl[:, 1, :].rearrange("p (a b) -> p a b", a=8), 1.0, fZ, ALU.add, ALU.mult)
                for h in range(KT + 1):
                    at = slice(h * T, (h + 1) * T)
                    if h in (0, 4):
                        dve.wait_ge(*once(("hg_rs", "hg_rs2")[h // 4]))
                        half = slice(h * T, (h + 4) * T)
                        tt(dif[:, 1, half], dif[:, 1, half], ps[:, 4 + h // 2:6 + h // 2, :].rearrange("p a b -> p (a b)"), ALU.mult)
                    if h < KT:
                        stt(mixT[:, h, TM:TT], dif[:, 1, at], V("hnorm", h), fZ[:, h, :], ALU.mult, ALU.mult, "mix_x")
                    if h >= 1:
                        mix_low(4 + h, h - 1, TM)

            def ffn(u0, g0, first):
                d0 = drained("v", g0 - 1)

                def pair(it, f4, f):
                    half, prod = fhalf[:], fact[:, f4 % 2, :]
                    dve.wait_ge(S("ffn_th"), it * 4 + (first + f4 + 1))
                    dve.wait_ge(S("drained_v"), it * 8 + (d0 + 2 * f4))
                    nc.vector.scalar_tensor_tensor(out=half, in0=fth[:, f4, :], scalar=1.0,
                                                   in1=ps[:, (g0 + 2 * f4) % MM_BANKS, 0:TT], op0=ALU.add,
                                                   op1=ALU.mult).then_inc(S("drained_v"), 1)
                    dve.wait_ge(S("drained_v"), it * 8 + (d0 + 2 * f4 + 1))
                    dve.wait_ge(S("w_used"), it * 8 + (u0 + 2 * f4 + 2))
                    nc.vector.tensor_tensor(prod, half, ps[:, (g0 + 2 * f4 + 1) % MM_BANKS, 0:TT],
                                            ALU.mult).then_inc(S("drained_v"), 1)
                    dve.wait_ge(S("drained_v"), it * 8 + (d0 + 2 * f4 + 2))
                    nc.vector.tensor_copy(fH[:, f, :], prod).then_inc(S("ffn_hi"), 1)
                    dve.wait_ge(S("ffn_hi"), it * 4 + (first + f4 + 1))
                    nc.vector.tensor_tensor(fL[:, f, :], prod, fH[:, f, :].bitcast(F32),
                                            ALU.subtract).then_inc(S("ffn_split"), 1)
                    dve.wait_ge(S("ffn_split"), it * 4 + (first + f4 + 1))

                with dve.Fori(0, FT // 4) as it:
                    for f4 in range(4):
                        pair(it, f4, it * 4 + f4)
                for f4 in range(FT % 4):
                    pair(FT // 4, f4, FT - FT % 4 + f4)
                dve.wait_ge(S("drained_v"), d0 + GU_UNITS)
                dve_n["drained_v"] += GU_UNITS
                residual("mix" if first == 0 else "final", g0 + GU_UNITS, 0, 0.25)

            def mixer_in():
                step(nc.vector.memset(pr[:, :, 0:1], 0.0))
                step(nc.vector.memset(sbk[:, :, TT:], 0.0), "sb_pad")
                step(nc.vector.memset(sbv[:, :, TT:], 0.0), "sb_pad")
                for j in range(14):
                    dve.wait_ge(S("drained_a"), drained("a", G_P + 12 + j))
                    tmp = pT[:, j % 4, :]
                    tt(tmp, pr[:, j, 0:TT], pr[:, j, 1:1 + TT], ALU.subtract)
                    stt(pr[:, j, 1:1 + TT], tmp, V("mu", j), pr[:, j, 1:1 + TT], ALU.mult, ALU.add, "shifted")
                k = pr[:, 4:8, 1:1 + TT]
                for j in range(4):
                    ts(pK[:, j, :], k[:, j, :], V("k_k", j), None, ALU.mult, sem="kk_raw")

            def sticks():
                k = pr[:, 4:8, 1:1 + TT]
                flat = lambda t: t[:].rearrange("p a b -> p (a b)")

                def gates():
                    dve.wait_ge(*once("decay_th"))
                    ts(pD[:], pD[:], -0.5 * DECAY, -0.5 * DECAY, ALU.mult, ALU.add)
                    dve.wait_ge(*once("a_th"))
                    ts(pA[:], pA[:], 0.5, 0.5, ALU.mult, ALU.add)
                    dve.wait_ge(*once("kk_ss"))
                    ts(pT[:, 0:2, :], ps[:, 2:4, 0:TT], 1e-24, None, ALU.max, sem="kk_n2")

                def lengths():
                    dve.wait_ge(*once("kk_ss2"))
                    ts(pT[:, 2:4, :], ps[:, 2:4, 0:TT], 1e-24, None, ALU.max, sem="kk_n2b")

                def keys():
                    dve.wait_ge(*once("kk_rs"))
                    tt(pK[:], pK[:], pT[:], ALU.mult)
                    for j in range(4):
                        ts(pT[:, j, :], pA[:, j, :], 1.0, V("k_a", j), ALU.subtract, ALU.mult)

                def scaled_keys():
                    stt(k, pT[:], 1.0, k, ALU.add, ALU.mult)
                    tt(pA[:], pA[:], pK[:], ALU.mult)

                def cumulative():
                    step(nc.vector.memset(pT[:], 1.0))
                    step(nc.vector.memset(pT[:, :, 0:TT:RW_CHUNK], 0.0))
                    step(nc.vector.tensor_tensor_scan(flat(pC), flat(pT), flat(pD), 0.0, ALU.mult, ALU.add), "cum")

                def exclusive():
                    tt(pD[:], pC[:], pD[:], ALU.subtract, "cum_x")

                def rho():
                    dve.wait_ge(*once("e_c"))
                    step(nc.vector.tensor_copy(eL[:, :, 0:4], pT[:, :, RW_CHUNK - 1:4 * RW_CHUNK:RW_CHUNK]))
                    tt(AR[:, :, 1, :], pr[:, 0:4, 1:1 + TT], pT[:], ALU.mult)

                def alpha():
                    dve.wait_ge(*once("e_cx"))
                    tt(AR[:, :, 0, :], pK[:], pD[:], ALU.mult)

                def beta():
                    dve.wait_ge(*once("e_nc"))
                    tt(BK[:, :, 0, :], pA[:], pC[:], ALU.mult, "bk_ready")

                def kappa():
                    tt(BK[:, :, 1, :], k, pC[:], ALU.mult, "bk_ready")

                between = (gates, lengths, None, keys, scaled_keys, cumulative, exclusive, rho, alpha, beta, kappa)
                for h in range(11):
                    if h == 1:
                        lengths()
                    if h >= 3:
                        r = h - 3
                        dve.wait_ge(S("sb_rest"), r + 1)
                        tt(zs[:, r % 4, :], zs[:, r % 4, :], ps[:, 4 + r % 2, 0:432], ALU.subtract, "sb_arg")
                    if h < 8:
                        dve.wait_ge(S("sb_ln"), h + 1)
                        if h >= 3:
                            dve.wait_ge(S("sb_rest"), h - 2)
                        stt(zl[:, h % 2, :], zs[:, h % 4, :], 0.0, zl[:, h % 2, :], ALU.max, ALU.add)
                        tt(zp[:, h % 3, :], zl[:, h % 2, :], C("sbok", 432), ALU.mult, "sb_sp")
                    if between[h] and h != 1:
                        between[h]()

            def rwkv():
                dve.wait_ge(S("sb_out"), 8)
                for k in range(4):
                    mix_split(k, 0)
                for j in range(4):
                    ts(pK[:, j, :], pr[:, j, 1:1 + TT], V("r_k", j), None, ALU.mult)
                tt(pK[:], pK[:], pr[:, 4:8, 1:1 + TT], ALU.mult, "bonus_in")
                dve.wait_ge(*once("g_th"))
                ts(pr[:, 13, 1:1 + TT], pr[:, 13, 1:1 + TT], 0.5, 0.5, ALU.mult, ALU.add, "g_in")
                nth = [0]
                for tau, (t0, n) in enumerate(TILES2):
                    q8 = lambda ap: mid(ap, 8)
                    part = lambda t: t[0:n, :, 0:n]
                    rl = lambda j: C("rlev", 6 * P)[0:n, j * P:j * P + n]
                    dve.wait_ge(S("r_ab"), tau + 1)
                    for q in range(2):
                        step(nc.vector.tensor_copy(rN0[0:n, 4 * q:4 * q + 4, 0:n], ps[0:n, 6 + q, 0:4 * n].rearrange("p (q t) -> p q t", q=4)))
                    mask = C("rwmask", 512)[0:n].rearrange("p (k t) -> p k t", k=4)[:, :, 0:n]
                    for h in range(8):
                        dve.wait_ge(S("r_mats"), 8 * tau + h + 1)
                        q = (h % 2) * 4 + h // 2
                        tt(rA[0:n, q, 0:4 * n].rearrange("p (k t) -> p k t", k=4),
                           ps[0:n, h % 6, 0:4 * n].rearrange("p (k t) -> p k t", k=4), mask, ALU.mult, "r_mask")
                    tt(part(rG), rA[0:n, :, 0:n], q8(C("rlevt")[0:n, 0:n]), ALU.mult)
                    tt(part(rG), q8(C("ident")[0:n, 0:n]), part(rG), ALU.subtract)
                    tt(part(rI), part(rN0), q8(rl(0)), ALU.mult)
                    tt(part(rI), q8(C("ident")[0:n, 0:n]), part(rI), ALU.subtract)
                    levels = [j for j in range(1, 6) if LEVELS[j] < n]
                    def level_part(j):
                        nth[0] += 1
                        tt(rN[0:n, (nth[0] - 1) % 2, :, 0:n], part(rN0), q8(rl(j)), ALU.mult, "r_n")

                    level_part(levels[0])
                    for j in levels:
                        i = 2 * nth[0] - 2
                        if j != levels[-1]:
                            level_part(j + 1)
                        for q in range(2):
                            dve.wait_ge(S("r_d"), i + q + 1)
                            for dst, b in ((rG, 2), (rI, 4)):
                                if b == 4 and j == levels[-1]:
                                    dve.sem_inc(S("r_g"), 1)
                                    dve_n["r_g"] += 1
                                    continue
                                d = dst[0:n, 4 * q:4 * q + 4, 0:n]
                                tt(d, d, ps[0:n, b + q, 0:4 * n].rearrange("p (q t) -> p q t", q=4), ALU.subtract, "r_g")
                    dve.wait_ge(S("r_y0"), tau + 1)
                    tt(rR[:, :, 0:n], ps[:, 2, 0:4 * n].rearrange("p (q t) -> p q t", q=4), AR[:, :, 1, t0:t0 + n], ALU.add, "r_r")
                    dve.wait_ge(S("r_y0c"), tau + 1)
                    if tau < 2:
                        for c in (2 * tau, 2 * tau + 1):
                            dve.wait_ge(S("r_phi"), c + 1)
                            v = ps[:, 4 + c % 2, :].rearrange("p (w q i) -> p w q i", w=2, q=4)
                            tt(psi[:, c % 2], v[:, 1], end(eL[:, :, c], 64), ALU.mult)
                            tt(phi[:, c % 2], v[:, 0], mid(C("istack", 64), 4), ALU.add, "r_phic")
                    for c in [c for c, (s, _) in enumerate(RW_CHUNKS) if t0 <= s < t0 + n]:
                        start, width = RW_CHUNKS[c]
                        if c >= 1:
                            dve.wait_ge(S("r_ys"), c)
                            for a in range(2):
                                rows = slice(64 * a, 64 * a + 64)
                                o = ps[rows, 6 + a, 0:4 * n].rearrange("p (q t) -> p q t", q=4)[:, :, start - t0:start - t0 + width]
                                tt(yT[rows, :, start:start + width], yT[rows, :, start:start + width], o, ALU.add)
                        if c == 0:
                            step(nc.vector.tensor_copy(state[:, 1], psi[:, 0]), "r_state")
                        elif c < 4:
                            dve.wait_ge(S("r_s"), c)
                            for a in range(2):
                                rows = slice(64 * a, 64 * a + 64)
                                s = state[rows, (c + 1) % 2]
                                tt(s, ps[rows, a, 0:256].rearrange("p (q i) -> p q i", q=4), end(eL[rows, :, c], 64), ALU.mult)
                            tt(state[:, (c + 1) % 2], state[:, (c + 1) % 2], psi[:, c % 2], ALU.add, "r_state")
                    step(nc.vector.memset(rstd[:, 0:1], 0.0), "y_done")
                for j in range(4):
                    if j == 0:
                        dve.wait_ge(*once("gn_mean"))
                    stt(yT[:, j, :], ps[:, j, 0:TT], -1.0 / 64, yT[:, j, :], ALU.mult, ALU.add, "gn_d")
                dve.wait_ge(*once("bonus"))
                tt(pK[:], ps[:, 4:8, 0:TT], pr[:, 8:12, 1:1 + TT], ALU.mult, "bonus_out")
                dve.wait_ge(*once("gn_rs"))
                for j in range(4):
                    stt(yT[:, j, :], yT[:, j, :], V("lnx_w", j), pT[:, j, :], ALU.mult, ALU.mult)
                    stt(yT[:, j, :], yT[:, j, :], V("lnx_b", j), pK[:, j, :], ALU.add, ALU.add)
                    if j == 0:
                        dve.wait_ge(*once("g_out"))
                    tt(mixT[:, 4 + j, :], yT[:, j, :], ps[:, 4 + j, 0:TT], ALU.mult, "mix_x")
                for j in range(4):
                    mix_low(4 + KT + j + 1, 4 + j, 0)

            setup()
            norm("norm0", TM, T, "norm0")
            masks()
            even_in()
            mlstm()
            attention()
            residual("norm1", G_EO, TM)
            norm("norm1", TM, T, "norm1")
            hgrn_in()
            hgrn()
            residual("ffn1", G_HO, TM)
            norm("ffn1", 0, TT, "ffn1")
            ffn(U_F1, G_F1, 0)
            norm("mix", 0, TT, "mix")
            mixer_in()
            sticks()
            rwkv()
            residual("ffn2", G_PO, 0)
            norm("ffn2", 0, TT, "ffn2")
            ffn(U_F2, G_F2, FT)
            norm("final", 0, TT, "final")


_ORDER = ("stream", "vec", "row", "mat", "cst", "x")


def kernel(**inputs):
    import concourse.bacc as bacc
    from concourse.bass_utils import run_bass_kernel_spmd

    packed = pack(inputs)
    nc = bacc.Bacc("TRN2", target_bir_lowering=False, num_devices=1)
    arrays = {"in_" + n: packed[n] for n in _ORDER}
    args = [nc.dram_tensor("in_" + n, packed[n].shape, F32, kind="ExternalInput").ap() for n in _ORDER]
    out = nc.dram_tensor("out", (P, KT, T), F32, kind="ExternalOutput").ap()
    program(nc, *args, out)
    r = run_bass_kernel_spmd(nc, [arrays], core_ids=[0])
    got = np.asarray(r.results[0]["out"])
    return np.ascontiguousarray(got.transpose(2, 1, 0).reshape(1, T, D))
```
